# Optimizing a Trainium2 kernel written in Bass

```python
import math
import jax, jax.numpy as jnp
from jax import lax
import numpy as np

D_MODEL = 1024
BATCH = 1
SEQ = 256
DEPTH = 2
DEC_BATCH = 8
DEC_SEQ = 1
PAST_LEN = 2048
PAGE_SIZE = 128

D_MIX = 2 * D_MODEL
GROUP_W = D_MIX // 4
SSD_HEAD_DIM = 64
SSD_HEADS = GROUP_W // SSD_HEAD_DIM
SSD_GROUPS = 2
SSD_HPG = SSD_HEADS // SSD_GROUPS
SSD_STATE = 128
CONV_W = 4
SSD_CONV_CH = GROUP_W + 2 * SSD_GROUPS * SSD_STATE
ML_HEADS = 4
ML_HEAD_DIM = GROUP_W // ML_HEADS
MLA_HEADS = 4
MLA_NOPE = 128
MLA_ROPE = 64
MLA_V = GROUP_W // MLA_HEADS
Q_RANK = 3 * D_MODEL // 8
KV_RANK = D_MODEL // 4
ROPE_BASE = 10000.0
X_HEADS = 4
X_HEAD_DIM = GROUP_W // X_HEADS
MEM_LEN = 256
CHUNK = 128
Q_BLOCK = 128
EPS = 1e-6
IN_SIZES = (D_MIX, SSD_CONV_CH, SSD_HEADS, GROUP_W, ML_HEADS, ML_HEADS, GROUP_W, Q_RANK, KV_RANK, MLA_ROPE, GROUP_W)
D_IN = sum(IN_SIZES)

kernel_name = 'hymba_ssd_mlstm_mla_memory_decoder_step'

def rms_norm(x, g):
    xf = x.astype(jnp.float32)
    y = xf * lax.rsqrt(jnp.mean(xf * xf, axis=-1, keepdims=True) + EPS)
    return (y * g.astype(jnp.float32)).astype(x.dtype)

def rope(x, pos):
    half = MLA_ROPE // 2
    inv = ROPE_BASE ** (-jnp.arange(half, dtype=jnp.float32) * 2.0 / MLA_ROPE)
    ang = pos.astype(jnp.float32)[:, None] * inv[None, :]
    shape = (pos.shape[0],) + (1,) * (x.ndim - 3) + (half,)
    cos = jnp.cos(ang).reshape(shape)
    sin = jnp.sin(ang).reshape(shape)
    xf = x.astype(jnp.float32)
    x1, x2 = xf[..., :half], xf[..., half:]
    return jnp.concatenate([x1 * cos - x2 * sin, x1 * sin + x2 * cos], axis=-1).astype(x.dtype)

def to_chunks(t, c):
    return t.reshape(t.shape[0], t.shape[1] // c, c, *t.shape[2:]).swapaxes(0, 1)

def from_chunks(t):
    t = t.swapaxes(0, 1)
    return t.reshape(t.shape[0], t.shape[1] * t.shape[2], *t.shape[3:])

def causal_conv(u, buf, w, b):
    seq_len = u.shape[1]
    full = jnp.concatenate([buf.astype(u.dtype), u], axis=1)
    y = b + sum(full[:, j:j + seq_len] * w[j] for j in range(CONV_W))
    return y, full[:, full.shape[1] - (CONV_W - 1):]

def ssd_scan(x, dt, a, bm, cm, h0):
    c = math.gcd(x.shape[1], CHUNK)
    tri = jnp.tril(jnp.ones((c, c), dtype=bool))[None, :, :, None, None]

    def step(h, inp):
        xc, dtc, bc, cc = inp
        acum = jnp.cumsum(dtc * a, axis=1)
        seg = jnp.where(tri, acum[:, :, None] - acum[:, None, :], -jnp.inf)
        w = jnp.einsum('bign,bjgn->bijg', cc, bc)[..., None] * jnp.exp(seg) * dtc[:, None]
        y = (jnp.einsum('bijgh,bjghp->bighp', w, xc)
             + jnp.einsum('bign,bghpn->bighp', cc, h) * jnp.exp(acum)[..., None])
        w_end = jnp.exp(acum[:, -1:] - acum) * dtc
        h_new = (jnp.exp(acum[:, -1])[..., None, None] * h
                 + jnp.einsum('bjghp,bjgn->bghpn', w_end[..., None] * xc, bc))
        return h_new, y

    h_fin, ys = lax.scan(step, h0, (to_chunks(x, c), to_chunks(dt, c), to_chunks(bm, c), to_chunks(cm, c)))
    return from_chunks(ys), h_fin

def mlstm_scan(q, k, v, log_i, log_f, c0, n0, m0):
    c = math.gcd(q.shape[1], CHUNK)
    tri = jnp.tril(jnp.ones((c, c), dtype=bool))[None, :, :, None]

    def step(carry, inp):
        cmat, nvec, mval = carry
        qc, kc, vc, lic, lfc = inp
        bcum = jnp.cumsum(lfc, axis=1)
        lw = jnp.where(tri, bcum[:, :, None] - bcum[:, None, :] + lic[:, None], -jnp.inf)
        l_prev = bcum + mval[:, None]
        m_t = jnp.maximum(l_prev, jnp.max(lw, axis=2))
        sc = jnp.einsum('bthd,bshd->btsh', qc, kc) * jnp.exp(lw - m_t[:, :, None])
        g_prev = jnp.exp(l_prev - m_t)
        num = (jnp.einsum('btsh,bshv->bthv', sc, vc)
               + g_prev[..., None] * jnp.einsum('bhvd,bthd->bthv', cmat, qc))
        den = jnp.sum(sc, axis=2) + g_prev * jnp.einsum('bhd,bthd->bth', nvec, qc)
        h = num / jnp.maximum(jnp.abs(den), jnp.exp(-m_t))[..., None]
        m_new = m_t[:, -1]
        w_end = jnp.exp(bcum[:, -1:] - bcum + lic - m_new[:, None])
        decay = jnp.exp(bcum[:, -1] + mval - m_new)
        c_new = decay[..., None, None] * cmat + jnp.einsum('bshv,bshd->bhvd', w_end[..., None] * vc, kc)
        n_new = decay[..., None] * nvec + jnp.einsum('bsh,bshd->bhd', w_end, kc)
        return (c_new, n_new, m_new), h

    xs = tuple(to_chunks(t, c) for t in (q, k, v, log_i, log_f))
    (c_fin, n_fin, m_fin), hs = lax.scan(step, (c0, n0, m0), xs)
    return from_chunks(hs), c_fin, n_fin, m_fin

def mla_attention(q_nope, q_rope, q_pos, k_nope, k_rope, lat, k_pos, w_uv):
    scale = (MLA_NOPE + MLA_ROPE) ** -0.5

    def block(args):
        qn, qr, qp = args
        s = (jnp.einsum('bqhd,bkhd->bhqk', qn, k_nope)
             + jnp.einsum('bqhr,bkr->bhqk', qr, k_rope)).astype(jnp.float32) * scale
        s = jnp.where(k_pos[None, None, None, :] <= qp[None, None, :, None], s, -jnp.inf)
        p = jax.nn.softmax(s, axis=-1).astype(lat.dtype)
        ctx = jnp.einsum('bhqk,bkc->bqhc', p, lat)
        return jnp.einsum('bqhc,chv->bqhv', ctx, w_uv)

    seq_len = q_nope.shape[1]
    if seq_len > Q_BLOCK and seq_len % Q_BLOCK == 0:
        nb = seq_len // Q_BLOCK
        blk = lambda t: t.reshape(t.shape[0], nb, Q_BLOCK, *t.shape[2:]).swapaxes(0, 1)
        out = lax.map(block, (blk(q_nope), blk(q_rope), q_pos.reshape(nb, Q_BLOCK)))
        return out.swapaxes(0, 1).reshape(q_nope.shape[0], seq_len, MLA_HEADS, MLA_V)
    return block((q_nope, q_rope, q_pos))

def mixer_layer(lp, x, pos, k_pos, mem_k, mem_v, past_lat, past_kr,
                ssm_h0, ssm_buf0, ml_c0, ml_n0, ml_m0, ml_buf0):
    bsz, seq_len, _ = x.shape
    act = x.dtype
    u = rms_norm(x, lp['norm_g'])
    proj = u @ lp['w_in']
    split_at = [int(i) for i in np.cumsum(IN_SIZES)[:-1]]
    (z, xbc_raw, dt_raw, xm_raw, i_raw, f_raw, o_raw,
     cq_raw, ckv_raw, kr_raw, xq_raw) = jnp.split(proj, split_at, axis=-1)
    z_a, z_b, z_c, z_d = jnp.split(z, 4, axis=-1)

    xbc, ssm_buf = causal_conv(xbc_raw, ssm_buf0, lp['conv_a_w'], lp['conv_a_b'])
    xbc = jax.nn.silu(xbc).astype(jnp.float32)
    xa, ba, ca = jnp.split(xbc, [GROUP_W, GROUP_W + SSD_GROUPS * SSD_STATE], axis=-1)
    xa = xa.reshape(bsz, seq_len, SSD_GROUPS, SSD_HPG, SSD_HEAD_DIM)
    ba = ba.reshape(bsz, seq_len, SSD_GROUPS, SSD_STATE)
    ca = ca.reshape(bsz, seq_len, SSD_GROUPS, SSD_STATE)
    dt = jax.nn.softplus((dt_raw + lp['dt_bias']).astype(jnp.float32)).reshape(bsz, seq_len, SSD_GROUPS, SSD_HPG)
    a = -jnp.exp(lp['a_log'].astype(jnp.float32)).reshape(SSD_GROUPS, SSD_HPG)
    h0 = ssm_h0.astype(jnp.float32).reshape(bsz, SSD_GROUPS, SSD_HPG, SSD_HEAD_DIM, SSD_STATE)
    ya, ssm_h = ssd_scan(xa, dt, a, ba, ca, h0)
    ya = ya + lp['d_skip'].astype(jnp.float32).reshape(SSD_GROUPS, SSD_HPG, 1) * xa
    ya = ya.reshape(bsz, seq_len, GROUP_W).astype(act) * jax.nn.silu(z_a)
    gw = GROUP_W // SSD_GROUPS
    ya = rms_norm(ya.reshape(bsz, seq_len, SSD_GROUPS, gw),
                  lp['ssd_norm_g'].reshape(SSD_GROUPS, gw)).reshape(bsz, seq_len, GROUP_W)

    xmc, ml_buf = causal_conv(xm_raw, ml_buf0, lp['conv_b_w'], lp['conv_b_b'])
    xmc = jax.nn.silu(xmc).reshape(bsz, seq_len, ML_HEADS, ML_HEAD_DIM)
    xmv = xm_raw.reshape(bsz, seq_len, ML_HEADS, ML_HEAD_DIM)
    q_m = jnp.einsum('blhd,hde->blhe', xmc, lp['w_mq']).astype(jnp.float32)
    k_m = (jnp.einsum('blhd,hde->blhe', xmc, lp['w_mk']) * ML_HEAD_DIM ** -0.5).astype(jnp.float32)
    v_m = jnp.einsum('blhd,hde->blhe', xmv, lp['w_mv']).astype(jnp.float32)
    log_i = (i_raw + lp['b_i']).astype(jnp.float32)
    log_f = jax.nn.log_sigmoid((f_raw + lp['b_f']).astype(jnp.float32))
    hb, ml_c, ml_n, ml_m = mlstm_scan(q_m, k_m, v_m, log_i, log_f, ml_c0.astype(jnp.float32),
                                      ml_n0.astype(jnp.float32), ml_m0.astype(jnp.float32))
    hb = jax.nn.sigmoid(o_raw).reshape(bsz, seq_len, ML_HEADS, ML_HEAD_DIM) * hb.astype(act)
    yb = rms_norm(hb, lp['ml_norm_g'].reshape(ML_HEADS, ML_HEAD_DIM)).reshape(bsz, seq_len, GROUP_W) * jax.nn.silu(z_b)

    c_q = rms_norm(cq_raw, lp['q_norm_g'])
    qf = jnp.einsum('blr,rhd->blhd', c_q, lp['w_uq'])
    q_nope = rms_norm(qf[..., :MLA_NOPE], lp['qn_nope_g'])
    q_rope = rope(rms_norm(qf[..., MLA_NOPE:], lp['qn_rope_g']), pos)
    c_kv = rms_norm(ckv_raw, lp['kv_norm_g'])
    k_rope = rope(rms_norm(kr_raw, lp['kn_rope_g']), pos)
    if past_lat is None:
        all_lat, all_kr = c_kv, k_rope
    else:
        all_lat = jnp.concatenate([past_lat.astype(act), c_kv], axis=1)
        all_kr = jnp.concatenate([past_kr.astype(act), k_rope], axis=1)
    k_nope = rms_norm(jnp.einsum('bkr,rhd->bkhd', all_lat, lp['w_uk']), lp['kn_nope_g'])
    yc = mla_attention(q_nope, q_rope, pos, k_nope, all_kr, all_lat, k_pos, lp['w_uv'])
    yc = yc.reshape(bsz, seq_len, GROUP_W) * jax.nn.silu(z_c)

    xq = rms_norm(xq_raw.reshape(bsz, seq_len, X_HEADS, X_HEAD_DIM), lp['xq_norm_g'])
    s = jnp.einsum('blhd,bmhd->bhlm', xq, mem_k.astype(act)).astype(jnp.float32) * X_HEAD_DIM ** -0.5
    p = jax.nn.softmax(s, axis=-1).astype(act)
    yd = jnp.einsum('bhlm,bmhd->blhd', p, mem_v.astype(act)).reshape(bsz, seq_len, GROUP_W) * jax.nn.silu(z_d)

    y = jnp.concatenate([ya, yb, yc, yd], axis=-1) @ lp['w_out']
    new_state = (c_kv, k_rope,
                 ssm_h.reshape(bsz, SSD_HEADS, SSD_HEAD_DIM, SSD_STATE).astype(act), ssm_buf,
                 ml_c.astype(act), ml_n.astype(act), ml_m.astype(act), ml_buf)
    return x + y, new_state

def setup_inputs(seed: int = 0) -> dict:
    key = jax.random.key(seed)
    keys = jax.random.split(key, 64)
    counter = [0]

    def nxt():
        counter[0] += 1
        return keys[counter[0] - 1]

    def nrm(shape, scale=1.0):
        return jax.random.normal(nxt(), shape, jnp.float32) * scale

    def gain(shape):
        return 1.0 + nrm(shape, 0.02)

    n_pages = PAST_LEN // PAGE_SIZE
    n_used = DEC_BATCH * n_pages
    n_pool = n_used + max(1, n_used // 4)

    x_prompt = nrm((BATCH, SEQ, D_MODEL))
    x_sample = nrm((DEC_BATCH, DEC_SEQ, D_MODEL))
    mem_prompt = nrm((BATCH, MEM_LEN, D_MODEL))
    cache_mla_latent = nrm((DEPTH, n_pool, PAGE_SIZE, KV_RANK))
    cache_mla_krope = nrm((DEPTH, n_pool, PAGE_SIZE, MLA_ROPE))
    cache_mem_k = nrm((DEPTH, DEC_BATCH, MEM_LEN, X_HEADS, X_HEAD_DIM))
    cache_mem_v = nrm((DEPTH, DEC_BATCH, MEM_LEN, X_HEADS, X_HEAD_DIM))
    state_ssm = nrm((DEPTH, DEC_BATCH, SSD_HEADS, SSD_HEAD_DIM, SSD_STATE), 0.3)
    state_ssm_conv = nrm((DEPTH, DEC_BATCH, CONV_W - 1, SSD_CONV_CH))
    state_mlstm_C = nrm((DEPTH, DEC_BATCH, ML_HEADS, ML_HEAD_DIM, ML_HEAD_DIM), 0.1)
    state_mlstm_n = nrm((DEPTH, DEC_BATCH, ML_HEADS, ML_HEAD_DIM), 0.1)
    state_mlstm_m = nrm((DEPTH, DEC_BATCH, ML_HEADS), 0.5)
    state_mlstm_conv = nrm((DEPTH, DEC_BATCH, CONV_W - 1, GROUP_W))
    page_table = jax.random.permutation(nxt(), n_pool)[:n_used].reshape(DEC_BATCH, n_pages).astype(jnp.int32)

    dt0 = jnp.exp(jax.random.uniform(nxt(), (DEPTH, SSD_HEADS), jnp.float32, math.log(1e-3), math.log(1e-1)))
    dt_bias = dt0 + jnp.log(-jnp.expm1(-dt0))
    a_log = jnp.log(jax.random.uniform(nxt(), (DEPTH, SSD_HEADS), jnp.float32, 1.0, 16.0))

    return {
        'x_prompt': x_prompt,
        'x_sample': x_sample,
        'mem_prompt': mem_prompt,
        'cache_mla_latent': cache_mla_latent,
        'cache_mla_krope': cache_mla_krope,
        'cache_mem_k': cache_mem_k,
        'cache_mem_v': cache_mem_v,
        'state_ssm': state_ssm,
        'state_ssm_conv': state_ssm_conv,
        'state_mlstm_C': state_mlstm_C,
        'state_mlstm_n': state_mlstm_n,
        'state_mlstm_m': state_mlstm_m,
        'state_mlstm_conv': state_mlstm_conv,
        'page_table': page_table,
        'norm_g': gain((DEPTH, D_MODEL)),
        'w_in': nrm((DEPTH, D_MODEL, D_IN), D_MODEL ** -0.5),
        'conv_a_w': nrm((DEPTH, CONV_W, SSD_CONV_CH), CONV_W ** -0.5),
        'conv_a_b': nrm((DEPTH, SSD_CONV_CH), 0.02),
        'dt_bias': dt_bias,
        'a_log': a_log,
        'd_skip': 1.0 + nrm((DEPTH, SSD_HEADS), 0.1),
        'ssd_norm_g': gain((DEPTH, GROUP_W)),
        'conv_b_w': nrm((DEPTH, CONV_W, GROUP_W), CONV_W ** -0.5),
        'conv_b_b': nrm((DEPTH, GROUP_W), 0.02),
        'w_mq': nrm((DEPTH, ML_HEADS, ML_HEAD_DIM, ML_HEAD_DIM), ML_HEAD_DIM ** -0.5),
        'w_mk': nrm((DEPTH, ML_HEADS, ML_HEAD_DIM, ML_HEAD_DIM), ML_HEAD_DIM ** -0.5),
        'w_mv': nrm((DEPTH, ML_HEADS, ML_HEAD_DIM, ML_HEAD_DIM), ML_HEAD_DIM ** -0.5),
        'b_i': nrm((DEPTH, ML_HEADS), 0.1),
        'b_f': jnp.linspace(3.0, 6.0, ML_HEADS, dtype=jnp.float32)[None, :] + nrm((DEPTH, ML_HEADS), 0.1),
        'ml_norm_g': gain((DEPTH, GROUP_W)),
        'q_norm_g': gain((DEPTH, Q_RANK)),
        'kv_norm_g': gain((DEPTH, KV_RANK)),
        'w_uq': nrm((DEPTH, Q_RANK, MLA_HEADS, MLA_NOPE + MLA_ROPE), Q_RANK ** -0.5),
        'w_uk': nrm((DEPTH, KV_RANK, MLA_HEADS, MLA_NOPE), KV_RANK ** -0.5),
        'w_uv': nrm((DEPTH, KV_RANK, MLA_HEADS, MLA_V), KV_RANK ** -0.5),
        'qn_nope_g': gain((DEPTH, MLA_NOPE)),
        'qn_rope_g': gain((DEPTH, MLA_ROPE)),
        'kn_nope_g': gain((DEPTH, MLA_NOPE)),
        'kn_rope_g': gain((DEPTH, MLA_ROPE)),
        'mem_norm_g': gain((DEPTH, D_MODEL)),
        'w_mem_k': nrm((DEPTH, D_MODEL, GROUP_W), D_MODEL ** -0.5),
        'w_mem_v': nrm((DEPTH, D_MODEL, GROUP_W), D_MODEL ** -0.5),
        'xk_norm_g': gain((DEPTH, X_HEAD_DIM)),
        'xq_norm_g': gain((DEPTH, X_HEAD_DIM)),
        'w_out': nrm((DEPTH, D_MIX, D_MODEL), D_MIX ** -0.5),
        'final_norm_g': gain((D_MODEL,)),
    }

def reference(x_prompt, x_sample, mem_prompt, cache_mla_latent, cache_mla_krope, cache_mem_k, cache_mem_v,
              state_ssm, state_ssm_conv, state_mlstm_C, state_mlstm_n, state_mlstm_m, state_mlstm_conv,
              page_table, norm_g, w_in, conv_a_w, conv_a_b, dt_bias, a_log, d_skip, ssd_norm_g,
              conv_b_w, conv_b_b, w_mq, w_mk, w_mv, b_i, b_f, ml_norm_g, q_norm_g, kv_norm_g,
              w_uq, w_uk, w_uv, qn_nope_g, qn_rope_g, kn_nope_g, kn_rope_g, mem_norm_g,
              w_mem_k, w_mem_v, xk_norm_g, xq_norm_g, w_out, final_norm_g):
    act = x_prompt.dtype
    bp, lp_len, _ = x_prompt.shape
    bs, ls_len, _ = x_sample.shape
    n_pages = page_table.shape[1]
    past_len = n_pages * cache_mla_latent.shape[2]
    mem_len = mem_prompt.shape[1]
    pos_p = jnp.arange(lp_len, dtype=jnp.int32)
    pos_s = past_len + jnp.arange(ls_len, dtype=jnp.int32)
    kpos_s = jnp.arange(past_len + ls_len, dtype=jnp.int32)

    p_h0 = jnp.zeros((bp, SSD_HEADS, SSD_HEAD_DIM, SSD_STATE), act)
    p_sbuf0 = jnp.zeros((bp, CONV_W - 1, SSD_CONV_CH), act)
    p_c0 = jnp.zeros((bp, ML_HEADS, ML_HEAD_DIM, ML_HEAD_DIM), act)
    p_n0 = jnp.zeros((bp, ML_HEADS, ML_HEAD_DIM), act)
    p_m0 = jnp.zeros((bp, ML_HEADS), act)
    p_mbuf0 = jnp.zeros((bp, CONV_W - 1, GROUP_W), act)

    hp, hs = x_prompt, x_sample
    p_states, s_states, p_mks, p_mvs = [], [], [], []
    for l in range(DEPTH):
        lp = {
            'norm_g': norm_g[l], 'w_in': w_in[l], 'conv_a_w': conv_a_w[l], 'conv_a_b': conv_a_b[l],
            'dt_bias': dt_bias[l], 'a_log': a_log[l], 'd_skip': d_skip[l], 'ssd_norm_g': ssd_norm_g[l],
            'conv_b_w': conv_b_w[l], 'conv_b_b': conv_b_b[l], 'w_mq': w_mq[l], 'w_mk': w_mk[l],
            'w_mv': w_mv[l], 'b_i': b_i[l], 'b_f': b_f[l], 'ml_norm_g': ml_norm_g[l],
            'q_norm_g': q_norm_g[l], 'kv_norm_g': kv_norm_g[l], 'w_uq': w_uq[l], 'w_uk': w_uk[l],
            'w_uv': w_uv[l], 'qn_nope_g': qn_nope_g[l], 'qn_rope_g': qn_rope_g[l],
            'kn_nope_g': kn_nope_g[l], 'kn_rope_g': kn_rope_g[l], 'xq_norm_g': xq_norm_g[l],
            'w_out': w_out[l],
        }
        mem_n = rms_norm(mem_prompt, mem_norm_g[l])
        mk = rms_norm((mem_n @ w_mem_k[l]).reshape(bp, mem_len, X_HEADS, X_HEAD_DIM), xk_norm_g[l])
        mv = (mem_n @ w_mem_v[l]).reshape(bp, mem_len, X_HEADS, X_HEAD_DIM)
        hp, st_p = mixer_layer(lp, hp, pos_p, pos_p, mk, mv, None, None,
                               p_h0, p_sbuf0, p_c0, p_n0, p_m0, p_mbuf0)
        p_states.append(st_p)
        p_mks.append(mk)
        p_mvs.append(mv)
        past_lat = cache_mla_latent[l, page_table].reshape(bs, past_len, KV_RANK)
        past_kr = cache_mla_krope[l, page_table].reshape(bs, past_len, MLA_ROPE)
        hs, st_s = mixer_layer(lp, hs, pos_s, kpos_s, cache_mem_k[l], cache_mem_v[l], past_lat, past_kr,
                               state_ssm[l], state_ssm_conv[l], state_mlstm_C[l], state_mlstm_n[l],
                               state_mlstm_m[l], state_mlstm_conv[l])
        s_states.append(st_s)

    y_prompt = rms_norm(hp, final_norm_g)
    y_sample = rms_norm(hs, final_norm_g)
    (p_lat, p_kr, p_ssm, p_sconv, p_mc, p_mn, p_mm, p_mconv) = [
        jnp.stack([st[i] for st in p_states]) for i in range(8)]
    (s_lat, s_kr, s_ssm, s_sconv, s_mc, s_mn, s_mm, s_mconv) = [
        jnp.stack([st[i] for st in s_states]) for i in range(8)]
    p_mem_k = jnp.stack(p_mks)
    p_mem_v = jnp.stack(p_mvs)
    return (y_prompt, y_sample, p_lat, p_kr, p_mem_k, p_mem_v, p_ssm, p_sconv, p_mc, p_mn, p_mm, p_mconv,
            s_lat, s_kr, s_ssm, s_sconv, s_mc, s_mn, s_mm, s_mconv)


_drawn_inputs = setup_inputs


def setup_inputs(seed=0):
    import zlib

    import numpy as np

    out = dict(_drawn_inputs(seed))
    spreads = {}
    factors = {'cache_mla_latent': 4.688,
     'cache_mla_krope': 8.0,
     'ssd_norm_g': 4.326,
     'ml_norm_g': 7.736,
     'q_norm_g': 8.0,
     'qn_nope_g': 8.0,
     'qn_rope_g': 8.0,
     'kn_nope_g': 8.0,
     'kn_rope_g': 21.314,
     'mem_norm_g': 2.773,
     'xk_norm_g': 2.81,
     'xq_norm_g': 8.0,
     'final_norm_g': 22.152}
    for name, (base, spread) in spreads.items():
        noise = np.random.default_rng([zlib.crc32(name.encode()), seed]).standard_normal(out[name].shape)
        drawn = base * np.exp(spread * noise) if base else spread * noise
        out[name] = __import__('jax').numpy.asarray(drawn.astype(out[name].dtype))
    for name, factor in factors.items():
        out[name] = (out[name] * factor).astype(out[name].dtype)
    return out
```

```python
import math
from contextlib import ExitStack

import numpy as np

import concourse.bass as bass
from concourse import mybir
from concourse.alu_op_type import AluOpType as ALU

F32 = mybir.dt.float32
ACT = mybir.ActivationFunctionType
LN_EXP = "natural_log_exp_and_others"
AXX = mybir.AxisListType.X

P = 128
DEPTH, D_MODEL, SEQ, NB = 2, 1024, 256, 8
T = SEQ + NB
KT = D_MODEL // P
HEADS = 4
SSD_HEADS, SSD_W = 8, 64
ROPE = 64
Q_TILES, KV_TILES = 3, 2
PAGES, PAGE, POOL = 16, 128, 160
MEM = 256
EPS = 1e-6
NEG = -1.0e30
MLA_SCALE = (P + ROPE) ** -0.5
X_SCALE = P ** -0.5
K_SCALE = P ** -0.5

CONV, GATE, KR, CQ, CKV, XQ, OG, Z = 0, 12, 13, 14, 17, 19, 23, 27
IN_TILES = 43
CT = 12
OUT_TILES, MIX_TILES = 8, 16
NORMS = 8
IN_CHUNKS = (IN_TILES + 1) // 2
FILL = IN_TILES // 4

C_NORM, C_CW, C_CB, C_SSD, C_ML, C_Q, C_KV = 0, 8, 56, 68, 72, 76, 79
C_QNN, C_QNR, C_KNN, C_KNR, C_MEM, C_XK, C_XQ, C_D = 81, 82, 83, 84, 85, 93, 94, 95
C_FIN, C_DTB, C_ALOG, C_BI, C_BF, C_M0, C_N0, C_ST = 99, 107, 108, 109, 110, 111, 119, 151
N_PAR = C_ST + CT * 3 * NB

K_ID, K_ONE, K_MASK, K_TRI, K_ROT, K_COS, K_SIN, K_SEL, K_EXP, K_EPS = (
    0, 128, 392, 776, 1160, 1224, 1488, 1752, 2776, 3288)
N_CST = 3289

SLOT = 2048
CHUNKS = 38
R_MK, R_MV, R_UQ, R_MLQK, R_MLV, R_OUT = 22, 24, 26, 28, 29, 30
ROWS = 2048
ROW_B, ROW_C, ROW_K, ROW_Q, ROW_X = 0, 256, 512, 1024, 1536


S_BANK = (0, 1, 6, 7)


def spread_bank(n):
    return (0, 1, 4, 5)[n % 4] if n < 8 else n % 2


class Signal:

    def __init__(self, sem, per_layer, before=0):
        self.sem, self.per_layer, self.before = sem, per_layer, before

    def __call__(self, l, n):
        return self.sem, l * self.per_layer + (n + self.before)


def build(nc, d):
    ctx = ExitStack()
    with ctx:
        def sb(name, shape, dt=F32):
            return ctx.enter_context(nc.sbuf_tensor(name, shape, dt))

        def sig(name, per_layer=1, before=0):
            return Signal(ctx.enter_context(nc.semaphore(name)), per_layer, before)

        cst = sb("cst", [P, N_CST])
        xT = sb("xT", [P, KT, T])
        uT = sb("uT", [P, KT * T])
        pt = sb("pt", [P, IN_TILES, T])
        xc = sb("xc", [P, CT, T])
        ring = sb("ring", [P, 2, SLOT])
        lat0 = sb("lat0", [P, PAGES, 256])
        lat1 = sb("lat1", [P, PAGES, 256])
        kr = sb("kr", [P, 2, PAGES // 2, PAGE])
        states = sb("states", [P, 2, 2, 512])
        rows = sb("rows", [P, ROWS])
        scr = sb("scr", [P, 2112])
        wsm = sb("wsm", [P, 2, 1024])
        wk = sb("wk", [P, 4, 260])
        par = sb("par", [P, N_PAR])
        gates = sb("gates", [SSD_HEADS, 9, T])
        softp = sb("softp", [SSD_HEADS, 2, T])
        QR = sb("QR", [ROPE, HEADS + 1, T])
        btok = sb("btok", [P, 2, 256])
        dtmp = sb("dtmp", [P, 512])
        rsm = sb("rsm", [P, MEM])
        gsmall = sb("gsmall", [SSD_HEADS, 40])
        cols = sb("cols", [P, 2, 32])
        da = sb("da", [P, NB, 4])
        dtx = sb("dtx", [P, NB, 4])
        gb = sb("gb", [P, 3, NB, 4])
        wv = sb("wv", [P, NB, 4])
        qabs = sb("qabs", [P, NB, 2, 4])
        qrs = sb("qrs", [P, NB, 8])
        scur = sb("scur", [P, NB, 4])
        ctxall = sb("ctxall", [P, 2, 4, NB])
        ysa = sb("ysa", [P, NB, 4])
        ysb = sb("ysb", [P, NB, 4])
        ysd = sb("ysd", [P, NB, 4])
        pre = sb("pre", [P, 3, 32])
        ssq = sb("ssq", [P, 2, PAGES, 4])
        raws = sb("raws", [P, 2, PAGES, 4])
        owns = sb("owns", [P, NB, 4])
        dens = sb("dens", [P, NB, 4])
        sx = sb("sx", [P, 2, 2, 4])
        prob = sb("prob", [P, 2, PAGES, 4])
        probx = sb("probx", [P, 2, 2, 4])
        sm = sb("sm", [P, 2, 64])
        pages = sb("pages", [1, NB * PAGES * DEPTH], mybir.dt.int32)
        ps = ctx.enter_context(nc.psum_tensor("ps", [P, 8, 512], F32))

        ident = cst[:, K_ID:K_ID + P]
        ones = cst[:, K_ONE:K_ONE + P]
        tri = cst[:, K_TRI:K_TRI + 384]
        eps = cst[:, K_EPS:K_EPS + 1]
        latb = [lat0, lat1]
        u3 = uT[:, :].rearrange("p (k t) -> p k t", k=KT)
        memk = uT[:, 0:1024]
        memv = uT[:, 1024:2048].rearrange("p (m n) -> p m n", m=2)
        A1 = lat1[:, :, :].rearrange("p a b -> p (a b)")
        mkT = A1[:, 0:1024].rearrange("p (h m) -> p h m", h=4)
        memV = A1[:, 1024:2048].rearrange("p (m n) -> p m n", m=2)
        memn = A1[:, 2048:4096].rearrange("p (k t) -> p k t", k=KT)
        mlaV = A1[:, 2048:3072].rearrange("p (m n) -> p m n", m=2)
        ktok = A1[:, 0:1024].rearrange("p (m n) -> p m n", m=2)
        vtok = A1[:, 1024:2048].rearrange("p (m n) -> p m n", m=2)
        vw = A1[:, 2048:3072].rearrange("p (m n) -> p m n", m=2)
        xw = A1[:, 3072:4096].rearrange("p (m n) -> p m n", m=2)
        xtok = pt[:, XQ:XQ + 4, :].rearrange("p a b -> p (a b)")[:, 0:1024].rearrange("p (m n) -> p m n", m=2)
        qn, kn = pt[:, 0:4, :], pt[:, 4:8, :]
        mlq, mlk = pt[:, 0:4, :], pt[:, 4:8, :]
        A0 = lat0[:, :, :].rearrange("p a b -> p (a b)")
        nsq = [t[:, 0:4 * T].rearrange("p (h t) -> p h t", h=4) for t in (scr, rows)]
        nrs_ml = A0[:, 0:4 * T].rearrange("p (h t) -> p h t", h=4)
        nrs = scr[:, 4 * T:8 * T].rearrange("p (h t) -> p h t", h=4)
        att = rows[:, :].rearrange("p (u q k) -> p u q k", u=4, q=2)
        attT = scr[:, 1024:2048].rearrange("p (u k q) -> p u k q", u=2, k=2)
        dec = uT[:, 0:1536].rearrange("p (u i) -> p u i", u=4)
        stm = scr[:, 768:1536].rearrange("p (u i) -> p u i", u=2)
        emm = scr[:, 1536:2048].rearrange("p (u i) -> p u i", u=2)
        latT = scr[:, 0:1024].rearrange("p (u g c k) -> p u g c k", u=2, g=2, c=2)
        sqd = scr[:, 1024:2048].rearrange("p (u n) -> p u n", u=2)
        asm = sm[:, 0, 0:32].rearrange("p (u i) -> p u i", u=4)
        ctxr = gates[0:4].rearrange("p a t -> p (a t)")[:, 0:NB * 256].rearrange("p (b n) -> p b n", b=NB)
        gdt, acum, wend, la, li, lf, gi, nmx, mT = (gates[:, i, :] for i in range(9))


        first = sig("first_loads")
        layer_free = sig("layer_free", 4, 4)
        par_in, wsm_in, mem_in = sig("par_in", 16), sig("wsm_in", 32), sig("mem_in", 16)
        slot_in = [sig("slot0_in", 16 * CHUNKS // 2), sig("slot1_in", 16 * CHUNKS // 2)]
        slot_free = sig("slot_free", 8)
        x_sq, x_ss, x_rs, u_ready = sig("x_squares"), sig("x_sums"), sig("x_rstd"), sig("u_ready")
        pj_mm, pj_act, pj_dve = sig("proj_mm", IN_TILES), sig("proj_act", 22, 2), sig("proj_dve", 21, 2)
        conv_a, conv_d, xc_ready, z_ready = sig("conv_tap3"), sig("conv_done"), sig("xc_ready"), sig("z_ready")
        g_raw, g_neg, g_log, g_scan, g_exp, g_wend, g_pe, g_out = (
            sig(f"gates_{x}") for x in ("raw", "neg", "log", "scan", "exp", "wend", "mm", "out"))
        conv_saved = sig("conv_saved", 16)
        m_sq, m_ss, m_rs = sig("mem_squares"), sig("mem_sums"), sig("mem_rstd")
        mem_ready = sig("mem_ready")
        n_in = sig("norm_in", 4)
        n_sq, n_ss, n_rs, n_out = (sig(f"norm_{x}", NORMS) for x in ("squares", "sums", "rstd", "out"))
        mv_mm, mv_out, lv_mm, lv_out = sig("memv_mm"), sig("memv_out"), sig("latv_mm"), sig("latv_out")
        r_mm, r_out = sig("rot_mm"), sig("rot_out")
        s_mm, s_max, s_exp, s_p, s_t, s_pt, s_y, s_o = (
            sig(f"att_{x}", 8) for x in ("scores", "max", "exp", "prob", "probT", "probT_sb", "y", "out"))
        pre_in, pre_mm, pre_out, pre_row = sig("pre_in"), sig("pre_mm", 3), sig("pre_out"), sig("pre_rows", 2)
        tok_mm, tok_act, tok_dve = sig("tok_mm", 7), sig("tok_act", 4), sig("tok_dve", 3)
        weighted = sig("weighted")
        st_mm, st_out = sig("masked_mm", 6), sig("masked_out", 6)
        bc_mm, seg_out, seg_exp, seg_w, ry_mm = (
            sig(f"rec_{x}", 12) for x in ("bc", "seg", "exp", "weights", "y"))
        ry_out, em_out = sig("rec_out", 8), sig("rec_emm", 4)
        fin_mm, fin_out, fin_saved = sig("fin_mm"), sig("fin_out"), sig("fin_saved", 48)
        rows_saved = sig("rows_saved", 16)
        lat_in = [sig("lat0_in", 16 * 32 * 4), sig("lat1_in", 16 * 32 * 4)]
        mk_in, mv_in, rows_in = sig("memk_in", 16 * NB), sig("memv_in", 16 * NB), sig("rows_in", 16 * NB)
        st_in = [sig("state0_in", 32 * 4), sig("state1_in", 32 * 4)]
        st_saved = [sig("state0_saved", 32 * 4, 32), sig("state1_saved", 32 * 4, 32)]
        q_in, cr_mm, cr_out = sig("query_in", NB), sig("context_by_feature"), sig("context_ready")
        t_mm, t_sb, pair_mm = sig("latT", 8 * NB), sig("latT_sb", 8 * NB, 1), sig("pair_mm", 8 * NB, 2)
        k_mm, k_sq, k_red = sig("key_mm", PAGES * NB), sig("key_squares", PAGES * NB, 2), sig("key_sums", PAGES * NB, 2)
        k_rs, mx_in, mx_all, s_sub = sig("key_rstd", NB), sig("max_in", NB, 2), sig("max_all", NB), sig("shifted", NB)
        p_exp, p_sum, cx_mm, cx_out = sig("probs", NB), sig("prob_sums", NB), sig("context", NB, 2), sig("context_out", NB, 2)
        rows_used, memk_used, decayed, st_new = (
            sig("rows_used", NB), sig("memk_used", NB), sig("decayed", NB), sig("state_new", NB))
        ns_in, nq_mm, uv_mm, a_ready = sig("nstate_in"), sig("nstate_q"), sig("uv_mm"), sig("sample_out")
        mixed = sig("mixed")
        o_mm, o_out = sig("out_mm", OUT_TILES, 2), sig("out_add", OUT_TILES, 2)
        saved, kv_saved = sig("saved", 16 * 5), sig("memory_saved", 32)
        f_sq, f_ss, f_rs, f_out, y_saved = sig("fin_sq"), sig("fin_ss"), sig("fin_rs"), sig("fin_norm"), sig("y_saved")

        block = ctx.enter_context(nc.Block())

        @block.sync
        def _(sp):
            sp.dma_start(cst[:, :], d["cst"]).then_inc(first.sem, 16)
            sp.dma_start(memn, d["memT"]).then_inc(first.sem, 16)
            sp.dma_start(xT[:, :, :], d["xT"]).then_inc(first.sem, 16)
            sp.dma_start(pages[:, :], d["pages"]).then_inc(first.sem, 16)
            sp.wait_ge(first.sem, 64)

            def one(name, i):
                return d[name][bass.ds(i, 1)].rearrange("o p n -> p (o n)")

            def load_pages(l, b, u):
                places = [sp.value_load(pages[0:1, bass.ds(l * (NB * PAGES) + (b * PAGES + j), 1)],
                                        min_val=0, max_val=DEPTH * POOL - 1) for j in range(PAGES)]
                if type(b) is not int or b:
                    sp.wait_ge(*pair_mm(l, 8 * (b - 1)))
                for j, page in enumerate(places):
                    half = ROPE * (j // 8)
                    sp.dma_start(kr[half:half + ROPE, u, j % 8, :], one("krope", page)).then_inc(lat_in[u].sem, 16)
                sp.wait_ge(*cx_mm(l, b - 1))
                if type(b) is not int or b:
                    sp.dma_start(uT[:, 1024:2048], one("memv", l * NB + (b - 1))).then_inc(mv_in.sem, 16)
                for j, page in enumerate(places):
                    sp.dma_start(latb[u][:, j, :], one("lat", page)).then_inc(lat_in[u].sem, 16)

            def load_states(l, b, u, k):
                sp.wait_ge(*st_saved[u](l, 32 * k))
                sp.dma_start(states[:, u, 0, :], one("ssm", l * NB + b)).then_inc(st_in[u].sem, 16)
                sp.dma_start(states[:, u, 1, :], one("mlC", l * NB + b)).then_inc(st_in[u].sem, 16)

            def load_rows(l, b):
                if type(b) is not int or b:
                    sp.wait_ge(*memk_used(l, b))
                sp.dma_start(memk, one("memk", l * NB + b)).then_inc(mk_in.sem, 16)
                if type(b) is not int or b:
                    sp.wait_ge(*rows_used(l, b))
                sp.dma_start(rows[:, :], d["rowscr"][bass.ds(b, 1), :].rearrange("o n -> (o n)")
                             .partition_broadcast(P)).then_inc(rows_in.sem, 16)

            sp.wait_ge(m_sq.sem, 1)
            with sp.Fori(0, DEPTH) as l:
                sp.wait_ge(*layer_free(l, 0))
                sp.dma_start(par[:, :], one("par", l)).then_inc(par_in.sem, 16)
                sp.dma_start(memn, d["memT"]).then_inc(mem_in.sem, 16)
                small = one("wsm", l)
                sp.dma_start(wsm[:, :, :].rearrange("p a n -> p (a n)"), small[:, 1024:3072]).then_inc(wsm_in.sem, 16)
                sp.dma_start(wk[:, :, 2:258], small[:, 0:1024].rearrange("p (a n) -> p a n", a=4)).then_inc(wsm_in.sem, 16)
                load_pages(l, 0, 0)
                load_states(l, 0, 0, 0)
                sp.wait_ge(*par_in(l, 16))
                sp.dma_start(one("o_conv_old", l), par[:, C_ST:]).then_inc(saved.sem, 16)
                sp.wait_ge(*pj_act(l, 22))
                sp.wait_ge(*pj_dve(l, 21))
                sp.dma_start(d["o_conv"][bass.ds(l, 1)].rearrange("o p c t -> p (o c) t"),
                             pt[:, 0:CT, SEQ - 3:T]).then_inc(conv_saved.sem, 16)
                sp.wait_ge(*n_out(l, 2))
                sp.dma_start(one("o_mk", l), A1[:, 0:1024]).then_inc(kv_saved.sem, 16)
                sp.wait_ge(*mv_out(l, 1))
                sp.dma_start(one("o_mv", l), A1[:, 1024:2048]).then_inc(kv_saved.sem, 16)
                sp.wait_ge(*n_out(l, 1))
                sp.dma_start(d["o_lat"][bass.ds(l, 1)].rearrange("o p c t -> p (o c) t"),
                             pt[:, CKV:CKV + 2, :]).then_inc(saved.sem, 16)
                sp.wait_ge(*r_out(l, 1))
                sp.dma_start(one("o_kr", l), QR[:, HEADS, :]).then_inc(saved.sem, 16)
                sp.wait_ge(*g_scan(l, 1))
                sp.dma_start(one("o_m", l), mT[0:4, :]).then_inc(saved.sem, 16)
                sp.wait_ge(*pre_row(l, 2))
                sp.dma_start(d["rowscr"], rows[0:NB, :]).then_inc(rows_saved.sem, 16)
                sp.wait_ge(*fin_out(l, 1))
                sp.wait_ge(*rows_saved(l, 16))
                load_rows(l, 0)
                sp.dma_start(one("o_ssm", l), A1[:, 0:512]).then_inc(fin_saved.sem, 16)
                sp.dma_start(one("o_C", l), A1[:, 512:1024]).then_inc(fin_saved.sem, 16)
                sp.dma_start(one("o_n", l), A1[0:1, 1024:1536]).then_inc(fin_saved.sem, 16)
                sp.wait_ge(*fin_saved(l, 48))
                load_pages(l, 1, 1)
                load_states(l, 1, 1, 0)
                load_rows(l, 1)
                with sp.Fori(0, NB // 2 - 1) as i:
                    for u in range(2):
                        load_pages(l, 2 * i + (2 + u), u)
                        load_states(l, 2 * i + (2 + u), u, i + 1)
                        load_rows(l, 2 * i + (2 + u))
                sp.wait_ge(*cx_mm(l, NB - 1))
                sp.dma_start(uT[:, 1024:2048], one("memv", l * NB + (NB - 1))).then_inc(mv_in.sem, 16)
                sp.wait_ge(*ns_in(l, 1))
                sp.dma_start(one("o_ns", l), par[:, C_N0:C_N0 + 32]).then_inc(saved.sem, 16)
                sp.wait_ge(*saved(l, 80))
                sp.wait_ge(*conv_saved(l, 16))
                sp.sem_inc(layer_free.sem, 1)
            sp.wait_ge(f_out.sem, 1)
            sp.dma_start(d["o_y"], u3).then_inc(y_saved.sem, 16)
            sp.wait_ge(y_saved.sem, 16)

        @block.gpsimd
        def _(pool):
            def chunk(l, n, u, free, wide=2048):
                pool.wait_ge(*free)
                weights = d["weights"][bass.ds(pool.snap(CHUNKS * l + n), 1)].rearrange("o p n -> p (o n)")
                pool.dma_start(ring[:, u, 0:wide], weights[:, 0:wide]).then_inc(slot_in[u].sem, 16)

            with pool.Fori(0, DEPTH) as l:
                for u in range(2):
                    chunk(l, u, u, o_mm(l, u - 1))
                with pool.Fori(1, R_MK // 2) as i:
                    for u in range(2):
                        chunk(l, 2 * i + u, u, pj_mm(l, 4 * i + (2 * u - 2)))
                for u in range(2):
                    chunk(l, R_MK + u, u, pj_mm(l, IN_TILES - 1 + u))
                for u in range(2):
                    chunk(l, R_MV + u, u, slot_free(l, 1 + u))
                for u in range(2):
                    chunk(l, R_UQ + u, u, slot_free(l, 3 + u), 1152)
                for u in range(2):
                    chunk(l, R_MLQK + u, u, slot_free(l, 5 + u), 1024)
                for u in range(2):
                    chunk(l, R_OUT + u, u, slot_free(l, 7 + u))
                with pool.Fori(0, NB // 2) as i:
                    for u in range(2):
                        b = 2 * i + u
                        pool.wait_ge(*st_in[u](l, 32 * i + 32))
                        pool.wait_ge(*g_out(l, 1))
                        for s, factor in ((0, da[:, :, :]), (1, gb[:, 0])):
                            st = states[:, u, s, :].rearrange("p (h n) -> p h n", h=4)
                            f = factor[:, bass.ds(b, 1), :].rearrange("p o h -> p (o h)").unsqueeze(2).broadcast_to([P, 4, P])
                            ins = nc.gpsimd.tensor_tensor(st, st, f, ALU.mult)
                        ins.then_inc(decayed.sem, 1)
                        pool.wait_ge(*mx_in(l, b + 1))
                        nc.gpsimd.tensor_tensor(sm[:, u, 56:64], sm[:, u, 0:8], ones[:, 0:8], ALU.mult)
                        pool.drain()
                        nc.gpsimd.partition_all_reduce(sm[:, u, 8:16], sm[:, u, 56:64], P, bass.bass_isa.ReduceOp.max
                                                       ).then_inc(mx_all.sem, 1)
                with pool.Fori(1, OUT_TILES // 2) as i:
                    for c in range(2):
                        chunk(l, 2 * i + (R_OUT + c), c, o_mm(l, 2 * i + (c - 1)))
        @block.tensor
        def _(pe):
            mm = nc.tensor.matmul

            def slot(l, n):
                pe.wait_ge(*slot_in[n % 2](l, 16 * (n // 2 + 1)))
                return ring[:, n % 2, :]

            def tile_mm(l, m, u, a, bank):
                w = ring[:, u, a * 1024:(a + 1) * 1024].rearrange("p (k m) -> p k m", k=KT)
                for k in range(KT):
                    last = mm(ps[:, bank, 0:T], w[:, k, :], u3[:, k, :], start=k == 0, stop=k == KT - 1)
                last.then_inc(pj_mm.sem, 1)
                return last

            def sums(l, k, bank, groups, width=T):
                pe.wait_ge(*n_sq(l, k + 1))
                for i, group in enumerate(groups):
                    for j, (n, t) in enumerate(group):
                        last = mm(ps[:, bank + i, 0:width], ones[0:n, :], t, start=j == 0, stop=j == len(group) - 1)
                last.then_inc(n_ss.sem, 1)

            def heads(k, n=P):
                return [[(n, nsq[k % 2][0:n, h, :])] for h in range(4)]

            def scores(l, h):
                x = h < 4
                if h >= 4:
                    pe.wait_ge(*s_max(l, h - 3))
                for q in range(2):
                    out = ps[:, S_BANK[h % 4], q * 256:(q + 1) * 256]
                    tokens = slice(q * P, (q + 1) * P)
                    if x:
                        last = mm(out, pt[:, XQ + h, tokens], mkT[:, h, :], start=True, stop=True)
                    else:
                        mm(out, qn[:, h - 4, tokens], kn[:, h - 4, 0:SEQ], start=True, stop=False)
                        last = mm(out, QR[:, h - 4, tokens], QR[:, HEADS, 0:SEQ], start=False, stop=True)
                last.then_inc(s_mm.sem, 1)

            def masked(l, item):
                if item >= 2:
                    pe.wait_ge(*st_out(l, item - 1))
                k, q = (xc[:, 4 + item], xc[:, 6 + item]) if item < 2 else (mlk[:, item - 2], mlq[:, item - 2])
                mm(ps[:, 6 + item % 2, 0:256], k[:, 0:P], q[:, 0:256], start=True, stop=True)
                mm(ps[:, 6 + item % 2, 256:384], k[:, P:256], q[:, P:256], start=True, stop=True
                   ).then_inc(st_mm.sem, 1)

            def spread(l, n):
                if n >= 4:
                    pe.wait_ge(*seg_out(l, n - 3 if n < 8 else n - 1))
                if n >= 10:
                    pe.wait_ge(*em_out(l, n - 9))
                h, row = (n, acum[:, 0:SEQ]) if n < 8 else (n - 8, nmx[0:4, 0:SEQ])
                k = 8 if n < 8 else 4
                sel = cst[0:k, K_SEL + h * P:K_SEL + (h + 1) * P]
                last = mm(ps[:, spread_bank(n), 0:256], sel, row, start=True, stop=True)
                if n >= 8:
                    last = mm(ps[:, n % 2, 256:512], sel, mT[0:4, 0:SEQ], start=True, stop=True)
                last.then_inc(bc_mm.sem, 1)

            def recur(l, n):
                pe.wait_ge(*seg_w(l, n + 1))
                s = n // 2 if n < 8 else n - 4
                if s >= 2 and not (n < 8 and n % 2):
                    pe.wait_ge(*ry_out(l, s - 1))
                if n < 8:
                    out = ps[SSD_W * (n % 2):SSD_W * (n % 2 + 1), 2 + s % 2, 0:SEQ]
                    v = [xtok[:, m, n * SSD_W:(n + 1) * SSD_W] for m in range(2)]
                    sets = [(out, v)]
                else:
                    v = [vtok[:, m, (n - 8) * P:(n - 7) * P] for m in range(2)]
                    sets = [(ps[:, 2 + s % 2, 0:SEQ], v), (ps[:, 4 + s % 2, 0:SEQ], [ones, ones])]
                for out, v in sets:
                    mm(out, v[0], dec[:, n % 4, 0:256], start=True, stop=False)
                    last = mm(out[:, P:256], v[1], dec[:, n % 4, 256:384], start=False, stop=True)
                last.then_inc(ry_mm.sem, 1)

            def turn(l, b, u, g):
                pe.wait_ge(*t_sb(l, 8 * b + g))
                for q in range(2):
                    for c in range(2):
                        last = nc.tensor.transpose(ps[:, 0, (2 * q + c) * P:(2 * q + c + 1) * P],
                                                   latb[u][:, 2 * g + q, c * P:(c + 1) * P], ident)
                last.then_inc(t_mm.sem, 1)

            def keys(l, b, u, g):
                if g < 7:
                    turn(l, b, u, g + 1)
                pe.wait_ge(*t_sb(l, 8 * b + (g + 1)))
                for q in range(2):
                    j = 2 * g + q
                    pe.wait_ge(*k_sq(l, PAGES * b + (j - 1)))
                    at = 2 * u
                    for half in range(2):
                        for c in range(2):
                            last = mm(ps[:, 1 + 2 * (j % 2) + half, 0:258], latT[:, g % 2, q, c, :],
                                      wk[:, 2 * c + half, at:at + 258], start=c == 0, stop=c == 1)
                    last.then_inc(k_mm.sem, 1)
                mm(ps[:, 5 + u, 8 * g:8 * g + 8], kr[:, u, g, :],
                   qrs[:, bass.ds(b, 1), :].rearrange("p o h -> p (o h)"), start=True, stop=True).then_inc(pair_mm.sem, 1)

            def context(l, b, u):
                pe.wait_ge(*p_sum(l, b + 1))
                pe.wait_ge(*cx_out(l, b - 1))
                pe.wait_ge(*mv_in(l, 16 * b + 16))
                at = 32 * u
                mm(ps[:, 7, at:at + 8], ones, sm[:, u, 16:24], start=True, stop=True)
                for j in range(PAGES):
                    mm(ps[0:4, 7, 128:384], prob[:, u, j, :], latb[u][:, j, :], start=j == 0, stop=j == PAGES - 1)
                for h in range(HEADS):
                    for m in range(2):
                        last = mm(ps[:, 7, at + 16 + h:at + 17 + h], memv[:, m, h * P:(h + 1) * P],
                                  probx[:, u, m, h:h + 1], start=m == 0, stop=m == 1)
                last.then_inc(cx_mm.sem, 1)

            def sample(l, b, u, before):
                if before is not None:
                    pe.wait_ge(*mx_in(l, b - 1))
                pe.wait_ge(*q_in(l, b + 1))
                turn(l, b, u, 0)
                for g in range(8):
                    keys(l, b, u, g)
                    if g == 2 and before is not None:
                        context(l, before, 1 - u)

            pe.sem_inc(o_mm.sem, 2)
            pe.sem_inc(pair_mm.sem, 2)
            pe.sem_inc(cx_mm.sem, 2)
            pe.wait_ge(m_sq.sem, 1)
            for k in range(KT):
                last = mm(ps[:, 0, 0:MEM], ones, pt[:, k, 0:MEM], start=k == 0, stop=k == KT - 1)
            last.then_inc(m_ss.sem, 1)
            pe.wait_ge(m_rs.sem, 1)

            with pe.Fori(0, DEPTH) as l:
                pe.wait_ge(*layer_free(l, 0))
                pe.wait_ge(*x_sq(l, 1))
                for k in range(KT):
                    last = mm(ps[:, 4, 0:T], ones, u3[:, k, :], start=k == 0, stop=k == KT - 1)
                last.then_inc(x_ss.sem, 1)
                with pe.Fori(0, FILL) as i:
                    for u in range(2):
                        pe.wait_ge(*u_ready(l, 1))
                        pe.wait_ge(*slot_in[u](l, 16 * i + 16))
                        for a in range(2):
                            pe.wait_ge(*(pj_dve if a else pj_act)(l, 2 * i + (u - 1)))
                            tile_mm(l, None, u, a, 2 * u + a)
                for m in range(4 * FILL, IN_TILES):
                    if m % 2 == 0:
                        slot(l, m // 2)
                    pe.wait_ge(*(pj_dve if m % 2 else pj_act)(l, m // 2 - 1))
                    tile_mm(l, m, (m // 2) % 2, m % 2, m % 4)
                pe.wait_ge(*mem_ready(l, 1))
                pe.wait_ge(*pj_act(l, 22))
                pe.wait_ge(*pj_dve(l, 21))
                for c in range(2):
                    w = slot(l, R_MK + c).rearrange("p (h k m) -> p h k m", h=2, k=KT)
                    for h in range(2):
                        for k in range(KT):
                            last = mm(ps[:, 2 * c + h, 0:MEM], w[:, h, k, :], memn[:, k, :], start=k == 0, stop=k == KT - 1)
                    last.then_inc(slot_free.sem, 1)
                    if c == 0:
                        sums(l, 0, 4, [[(P, nsq[0][:, i, :]) for i in range(3)], [(P, nsq[1][:, i, :]) for i in range(2)],
                                       [(ROPE, nsq[0][0:ROPE, 3, :])]])
                pe.drain().then_inc(n_in.sem, 1)
                pe.wait_ge(*n_rs(l, 1))
                for c in range(2):
                    w = slot(l, R_MV + c).rearrange("p (k n) -> p k n", k=4)
                    for m in range(2):
                        for k in range(4):
                            last = mm(ps[:, 6 + m, :], memn[:, 4 * c + k, m * P:(m + 1) * P], w[:, k, :],
                                      start=c == 0 and k == 0, stop=c == 1 and k == 3)
                    last.then_inc(slot_free.sem, 1)
                    if c == 0:
                        sums(l, 1, 4, [[(P, nsq[1][:, 2 * i:2 * i + 2, 0:MEM])] for i in range(2)], 2 * MEM)
                pe.drain().then_inc(mv_mm.sem, 1)
                pe.wait_ge(*n_rs(l, 2))
                pe.wait_ge(*g_wend(l, 1))
                for m in range(2):
                    t = slice(m * P, (m + 1) * P)
                    for at, k, row in ((0, 8, acum), (8, 8, gdt), (16, 8, wend), (24, 4, gi), (28, 4, lf)):
                        mm(ps[:, 4, 32 * m + at:32 * m + at + k], row[0:k, t], ident[0:k, 0:k], start=True, stop=True)
                for q in range(4):
                    ex = cst[0:8, K_EXP + q * P:K_EXP + (q + 1) * P]
                    mm(ps[:, 4, 64 + 8 * q:72 + 8 * q], ex, la[:, SEQ:T], start=True, stop=True)
                    mm(ps[:, 4, 96 + 8 * q:104 + 8 * q], ex, gdt[:, SEQ:T], start=True, stop=True)
                    last = mm(ps[:, 4, 128 + 24 * q:152 + 24 * q], cst[0:4, K_SEL + q * P:K_SEL + (q + 1) * P],
                              gsmall[0:4, 0:24], start=True, stop=True)
                last.then_inc(g_pe.sem, 1)
                pe.wait_ge(*n_out(l, 2))
                sums(l, 2, 0, heads(2))
                pe.wait_ge(*g_out(l, 1))
                pe.wait_ge(*mv_out(l, 1))
                for h in range(HEADS):
                    w = slot(l, R_UQ + h // 2)[:, 0:1152].rearrange("p (h k m) -> p h k m", h=2, k=Q_TILES)
                    for k in range(Q_TILES):
                        last = mm(ps[:, 4 + h, 0:T], w[:, h % 2, k, 0:P], pt[:, CQ + k, :], start=k == 0, stop=k == Q_TILES - 1)
                last.then_inc(n_in.sem, 1)
                pe.wait_ge(*n_rs(l, 3))
                sums(l, 3, 0, heads(3))
                pe.wait_ge(*n_rs(l, 4))
                for h in range(HEADS):
                    w = ring[:, h // 2, 0:1152].rearrange("p (h k m) -> p h k m", h=2, k=Q_TILES)
                    for k in range(Q_TILES):
                        last = mm(ps[0:ROPE, h, 0:T], w[:, h % 2, k, P:P + ROPE], pt[:, CQ + k, :],
                                  start=k == 0, stop=k == Q_TILES - 1)
                last.then_inc(n_in.sem, 1)
                pe.drain().then_inc(slot_free.sem, 2)
                pe.wait_ge(*n_out(l, 4))
                sums(l, 4, 4, heads(4, ROPE))
                pe.wait_ge(*n_rs(l, 5))
                pe.wait_ge(*wsm_in(l, 32))
                for h in range(HEADS):
                    for c in range(2):
                        last = mm(ps[:, 4 + h, 0:T], wk[:, 2 * c + h // 2, 2 + (h % 2) * P:2 + (h % 2 + 1) * P], pt[:, CKV + c, :],
                                  start=c == 0, stop=c == 1)
                last.then_inc(n_in.sem, 1)
                pe.wait_ge(*n_out(l, 5))
                sums(l, 5, 0, heads(5))
                pe.wait_ge(*n_out(l, 6))
                for m in range(2):
                    for c in range(2):
                        last = mm(ps[:, 5 + m, :], pt[:, CKV + c, m * P:(m + 1) * P], wsm[:, 0, c * 512:(c + 1) * 512],
                                  start=c == 0, stop=c == 1)
                last.then_inc(lv_mm.sem, 1)
                for h in range(HEADS + 1):
                    last = mm(ps[0:ROPE, h, 0:T], cst[0:ROPE, K_ROT:K_ROT + ROPE], QR[:, h, :], start=True, stop=True)
                last.then_inc(r_mm.sem, 1)
                pe.wait_ge(*r_out(l, 1))
                pe.wait_ge(*lv_out(l, 1))
                scores(l, 0)
                scores(l, 1)
                for h in range(8):
                    pe.wait_ge(*s_p(l, h + 1))
                    if h >= 2:
                        pe.wait_ge(*s_pt(l, h - 1))
                    for m in range(2):
                        for q in range(2):
                            last = nc.tensor.transpose(ps[:, 2 + h % 2, m * 256 + q * P:m * 256 + (q + 1) * P],
                                                       att[:, h % 4, q, m * P:(m + 1) * P], ident)
                    last.then_inc(s_t.sem, 1)
                    if h < 6:
                        scores(l, h + 2)
                    pe.wait_ge(*s_pt(l, h + 1))
                    if h >= 2:
                        pe.wait_ge(*s_o(l, h - 1))
                    v = memV if h < 4 else mlaV
                    for m in range(2):
                        last = mm(ps[:, 4 + h % 2, 0:SEQ], v[:, m, (h % 4) * P:(h % 4 + 1) * P], attT[:, h % 2, m, :],
                                  start=m == 0, stop=m == 1)
                    last.then_inc(s_y.sem, 1)
                pe.wait_ge(*pre_in(l, 1))
                for h in range(HEADS):
                    for c in range(2):
                        at = (c * 4 + h) * NB
                        mm(ps[:, 6, at:at + NB], wsm[:, 1, h * 256 + c * P:h * 256 + (c + 1) * P],
                           pre[:, 0, h * NB:(h + 1) * NB], start=True, stop=True)
                mm(ps[:, 6, 64:96], ones, pre[:, 1, :], start=True, stop=False)
                mm(ps[:, 6, 64:96], ones[0:ROPE, :], pre[0:ROPE, 2, :], start=False, stop=True).then_inc(pre_mm.sem, 1)
                for h in range(HEADS):
                    last = mm(ps[0:NB, 7, h * P:(h + 1) * P], pt[:, XQ + h, SEQ:T], ident, start=True, stop=True)
                last.then_inc(pre_mm.sem, 1)
                wq = slot(l, R_MLQK)[:, 0:1024].rearrange("p (a h m) -> p a h m", a=2, h=4)
                pe.wait_ge(*s_o(l, 8))
                pe.wait_ge(*pre_out(l, 1))
                pe.wait_ge(*xc_ready(l, 1))
                for h in range(HEADS):
                    last = mm(ps[:, h, 0:T], wq[:, 0, h, :], xc[:, 8 + h, :], start=True, stop=True)
                last.then_inc(tok_mm.sem, 1)
                pe.wait_ge(*tok_act(l, 1))
                for h in range(HEADS):
                    last = mm(ps[:, h, 0:T], wq[:, 1, h, :], xc[:, 8 + h, :], start=True, stop=True)
                last.then_inc(tok_mm.sem, 1)
                for m in range(2):
                    for h in range(HEADS):
                        last = mm(ps[:, 4 + m, h * P:(h + 1) * P], xc[:, 8 + h, m * P:(m + 1) * P], wq[:, 1, h, :],
                                  start=True, stop=True)
                last.then_inc(tok_mm.sem, 1)
                pe.drain().then_inc(slot_free.sem, 1)
                wvl = slot(l, R_MLV)[:, 0:512].rearrange("p (h m) -> p h m", h=4)
                pe.wait_ge(*tok_act(l, 2))
                for m in range(2):
                    for h in range(HEADS):
                        last = mm(ps[:, m, h * P:(h + 1) * P], pt[:, 8 + h, m * P:(m + 1) * P], wvl[:, h, :],
                                  start=True, stop=True)
                last.then_inc(tok_mm.sem, 1)
                for m in range(2):
                    for h in range(4):
                        last = nc.tensor.transpose(ps[:, 2 + m, h * P:(h + 1) * P], xc[:, h, m * P:(m + 1) * P], ident)
                last.then_inc(tok_mm.sem, 1)
                pe.wait_ge(*pre_row(l, 1))
                pe.wait_ge(*tok_act(l, 3))
                for m in range(2):
                    for h in range(2):
                        last = nc.tensor.transpose(ps[:, 4, m * 256 + h * P:m * 256 + (h + 1) * P],
                                                   xc[:, 4 + h, m * P:(m + 1) * P], ident)
                last.then_inc(tok_mm.sem, 1)
                for h in range(HEADS):
                    last = mm(ps[:, 7, h * NB:(h + 1) * NB], wvl[:, h, :], pt[:, 8 + h, SEQ:T], start=True, stop=True)
                last.then_inc(tok_mm.sem, 1)
                pe.drain().then_inc(slot_free.sem, 1)
                pe.wait_ge(*tok_dve(l, 2))
                for bank, tiles in ((0, xc[:, 4:8, :]), (1, mlk), (2, mlq)):
                    for h in range(4):
                        last = mm(ps[0:NB, bank, h * P:(h + 1) * P], tiles[:, h, SEQ:T], ident, start=True, stop=True)
                last.then_inc(pre_mm.sem, 1)
                pe.wait_ge(*tok_act(l, 4))
                pe.wait_ge(*tok_dve(l, 3))
                pe.wait_ge(*weighted(l, 1))
                masked(l, 0)
                pe.wait_ge(*pre_row(l, 2))
                spread(l, 0)
                spread(l, 1)
                for n in range(12):
                    if n + 1 in (4, 8, 9, 10, 11):
                        masked(l, 1 if n + 1 == 4 else n - 5)
                    recur(l, n)
                    if n < 10:
                        spread(l, n + 2)
                pe.wait_ge(*seg_out(l, 12))
                pe.wait_ge(*em_out(l, 4))
                for q in range(4):
                    for m in range(2):
                        mm(ps[:, 0, q * P:(q + 1) * P], xw[:, m, q * P:(q + 1) * P], btok[:, m, (q // 2) * P:(q // 2 + 1) * P],
                           start=m == 0, stop=m == 1)
                for h in range(HEADS):
                    for m in range(2):
                        mm(ps[:, 1, h * P:(h + 1) * P], vw[:, m, h * P:(h + 1) * P], ktok[:, m, h * P:(h + 1) * P],
                           start=m == 0, stop=m == 1)
                pe.wait_ge(*ry_out(l, 8))
                for h in range(HEADS):
                    for m in range(2):
                        last = mm(ps[0:1, 2, h * P:(h + 1) * P], cols[:, m, 28 + h:29 + h], ktok[:, m, h * P:(h + 1) * P],
                                  start=m == 0, stop=m == 1)
                last.then_inc(fin_mm.sem, 1)
                pe.wait_ge(*fin_out(l, 1))
                pe.wait_ge(*lat_in[0](l, 512))
                sample(l, 0, 0, None)
                with pe.Fori(0, NB // 2 - 1) as i:
                    for u in (1, 0):
                        pe.wait_ge(*lat_in[u](l, 512 * i + (512 if u else 1024)))
                        b = 2 * i + (1 if u else 2)
                        sample(l, b, u, b - 1)
                pe.wait_ge(*lat_in[1](l, 2048))
                sample(l, NB - 1, 1, NB - 2)
                pe.wait_ge(*ns_in(l, 1))
                mm(ps[:, 0, 0:32], ones, pre[:, 0, :], start=True, stop=True).then_inc(nq_mm.sem, 1)
                context(l, NB - 1, 1)
                sums(l, 6, 4, [[(P, nsq[0][:, 2 * i + j, :]) for j in range(2)] for i in range(2)])
                sums(l, 7, 0, heads(7))
                pe.wait_ge(*cx_out(l, NB))
                for c in range(2):
                    for b in range(NB):
                        at = (c * NB + b) * 4
                        last = mm(ps[:, 6, at:at + 4], ctxr[:, b, c * P:(c + 1) * P], ident[0:4, 0:4], start=True, stop=True)
                last.then_inc(cr_mm.sem, 1)
                pe.wait_ge(*cr_out(l, 1))
                for h in range(HEADS):
                    for c in range(2):
                        last = mm(ps[:, 6, 64 + h * NB:64 + (h + 1) * NB], wsm[:, 0, c * 512 + h * P:c * 512 + (h + 1) * P],
                                  ctxall[:, c, h, :], start=c == 0, stop=c == 1)
                last.then_inc(uv_mm.sem, 1)
                with pe.Fori(0, OUT_TILES // 2) as i:
                    for c in range(2):
                        pe.wait_ge(*mixed(l, 1))
                        pe.wait_ge(*slot_in[c](l, 16 * i + 16 * (R_OUT // 2 + 1)))
                        pe.wait_ge(*o_out(l, 2 * i + (c - 1)))
                        w = ring[:, c, :].rearrange("p (k m) -> p k m", k=MIX_TILES)
                        for k in range(MIX_TILES):
                            last = mm(ps[:, c, 0:T], w[:, k, :], pt[:, Z + k, :], start=k == 0, stop=k == MIX_TILES - 1)
                        last.then_inc(o_mm.sem, 1)
                pe.drain().then_inc(layer_free.sem, 1)
            pe.wait_ge(f_sq.sem, 1)
            for k in range(KT):
                last = mm(ps[:, 4, 0:T], ones, u3[:, k, :], start=k == 0, stop=k == KT - 1)
            last.then_inc(f_ss.sem, 1)

        @block.scalar
        def _(act):
            fn = nc.scalar.activation

            def root(out, mean, scale=1.0):
                fn(out, mean, ACT.Ln, bias=eps[0:out.shape[0]], scale=scale)
                act.drain()
                return fn(out, out, ACT.Exp, scale=-0.5)

            def squares(l, k, parts):
                if k:
                    act.wait_ge(*n_ss(l, max(k - 1, 1)))
                for i, (rows_, first_tile, src, n) in enumerate(parts):
                    tiles, width = src.shape[1], src.shape[2]
                    last = fn(nsq[k % 2 if k else i % 2][0:rows_, first_tile:first_tile + tiles, 0:width],
                              src, ACT.Square, scale=n ** -0.5)
                last.then_inc(n_sq.sem, 1)

            def roots(l, k, out, mean):
                act.wait_ge(*n_ss(l, k + 1))
                if k:
                    act.wait_ge(*n_out(l, k))
                root(out, mean).then_inc(n_rs.sem, 1)

            def probs(l, h):
                act.wait_ge(*s_max(l, h + 1))
                for q in range(2):
                    last = fn(att[:, h % 4, q, :], att[:, h % 4, q, :], ACT.Exp, bias=asm[:, h % 4, q:q + 1],
                              accum_out=asm[:, h % 4, 2 + q:3 + q])
                last.then_inc(s_exp.sem, 1)

            def copy_pair(l, b, g):
                act.wait_ge(*t_mm(l, 8 * b + (g + 1)))
                act.wait_ge(*pair_mm(l, 8 * b + (g - 1)))
                fn(latT[:, g % 2], ps[:, 0, :], ACT.Copy).then_inc(t_sb.sem, 1)

            def square(l, b, j, u):
                n = PAGES * b + j
                act.wait_ge(*k_mm(l, n + 1))
                first_bank, scores_at, keys_at = 1 + 2 * (j % 2), 256 * u, 2 - 2 * u
                fn(raws[:, u, j, :].rearrange("p (a h) -> p a h", a=2),
                   ps[:, first_bank:first_bank + 2, scores_at:scores_at + 2], ACT.Copy)
                act.wait_ge(*k_red(l, n - 1))
                fn(sqd[:, j % 2, :].rearrange("p (a n) -> p a n", a=2),
                   ps[:, first_bank:first_bank + 2, keys_at:keys_at + 256], ACT.Square).then_inc(k_sq.sem, 1)

            def key_roots(l, b, u):
                act.wait_ge(*k_red(l, PAGES * b + PAGES))
                root(ssq[:, u], ssq[:, u], 1.0 / P).then_inc(k_rs.sem, 1)

            def exps(l, b, u):
                act.wait_ge(*s_sub(l, b + 1))
                fn(prob[:, u], prob[:, u], ACT.Exp, scale=MLA_SCALE)
                fn(probx[:, u], probx[:, u], ACT.Exp, scale=X_SCALE)
                fn(sm[:, u, 24:28], sm[:, u, 24:28], ACT.Exp, scale=MLA_SCALE).then_inc(p_exp.sem, 1)

            def save_states(l, b, u):
                act.wait_ge(*st_new(l, b + 1))
                for s, name in ((0, "o_ssm_s"), (1, "o_C_s")):
                    act.dma_start(d[name][bass.ds(l * NB + b, 1)].rearrange("o p n -> p (o n)"), states[:, u, s, :]
                                  ).then_inc(st_saved[u].sem, 16)

            def sample(l, b, u, before):
                copy_pair(l, b, 0)
                if before is not None:
                    save_states(l, before, 1 - u)
                    key_roots(l, before, 1 - u)
                for g in range(8):
                    if g < 7:
                        copy_pair(l, b, g + 1)
                    square(l, b, 2 * g, u)
                    square(l, b, 2 * g + 1, u)
                    if g == 1 and before is not None:
                        exps(l, before, 1 - u)

            nc.scalar.preload_act_table_set(LN_EXP)
            act.sem_inc(pj_act.sem, 2)
            act.sem_inc(t_sb.sem, 1)
            act.sem_inc(k_sq.sem, 2)
            act.wait_ge(m_ss.sem, 1)
            root(rsm[:, :], ps[:, 0, 0:MEM], 1.0 / D_MODEL).then_inc(m_rs.sem, 1)
            with act.Fori(0, DEPTH) as l:
                act.wait_ge(*layer_free(l, 0))
                act.wait_ge(*x_ss(l, 1))
                root(nrs[:, 0, :], ps[:, 4, 0:T], 1.0 / D_MODEL).then_inc(x_rs.sem, 1)
                with act.Fori(0, FILL) as i:
                    for u in range(2):
                        act.wait_ge(*pj_mm(l, 4 * i + (2 * u + 1)))
                        fn(pt[:, bass.ds(4 * i + 2 * u, 1), :].rearrange("p o t -> p (o t)"), ps[:, 2 * u, 0:T], ACT.Copy
                           ).then_inc(pj_act.sem, 1)
                for m in (40, 42):
                    act.wait_ge(*pj_mm(l, m + 1))
                    fn(pt[:, m, :], ps[:, m % 4, 0:T], ACT.Copy).then_inc(pj_act.sem, 1)
                act.drain()
                act.wait_ge(*pj_dve(l, 21))
                squares(l, 0, ((P, 0, pt[:, CQ:CQ + 3, :], 3 * P), (P, 0, pt[:, CKV:CKV + 2, :], 2 * P),
                               (ROPE, 3, pt[0:ROPE, KR:KR + 1, :], ROPE)))
                act.wait_ge(*par_in(l, 16))
                fn(gdt[:, :], pt[0:8, GATE, :], ACT.Copy)
                fn(li[0:4, :], pt[32:36, GATE, :], ACT.Copy)
                fn(lf[0:4, :], pt[64:68, GATE, :], ACT.Copy).then_inc(g_raw.sem, 1)
                for c in range(CT):
                    last = fn(xc[:, c, 0:SEQ], pt[:, c, 0:SEQ], ACT.Identity, bias=par[:, C_CB + c:C_CB + c + 1],
                              scale=par[:, C_CW + 3 * CT + c:C_CW + 3 * CT + c + 1])
                last.then_inc(conv_a.sem, 1)
                act.wait_ge(*g_neg(l, 1))
                fn(softp[:, 0, :], softp[:, 0, :], ACT.Exp)
                fn(softp[0:4, 1, :], softp[0:4, 1, :], ACT.Exp)
                fn(gsmall[:, 32:33], par[0:8, C_ALOG:C_ALOG + 1], ACT.Exp)
                act.drain()
                fn(softp[:, 0, :], softp[:, 0, :], ACT.Ln, bias=1.0)
                fn(softp[0:4, 1, :], softp[0:4, 1, :], ACT.Ln, bias=1.0).then_inc(g_log.sem, 1)
                roots(l, 0, nrs[:, 0:3, :], ps[:, 4:7, 0:T])
                fn(pt[:, Z:Z + 16, :], pt[:, Z:Z + 16, :], ACT.Silu)
                fn(pt[:, OG:OG + 4, :], pt[:, OG:OG + 4, :], ACT.Sigmoid).then_inc(z_ready.sem, 1)
                nc.scalar.preload_act_table_set(LN_EXP)
                act.wait_ge(*g_scan(l, 1))
                fn(wend[:, 0:SEQ], acum[:, 0:SEQ], ACT.Exp, bias=acum[:, SEQ - 1:SEQ], scale=-1.0)
                fn(lf[0:4, 0:SEQ], gi[0:4, 0:SEQ], ACT.Exp, bias=nmx[0:4, SEQ - 1:SEQ])
                fn(la[:, SEQ:T], la[:, SEQ:T], ACT.Exp)
                fn(gsmall[0:4, 0:24], gsmall[0:4, 0:24], ACT.Exp).then_inc(g_exp.sem, 1)
                act.wait_ge(*n_in(l, 1))
                squares(l, 1, ((P, 0, ps[:, 0:4, 0:MEM], P),))
                squares(l, 2, ((P, 0, pt[:, XQ:XQ + 4, :], P),))
                act.wait_ge(*n_ss(l, 2))
                roots(l, 1, nrs[:, :, 0:MEM].rearrange("p (a h) t -> p a h t", a=2),
                      ps[:, 4:6, :].rearrange("p a (h t) -> p a h t", h=2))
                act.wait_ge(*mv_mm(l, 1))
                fn(memV, ps[:, 6:8, :], ACT.Copy).then_inc(mv_out.sem, 1)
                roots(l, 2, nrs, ps[:, 0:4, 0:T])
                for k, n, at, to in ((3, P, 4, 0), (4, ROPE, 0, 4), (5, P, 4, 0)):
                    act.wait_ge(*n_in(l, k - 1))
                    squares(l, k, ((n, 0, ps[0:n, at:at + 4, 0:T], n),))
                    roots(l, k, nrs[0:n], ps[0:n, to:to + 4, 0:T])
                act.wait_ge(*lv_mm(l, 1))
                fn(mlaV, ps[:, 5:7, :], ACT.Copy).then_inc(lv_out.sem, 1)
                probs(l, 0)
                probs(l, 1)
                for h in range(8):
                    act.wait_ge(*s_t(l, h + 1))
                    if h >= 2:
                        act.wait_ge(*s_y(l, h - 1))
                    fn(attT[:, h % 2], ps[:, 2 + h % 2, :], ACT.Copy).then_inc(s_pt.sem, 1)
                    if h < 6:
                        probs(l, h + 2)
                act.wait_ge(*conv_d(l, 1))
                fn(xc[:, :, :], xc[:, :, :], ACT.Silu).then_inc(xc_ready.sem, 1)
                nc.scalar.preload_act_table_set(LN_EXP)
                act.wait_ge(*conv_saved(l, 16))
                act.wait_ge(*kv_saved(l, 32))
                act.wait_ge(*tok_mm(l, 1))
                fn(mlq, ps[:, 0:4, 0:T], ACT.Copy).then_inc(tok_act.sem, 1)
                act.wait_ge(*tok_mm(l, 2))
                fn(mlk, ps[:, 0:4, 0:T], ACT.Copy, scale=K_SCALE).then_inc(tok_act.sem, 1)
                act.wait_ge(*tok_mm(l, 3))
                fn(ktok, ps[:, 4:6, :], ACT.Copy, scale=K_SCALE).then_inc(tok_act.sem, 1)
                act.wait_ge(*tok_mm(l, 6))
                fn(btok[:, :, :], ps[:, 4, :].rearrange("p (m n) -> p m n", m=2), ACT.Copy).then_inc(tok_act.sem, 1)
                for n in range(12):
                    act.wait_ge(*seg_out(l, n + 1))
                    fn(dec[:, n % 4, :], dec[:, n % 4, :], ACT.Exp).then_inc(seg_exp.sem, 1)
                    if n >= 8:
                        if n >= 10:
                            act.wait_ge(*ry_out(l, n - 5))
                        fn(emm[:, n % 2, :], ps[:, n % 2, 256:512], ACT.Exp, scale=-1.0).then_inc(em_out.sem, 1)
                act.wait_ge(*fin_mm(l, 1))
                fn(A1[:, 0:1024], ps[:, 0:2, :], ACT.Copy)
                fn(A1[0:1, 1024:1536], ps[0:1, 2, :], ACT.Copy).then_inc(fin_out.sem, 1)
                sample(l, 0, 0, None)
                with act.Fori(0, NB // 2 - 1) as i:
                    for u in (1, 0):
                        b = 2 * i + (1 if u else 2)
                        sample(l, b, u, b - 1)
                sample(l, NB - 1, 1, NB - 2)
                save_states(l, NB - 1, 1)
                key_roots(l, NB - 1, 1)
                exps(l, NB - 1, 1)
                act.wait_ge(*a_ready(l, 1))
                squares(l, 6, ((P, 0, xc[:, 0:4, :], 2 * P),))
                squares(l, 7, ((P, 0, xc[:, 8:12, :], P),))
                act.wait_ge(*n_ss(l, 7))
                root(nrs[:, 0:2, :], ps[:, 4:6, 0:T]).then_inc(n_rs.sem, 1)
                act.wait_ge(*n_ss(l, 8))
                root(nrs_ml, ps[:, 0:4, 0:T]).then_inc(n_rs.sem, 1)
                act.drain().then_inc(layer_free.sem, 1)
            for u in range(2):
                act.wait_ge(*st_saved[u](DEPTH - 1, 32 * 4))
            act.wait_ge(f_ss.sem, 1)
            root(nrs[:, 0, :], ps[:, 4, 0:T], 1.0 / D_MODEL).then_inc(f_rs.sem, 1)

        @block.vector
        def _(dve):
            tt, ts, stt = nc.vector.tensor_tensor, nc.vector.tensor_scalar, nc.vector.scalar_tensor_tensor
            red, copy = nc.vector.tensor_reduce, nc.vector.tensor_copy

            def col(i, k=P):
                return par[0:k, i:i + 1]

            def over(ap, n, axis=2):
                v = ap.unsqueeze(axis)
                shape = list(v.shape)
                shape[axis] = n
                return v.broadcast_to(shape)

            def at_b(t, b):
                return t[:, bass.ds(b, 1), :].rearrange("p o h -> p (o h)")

            def seg(l, n):
                dve.wait_ge(*bc_mm(l, n + 1))
                if n >= 4:
                    dve.wait_ge(*ry_mm(l, n - 3))
                c, op = (n, ALU.subtract) if n < 8 else (24 + n - 8, ALU.add)
                ts(dec[:, n % 4, 0:256], ps[:, spread_bank(n), 0:256], cols[:, 0, c:c + 1], 0.0, op, ALU.min)
                ts(dec[:, n % 4, 256:384], ps[:, spread_bank(n), P:256], cols[:, 1, c:c + 1], 0.0, op, ALU.min
                   ).then_inc(seg_out.sem, 1)

            def rec_out(l, n):
                if n < 8 and n % 2 == 0:
                    return
                dve.wait_ge(*ry_mm(l, n + 1))
                if n < 8:
                    q = n // 2
                    stt(xc[:, q, 0:SEQ], xc[:, q, 0:SEQ], col(C_D + q), ps[:, 2 + q % 2, 0:SEQ], ALU.mult, ALU.add
                        ).then_inc(ry_out.sem, 1)
                else:
                    h = n - 8
                    dve.wait_ge(*em_out(l, h + 1))
                    e = emm[:, n % 2, :]
                    stt(e, ps[:, 4 + h % 2, 0:SEQ], -1.0, e, ALU.mult, ALU.max)
                    dve.drain()
                    tt(e, ps[:, 4 + h % 2, 0:SEQ], e, ALU.max)
                    dve.drain()
                    nc.vector.reciprocal(e, e)
                    dve.drain()
                    tt(xc[:, 8 + h, 0:SEQ], ps[:, 2 + h % 2, 0:SEQ], e, ALU.mult).then_inc(ry_out.sem, 1)

            def key_sum(l, b, u, j):
                dve.wait_ge(*k_sq(l, PAGES * b + (j + 1)))
                red(ssq[:, u, j, :], sqd[:, j % 2, :].rearrange("p (h n) -> p h n", h=4), AXX, ALU.add
                    ).then_inc(k_red.sem, 1)

            def update(l, b, u, s):
                st = states[:, u, s, :].rearrange("p (h n) -> p h n", h=4)
                if s == 0:
                    for g in range(2):
                        tt(dtmp[:, g * 256:(g + 1) * 256].rearrange("p (r n) -> p r n", r=2),
                           over(rows[:, g * P:(g + 1) * P], 2, 1),
                           over(dtx[:, bass.ds(b, 1), 2 * g:2 * g + 2].rearrange("p o h -> p (o h)"), P), ALU.mult)
                else:
                    tt(dtmp[:, :].rearrange("p (h n) -> p h n", h=4),
                       rows[:, ROW_K:ROW_K + 512].rearrange("p (h n) -> p h n", h=4), over(at_b(wv, b), P), ALU.mult)
                dve.drain()
                tt(states[:, u, s, :], states[:, u, s, :], dtmp[:, :], ALU.add)
                dve.drain()
                if s == 0:
                    for g in range(2):
                        tt(dtmp[:, g * 256:(g + 1) * 256].rearrange("p (r n) -> p r n", r=2), st[:, 2 * g:2 * g + 2, :],
                           over(rows[:, ROW_C + g * P:ROW_C + (g + 1) * P], 2, 1), ALU.mult)
                else:
                    last = tt(dtmp[:, :], states[:, u, s, :], rows[:, ROW_Q:ROW_Q + 512], ALU.mult)
                    last.then_inc(st_new.sem, 1)
                dve.drain()
                last = red(at_b(ysa if s == 0 else ysb, b), dtmp[:, :].rearrange("p (h n) -> p h n", h=4), AXX, ALU.add)
                return last

            def mem_scores(l, b, u):
                dve.wait_ge(*mk_in(l, 16 * b + 16))
                k = memk.rearrange("p (m n) -> p m n", m=2)
                tt(k, k, over(rows[:, ROW_X:ROW_X + 512], 2, 1), ALU.mult)
                dve.drain()
                red(sx[:, u].rearrange("p m h -> p (m h)"), memk.rearrange("p (a n) -> p a n", a=8), AXX, ALU.add
                    ).then_inc(memk_used.sem, 1)

            def softmax_max(l, b, u):
                dve.wait_ge(*k_rs(l, b + 1))
                dve.wait_ge(*pair_mm(l, 8 * b + 8))
                rot = ps[:, 5 + u, 0:64].rearrange("p (j a h) -> p a j h", a=2, h=4)
                tt(prob[:, u], raws[:, u], ssq[:, u], ALU.mult)
                dve.drain()
                s = prob[:, u].rearrange("p (a j) h -> p a j h", a=2)
                tt(s, rot, s, ALU.add)
                dve.drain()
                red(sm[:, u, 0:4], prob[:, u].rearrange("p j h -> p h j"), AXX, ALU.max)
                red(sm[:, u, 4:8], sx[:, u].rearrange("p m h -> p h m"), AXX, ALU.max).then_inc(mx_in.sem, 1)

            def softmax_shift(l, b, u):
                dve.wait_ge(*mx_all(l, b + 1))
                tt(sm[:, u, 8:12], sm[:, u, 8:12], at_b(scur, b), ALU.max)
                dve.drain()
                tt(prob[:, u], prob[:, u], over(sm[:, u, 8:12], PAGES, 1), ALU.subtract)
                tt(probx[:, u], sx[:, u], over(sm[:, u, 12:16], 2, 1), ALU.subtract)
                tt(sm[:, u, 24:28], at_b(scur, b), sm[:, u, 8:12], ALU.subtract).then_inc(s_sub.sem, 1)

            def softmax_sum(l, b, u):
                dve.wait_ge(*p_exp(l, b + 1))
                red(sm[:, u, 16:20], prob[:, u].rearrange("p j h -> p h j"), AXX, ALU.add)
                red(sm[:, u, 20:24], probx[:, u].rearrange("p m h -> p h m"), AXX, ALU.add).then_inc(p_sum.sem, 1)

            def context_out(l, b, u):
                dve.wait_ge(*cx_mm(l, b + 1))
                at = 32 * u
                own = sm[:, u, 24:28]
                copy(at_b(owns, b), own)
                tt(at_b(dens, b), ps[:, 7, at:at + 4], own, ALU.add)
                nc.vector.reciprocal(sm[:, u, 36:40], ps[:, 7, at + 4:at + 8])
                copy(ctxr[:, bass.ds(b, 1), :].rearrange("p o n -> p (o n)"), ps[0:4, 7, 128:384])
                dve.drain()
                tt(at_b(ysd, b), ps[:, 7, at + 16:at + 20], sm[:, u, 36:40], ALU.mult).then_inc(cx_out.sem, 1)

            def query(l, b, u):
                copy(wk[:, :, 258 * u:258 * u + 2], qabs[:, bass.ds(b, 1), :, :].rearrange("p o c (a h) -> p (o c a) h", a=2)
                     ).then_inc(q_in.sem, 1)

            def sample(l, b, u, before, more=True):
                if before is not None:
                    softmax_max(l, before, 1 - u)
                for j in range(PAGES):
                    key_sum(l, b, u, j)
                    if before is not None:
                        if j == 1:
                            softmax_shift(l, before, 1 - u)
                        if j == 2 and more:
                            query(l, b + 1, 1 - u)
                        if j == 3:
                            softmax_sum(l, before, 1 - u)
                        if j == 7:
                            context_out(l, before, 1 - u)
                    if j == 9:
                        dve.wait_ge(*rows_in(l, 16 * b + 16))
                        mem_scores(l, b, u)
                    if j == 11:
                        dve.wait_ge(*decayed(l, b + 1))
                        update(l, b, u, 0)
                    if j == 14:
                        update(l, b, u, 1).then_inc(rows_used.sem, 1)

            dve.sem_inc(layer_free.sem, 4)
            dve.sem_inc(pj_dve.sem, 2)
            dve.sem_inc(k_red.sem, 2)
            dve.sem_inc(mx_in.sem, 2)
            dve.sem_inc(cx_out.sem, 2)
            dve.sem_inc(o_out.sem, 2)
            for u in range(2):
                dve.sem_inc(st_saved[u].sem, 32)
            nc.vector.memset(qrs[:, :, :], 0.0)
            dve.wait_ge(first.sem, 64)
            tt(pt[:, 0:8, 0:MEM], memn, memn, ALU.mult).then_inc(m_sq.sem, 1)
            dve.wait_ge(m_rs.sem, 1)

            with dve.Fori(0, DEPTH) as l:
                dve.wait_ge(*layer_free(l, 0))
                dve.wait_ge(*par_in(l, 16))
                tt(u3, xT[:, :, :], xT[:, :, :], ALU.mult).then_inc(x_sq.sem, 1)
                dve.wait_ge(*x_rs(l, 1))
                for k in range(KT):
                    last = stt(u3[:, k, :], xT[:, k, :], col(C_NORM + k), nrs[:, 0, :], ALU.mult, ALU.mult)
                last.then_inc(u_ready.sem, 1)
                dve.wait_ge(*mem_in(l, 16))
                for k in range(KT):
                    last = stt(memn[:, k, :], memn[:, k, :], col(C_MEM + k), rsm[:, :], ALU.mult, ALU.mult)
                last.then_inc(mem_ready.sem, 1)
                with dve.Fori(0, FILL) as i:
                    for u in range(2):
                        dve.wait_ge(*pj_mm(l, 4 * i + (2 * u + 2)))
                        copy(pt[:, bass.ds(4 * i + (2 * u + 1), 1), :].rearrange("p o t -> p (o t)"), ps[:, 2 * u + 1, 0:T]
                             ).then_inc(pj_dve.sem, 1)
                dve.wait_ge(*pj_mm(l, 42))
                copy(pt[:, 41, :], ps[:, 1, 0:T]).then_inc(pj_dve.sem, 1)
                dve.drain()
                dve.wait_ge(*pj_act(l, 22))
                dve.wait_ge(*g_raw(l, 1))
                ts(gdt[:, :], gdt[:, :], col(C_DTB, 8), None, ALU.add)
                ts(li[0:4, :], li[0:4, :], col(C_BI, 4), None, ALU.add)
                ts(lf[0:4, :], lf[0:4, :], col(C_BF, 4), None, ALU.add)
                dve.drain()
                stt(softp[:, 0, :], gdt[:, :], -1.0, gdt[:, :], ALU.mult, ALU.min)
                stt(softp[0:4, 1, :], lf[0:4, :], -1.0, lf[0:4, :], ALU.mult, ALU.min).then_inc(g_neg.sem, 1)
                dve.wait_ge(*n_rs(l, 1))
                for i, tile, g, n in ((0, CQ, C_Q, 3), (1, CKV, C_KV, 2)):
                    for c in range(n):
                        stt(pt[:, tile + c, :], pt[:, tile + c, :], col(g + c), nrs[:, i, :], ALU.mult, ALU.mult)
                stt(QR[:, HEADS, :], pt[0:ROPE, KR, :], col(C_KNR, ROPE), nrs[0:ROPE, 2, :], ALU.mult, ALU.mult
                    ).then_inc(n_out.sem, 1)
                def tap(j):
                    s = 3 - j
                    if j < 2:
                        dve.drain()
                    for c in range(CT):
                        stt(xc[:, c, s:SEQ], pt[:, c, 0:SEQ - s], col(C_CW + j * CT + c), xc[:, c, s:SEQ], ALU.mult, ALU.add)

                dve.wait_ge(*conv_a(l, 1))
                tap(2)
                dve.wait_ge(*g_log(l, 1))
                stt(gdt[:, :], gdt[:, :], 0.0, softp[:, 0, :], ALU.max, ALU.add)
                stt(lf[0:4, :], lf[0:4, :], 0.0, softp[0:4, 1, :], ALU.min, ALU.subtract)
                dve.drain()
                ts(la[:, :], gdt[:, :], gsmall[:, 32:33], -1.0, ALU.mult, ALU.mult)
                dve.drain()
                one8 = cst[0:8, K_ONE:K_ONE + SEQ]
                scan = nc.vector.tensor_tensor_scan
                scan(acum[:, 0:SEQ], one8, la[:, 0:SEQ], 0.0, ALU.mult, ALU.add)
                scan(mT[0:4, 0:SEQ], one8[0:4], lf[0:4, 0:SEQ], 0.0, ALU.mult, ALU.add)
                tt(lf[0:4, SEQ:T], lf[0:4, SEQ:T], par[0:4, C_M0:C_M0 + NB], ALU.add)
                dve.drain()
                tt(gi[0:4, 0:SEQ], li[0:4, 0:SEQ], mT[0:4, 0:SEQ], ALU.subtract)
                tt(mT[0:4, SEQ:T], lf[0:4, SEQ:T], li[0:4, SEQ:T], ALU.max)
                dve.drain()
                scan(nmx[0:4, 0:SEQ], one8[0:4], gi[0:4, 0:SEQ], 0.0, ALU.mult, ALU.max)
                tt(gsmall[0:4, 0:8], lf[0:4, SEQ:T], mT[0:4, SEQ:T], ALU.subtract)
                tt(gsmall[0:4, 8:16], li[0:4, SEQ:T], mT[0:4, SEQ:T], ALU.subtract)
                ts(gsmall[0:4, 16:24], mT[0:4, SEQ:T], -1.0, None, ALU.mult)
                dve.drain()
                tt(mT[0:4, 0:SEQ], mT[0:4, 0:SEQ], nmx[0:4, 0:SEQ], ALU.add)
                dve.drain()
                ts(nmx[0:4, 0:SEQ], nmx[0:4, 0:SEQ], -1.0, None, ALU.mult).then_inc(g_scan.sem, 1)
                dve.wait_ge(*g_exp(l, 1))
                tt(wend[:, 0:SEQ], wend[:, 0:SEQ], gdt[:, 0:SEQ], ALU.mult).then_inc(g_wend.sem, 1)
                tap(1)
                dve.wait_ge(*n_rs(l, 2))
                stt(mkT, ps[:, 0:4, 0:MEM], col(C_XK), nrs[:, :, 0:MEM], ALU.mult, ALU.mult).then_inc(n_out.sem, 1)
                dve.wait_ge(*g_pe(l, 1))
                bank = ps[:, 4, :]
                copy(cols[:, :, :], bank[:, 0:64].rearrange("p (m n) -> p m n", m=2))
                copy(da[:, :, :], bank[:, 64:96].rearrange("p (q b) -> p b q", q=4))
                copy(dtx[:, :, :], bank[:, 96:128].rearrange("p (q b) -> p b q", q=4))
                copy(gb[:, :, :, :].rearrange("p k b h -> p h k b"), bank[:, 128:224].rearrange("p (h k b) -> p h k b", h=4, k=3)
                     ).then_inc(g_out.sem, 1)
                tap(0)
                dve.drain()
                now = xc[:, :, SEQ:T]
                t = dtmp[:, 0:96].rearrange("p (c b) -> p c b", b=NB)
                old = par[:, C_ST:].rearrange("p (c j b) -> p j c b", j=3, b=NB)
                tt(now, pt[:, 0:CT, SEQ:T], over(par[:, C_CW + 3 * CT:C_CW + 4 * CT], NB), ALU.mult)
                dve.drain()
                tt(now, now, over(par[:, C_CB:C_CB + CT], NB), ALU.add)
                for j in range(3):
                    tt(t, old[:, j], over(par[:, C_CW + j * CT:C_CW + (j + 1) * CT], NB), ALU.mult)
                    dve.drain()
                    last = tt(now, now, t, ALU.add)
                    if j < 2:
                        dve.drain()
                last.then_inc(conv_d.sem, 1)
                dve.wait_ge(*n_rs(l, 3))
                stt(pt[:, XQ:XQ + 4, :], pt[:, XQ:XQ + 4, :], col(C_XQ), nrs, ALU.mult, ALU.mult).then_inc(n_out.sem, 1)
                dve.wait_ge(*conv_saved(l, 16))
                for k, dst, g, n, at in ((3, qn, C_QNN, P, 4), (4, QR[:, 0:4, :], C_QNR, ROPE, 0), (5, kn, C_KNN, P, 4)):
                    dve.wait_ge(*n_rs(l, k + 1))
                    stt(dst, ps[0:n, at:at + 4, 0:T], col(g, n), nrs[0:n], ALU.mult, ALU.mult).then_inc(n_out.sem, 1)
                dve.wait_ge(*r_mm(l, 1))
                t = scr[0:ROPE, 0:5 * T].rearrange("p (h t) -> p h t", h=5)
                cos, sin = (over(cst[0:ROPE, i:i + T], 5, 1) for i in (K_COS, K_SIN))
                tt(t, ps[0:ROPE, 0:5, 0:T], sin, ALU.mult)
                tt(QR[:, :, :], QR[:, :, :], cos, ALU.mult)
                dve.drain()
                tt(QR[:, :, :], QR[:, :, :], t, ALU.add).then_inc(r_out.sem, 1)
                dve.drain()

                def att_max(h):
                    x = h < 4
                    dve.wait_ge(*s_mm(l, h + 1))
                    if h >= 4:
                        dve.wait_ge(*s_t(l, h - 3))
                    for q in range(2):
                        src, dst = ps[:, S_BANK[h % 4], q * 256:(q + 1) * 256], att[:, h % 4, q, :]
                        if x:
                            ts(dst, src, X_SCALE, None, ALU.mult)
                        else:
                            m = cst[:, K_MASK + P * (1 - q):K_MASK + P * (1 - q) + 256]
                            stt(dst, src, MLA_SCALE, m, ALU.mult, ALU.add)
                    dve.drain()
                    red(asm[:, h % 4, 0:2], att[:, h % 4], AXX, ALU.max, negate=True).then_inc(s_max.sem, 1)

                def att_out(h):
                    dve.wait_ge(*s_y(l, h + 1))
                    z = pt[:, Z + 12 + h if h < 4 else Z + 8 + h - 4, 0:SEQ]
                    tt(z, ps[:, 4 + h % 2, 0:SEQ], z, ALU.mult).then_inc(s_o.sem, 1)

                dve.wait_ge(*z_ready(l, 1))
                att_max(0)
                att_max(1)
                for h in range(8):
                    dve.wait_ge(*s_exp(l, h + 1))
                    nc.vector.reciprocal(asm[:, h % 4, 4:6], asm[:, h % 4, 2:4])
                    dve.drain()
                    tt(att[:, h % 4], att[:, h % 4], over(asm[:, h % 4, 4:6], 256), ALU.mult).then_inc(s_p.sem, 1)
                    if h < 6:
                        att_max(h + 2)
                    if h:
                        att_out(h - 1)
                att_out(7)
                s8 = lambda i, n=P: pre[0:n, i, :].rearrange("p (h b) -> p h b", h=4)
                ts(s8(0), qn[:, :, SEQ:T], col(C_KNN), None, ALU.mult)
                tt(s8(1), qn[:, :, SEQ:T], kn[:, :, SEQ:T], ALU.mult)
                tt(s8(2, ROPE), QR[:, 0:4, SEQ:T], over(QR[:, HEADS, SEQ:T], 4, 1), ALU.mult).then_inc(pre_in.sem, 1)
                for half in range(2):
                    copy(qrs[ROPE * half:ROPE * (half + 1), :, 4 * half:4 * half + 4].rearrange("p b h -> p h b"),
                         QR[:, 0:4, SEQ:T])
                dve.wait_ge(*pre_mm(l, 1))
                copy(qabs[:, :, :, :].rearrange("p b c h -> p (c h) b"), ps[:, 6, 0:64].rearrange("p (n b) -> p n b", b=NB))
                copy(scur[:, :, :].rearrange("p b h -> p h b"), ps[:, 6, 64:96].rearrange("p (h b) -> p h b", h=4)
                     ).then_inc(pre_out.sem, 1)
                dve.drain()
                query(l, 0, 0)
                query(l, 1, 1)
                dve.wait_ge(*pre_mm(l, 2))
                copy(rows[0:NB, ROW_X:ROW_X + 512], ps[0:NB, 7, :]).then_inc(pre_row.sem, 1)
                dve.wait_ge(*xc_ready(l, 1))
                tt(dtx[:, :, :], dtx[:, :, :], xc[:, 0:4, SEQ:T].rearrange("p q b -> p b q"), ALU.mult)
                dve.wait_ge(*kv_saved(l, 32))
                dve.wait_ge(*tok_mm(l, 4))
                copy(vtok, ps[:, 0:2, :]).then_inc(tok_dve.sem, 1)
                dve.wait_ge(*tok_mm(l, 5))
                x8 = lambda t, m: t[:, m, :].rearrange("p (h n) -> p h n", h=8)
                for m in range(2):
                    v = ps[:, 2 + m, :].rearrange("p (h n) -> p h n", h=8)
                    tt(x8(xtok, m), v, over(cols[:, m, 8:16], SSD_W), ALU.mult)
                    last = tt(x8(xw, m), v, over(cols[:, m, 16:24], SSD_W), ALU.mult)
                last.then_inc(tok_dve.sem, 1)
                dve.wait_ge(*tok_mm(l, 7))
                tt(wv[:, :, :].rearrange("p b h -> p h b"), ps[:, 7, 0:32].rearrange("p (h b) -> p h b", h=4),
                   gb[:, 1].rearrange("p b h -> p h b"), ALU.mult).then_inc(tok_dve.sem, 1)
                dve.drain()
                for m in range(2):
                    last = tt(vw[:, m, :].rearrange("p (h n) -> p h n", h=4), vtok[:, m, :].rearrange("p (h n) -> p h n", h=4),
                              over(cols[:, m, 28:32], P), ALU.mult)
                last.then_inc(weighted.sem, 1)
                dve.wait_ge(*pre_mm(l, 3))
                copy(rows[0:NB, 0:1536].rearrange("p (k n) -> p k n", k=3), ps[0:NB, 0:3, :]).then_inc(pre_row.sem, 1)

                def mask(item):
                    dve.wait_ge(*st_mm(l, item + 1))
                    tt(stm[:, item % 2, :], ps[:, 6 + item % 2, 0:384], tri, ALU.mult).then_inc(st_out.sem, 1)

                mask(0)
                seg(l, 0)
                seg(l, 1)
                for n in range(12):
                    if n + 1 in (4, 8, 9, 10, 11):
                        mask(1 if n + 1 == 4 else n - 5)
                    dve.wait_ge(*seg_exp(l, n + 1))
                    item = n // 4 if n < 8 else n - 6
                    tt(dec[:, n % 4, :], dec[:, n % 4, :], stm[:, item % 2, :], ALU.mult).then_inc(seg_w.sem, 1)
                    if n < 10:
                        seg(l, n + 2)
                    if n:
                        rec_out(l, n - 1)
                rec_out(l, 11)
                sample(l, 0, 0, None)
                with dve.Fori(0, NB // 2 - 1) as i:
                    for u in (1, 0):
                        b = 2 * i + (1 if u else 2)
                        sample(l, b, u, b - 1)
                sample(l, NB - 1, 1, NB - 2, more=False)
                softmax_max(l, NB - 1, 1)
                n0 = par[:, C_N0:C_N0 + 32].rearrange("p (h b) -> p h b", h=4)
                by = lambda ap: ap.rearrange("p b h -> p h b")
                tt(n0, n0, by(gb[:, 0]), ALU.mult)
                tt(s8(1), mlk[:, :, SEQ:T], by(gb[:, 1]), ALU.mult)
                softmax_shift(l, NB - 1, 1)
                dve.drain()
                tt(n0, n0, s8(1), ALU.add)
                dve.drain()
                tt(s8(0), n0, mlq[:, :, SEQ:T], ALU.mult).then_inc(ns_in.sem, 1)
                softmax_sum(l, NB - 1, 1)
                tt(xc[:, 0:4, SEQ:T], xc[:, 0:4, SEQ:T], over(par[:, C_D:C_D + 4], NB), ALU.mult)
                dve.drain()
                tt(xc[:, 0:4, SEQ:T], xc[:, 0:4, SEQ:T], by(ysa[:, :, :]), ALU.add)
                dve.wait_ge(*nq_mm(l, 1))
                den = ps[:, 0, 0:32].rearrange("p (h b) -> p h b", h=4)
                stt(s8(1), den, -1.0, by(gb[:, 2]), ALU.mult, ALU.max)
                dve.drain()
                tt(s8(1), den, s8(1), ALU.max)
                dve.drain()
                nc.vector.reciprocal(s8(1), s8(1))
                dve.drain()
                tt(xc[:, 8:12, SEQ:T], by(ysb[:, :, :]), s8(1), ALU.mult)
                tt(xc[:, 0:4, :], xc[:, 0:4, :], pt[:, Z:Z + 4, :], ALU.mult)
                dve.drain()
                tt(xc[:, 8:12, :], xc[:, 8:12, :], pt[:, OG:OG + 4, :], ALU.mult).then_inc(a_ready.sem, 1)
                context_out(l, NB - 1, 1)
                dve.drain()
                z = pt[:, Z + 12:Z + 16, SEQ:T]
                tt(z, by(ysd[:, :, :]), z, ALU.mult)
                nc.vector.reciprocal(dens[:, :, :], dens[:, :, :])
                t = dtmp[:, 0:64].rearrange("p (c b h) -> p c b h", c=2, b=NB)
                tt(t, pt[:, CKV:CKV + 2, SEQ:T].unsqueeze(3).broadcast_to([P, 2, NB, 4]), over(owns[:, :, :], 2, 1), ALU.mult)
                dve.drain()
                dve.wait_ge(*cr_mm(l, 1))
                tt(t, ps[:, 6, 0:64].rearrange("p (c b h) -> p c b h", c=2, b=NB), t, ALU.add)
                dve.drain()
                tt(ctxall[:, :, :, :].rearrange("p c h b -> p c b h"), t, over(dens[:, :, :], 2, 1), ALU.mult
                   ).then_inc(cr_out.sem, 1)
                dve.wait_ge(*n_rs(l, 7))
                for c in range(4):
                    last = stt(pt[:, Z + c, :], xc[:, c, :], col(C_SSD + c), nrs[:, c // 2, :], ALU.mult, ALU.mult)
                last.then_inc(n_out.sem, 1)
                dve.wait_ge(*n_rs(l, 8))
                for c in range(4):
                    stt(xc[:, 8 + c, :], xc[:, 8 + c, :], col(C_ML + c), nrs_ml[:, c, :], ALU.mult, ALU.mult)
                dve.drain()
                tt(pt[:, Z + 4:Z + 8, :], pt[:, Z + 4:Z + 8, :], xc[:, 8:12, :], ALU.mult)
                dve.wait_ge(*uv_mm(l, 1))
                z = pt[:, Z + 8:Z + 12, SEQ:T]
                tt(z, ps[:, 6, 64:96].rearrange("p (h b) -> p h b", h=4), z, ALU.mult).then_inc(mixed.sem, 1)
                dve.sem_inc(n_out.sem, 1)
                with dve.Fori(0, OUT_TILES // 2) as i:
                    for c in range(2):
                        dve.wait_ge(*o_mm(l, 2 * i + (c + 1)))
                        x = xT[:, bass.ds(2 * i + c, 1), :].rearrange("p o t -> p (o t)")
                        tt(x, ps[:, c, 0:T], x, ALU.add).then_inc(o_out.sem, 1)
                dve.drain().then_inc(layer_free.sem, 1)
            tt(u3, xT[:, :, :], xT[:, :, :], ALU.mult).then_inc(f_sq.sem, 1)
            dve.wait_ge(f_rs.sem, 1)
            for k in range(KT):
                last = stt(u3[:, k, :], xT[:, k, :], col(C_FIN + k), nrs[:, 0, :], ALU.mult, ALU.mult)
            last.then_inc(f_out.sem, 1)


INS = dict(
    cst=(P, N_CST), xT=(P, KT, T), memT=(P, KT, MEM), pages=(1, DEPTH * NB * PAGES),
    par=(DEPTH, P, N_PAR), wsm=(DEPTH, P, 3072), weights=(DEPTH * CHUNKS, P, SLOT),
    lat=(DEPTH * POOL, P, 256), krope=(DEPTH * POOL, ROPE, P),
    memk=(DEPTH * NB, P, 1024), memv=(DEPTH * NB, P, 1024),
    ssm=(DEPTH * NB, P, 512), mlC=(DEPTH * NB, P, 512))
OUTS = dict(
    o_y=(P, KT, T), o_lat=(DEPTH, P, 2, T), o_kr=(DEPTH, ROPE, T), o_mk=(DEPTH, P, 1024), o_mv=(DEPTH, P, 1024),
    o_ssm=(DEPTH, P, 512), o_conv=(DEPTH, P, CT, T - SEQ + 3), o_conv_old=(DEPTH, P, CT * 3 * NB),
    o_C=(DEPTH, P, 512), o_n=(DEPTH, 1, 512), o_m=(DEPTH, 4, T), o_ssm_s=(DEPTH * NB, P, 512),
    o_C_s=(DEPTH * NB, P, 512), o_ns=(DEPTH, P, 32))


def constants():
    c = np.zeros((P, N_CST), np.float32)
    i = np.arange(P)
    c[:, K_ID:K_ID + P] = np.eye(P)
    c[:, K_ONE:K_ONE + T] = 1.0
    c[:, K_MASK + P:K_MASK + 2 * P] = np.where(i[None] <= i[:, None], 0.0, NEG)
    c[:, K_MASK + 2 * P:K_MASK + 3 * P] = NEG
    upper = (i[None] >= i[:, None]).astype(np.float32)
    c[:, K_TRI:K_TRI + P] = upper
    c[:, K_TRI + P:K_TRI + 2 * P] = 1.0
    c[:, K_TRI + 2 * P:K_TRI + 3 * P] = upper
    half = ROPE // 2
    for k in range(half):
        c[half + k, K_ROT + k] = -1.0
        c[k, K_ROT + half + k] = 1.0
    pos = np.concatenate([np.arange(SEQ), np.full(NB, PAGES * PAGE)]).astype(np.float32)
    inv = (np.float32(10000.0) ** (-np.arange(half, dtype=np.float32) * np.float32(2.0) / np.float32(ROPE))).astype(np.float32)
    ang = (inv[:, None] * pos[None]).astype(np.float32)
    c[0:ROPE, K_COS:K_COS + T] = np.tile(np.cos(ang), (2, 1))
    c[0:ROPE, K_SIN:K_SIN + T] = np.tile(np.sin(ang), (2, 1))
    for h in range(8):
        c[h, K_SEL + h * P:K_SEL + (h + 1) * P] = 1.0
        c[h, K_EXP + h * SSD_W:K_EXP + (h + 1) * SSD_W] = 1.0
    c[:, K_EPS] = EPS
    return c


def lay_in(x):
    x = {k: np.asarray(v) for k, v in x.items()}
    L = DEPTH

    def tiles(a):
        return np.swapaxes(a.reshape(*a.shape[:-1], -1, P), -1, -2)

    def rows_(a, n=P):
        out = np.zeros((*a.shape[:-1], n, 1), np.float32)
        out[..., :a.shape[-1], 0] = a
        return out

    def cols_pad(a):
        out = np.zeros((L, P, a.shape[-1]), np.float32)
        out[:, :a.shape[1]] = a
        return out

    d = {"cst": constants()}
    tokens = np.concatenate([x["x_prompt"][0], x["x_sample"][:, 0]], 0)
    d["xT"] = tokens.T.reshape(KT, P, T).swapaxes(0, 1)
    d["memT"] = x["mem_prompt"][0].T.reshape(KT, P, MEM).swapaxes(0, 1)
    table = x["page_table"].astype(np.int32).reshape(1, -1)
    d["pages"] = np.concatenate([table + POOL * l for l in range(L)], 1).astype(np.int32)
    cw = np.concatenate([tiles(x["conv_a_w"]), tiles(x["conv_b_w"])], -1)
    st = np.concatenate([x["state_ssm_conv"], x["state_mlstm_conv"]], -1)
    st = tiles(st).transpose(0, 3, 4, 2, 1).reshape(L, P, -1)
    n0 = x["state_mlstm_n"].transpose(0, 3, 2, 1).reshape(L, P, -1)
    m0 = cols_pad(x["state_mlstm_m"].transpose(0, 2, 1))
    dsk = tiles(np.repeat(x["d_skip"], SSD_W, axis=-1))
    fin = np.broadcast_to(tiles(x["final_norm_g"])[None], (L, P, KT))
    d["par"] = np.concatenate(
        [tiles(x["norm_g"]), cw.transpose(0, 2, 1, 3).reshape(L, P, -1),
         np.concatenate([tiles(x["conv_a_b"]), tiles(x["conv_b_b"])], -1), tiles(x["ssd_norm_g"]), tiles(x["ml_norm_g"]),
         tiles(x["q_norm_g"]), tiles(x["kv_norm_g"]), rows_(x["qn_nope_g"]), rows_(x["qn_rope_g"]), rows_(x["kn_nope_g"]),
         rows_(x["kn_rope_g"]), tiles(x["mem_norm_g"]), rows_(x["xk_norm_g"]), rows_(x["xq_norm_g"]), dsk, fin,
         rows_(x["dt_bias"]), rows_(x["a_log"]), rows_(x["b_i"]), rows_(x["b_f"]), m0, n0, st], -1)
    uk = x["w_uk"].reshape(L, 2, P, 512).transpose(0, 2, 1, 3).reshape(L, P, 1024)
    uv = x["w_uv"].reshape(L, 2, P, 512).transpose(0, 2, 1, 3).reshape(L, P, 1024)
    ukT = x["w_uk"].transpose(0, 3, 2, 1).reshape(L, P, 1024)
    d["wsm"] = np.concatenate([uk, uv, ukT], -1)
    w = x["w_in"]
    z, xbc, dt, xm, ig, fg, og, cq, ckv, krp, xq = np.split(
        w, np.cumsum([2048, 1024, 8, 512, 4, 4, 512, 384, 256, 64]).tolist(), axis=-1)
    gate = np.zeros((L, D_MODEL, P), np.float32)
    gate[..., 0:8], gate[..., 32:36], gate[..., 64:68] = dt, ig, fg
    krp = np.concatenate([krp, np.zeros((L, D_MODEL, P - ROPE), np.float32)], -1)
    w = np.concatenate([xbc, xm, gate, krp, cq, ckv, xq, og, z], -1)
    w = np.concatenate([w, np.zeros((L, D_MODEL, P), np.float32)], -1)
    w_in = w.reshape(L, KT, P, IN_CHUNKS, 2, P).transpose(0, 3, 2, 4, 1, 5)
    mk = x["w_mem_k"].reshape(L, KT, P, 2, 2, P).transpose(0, 3, 2, 4, 1, 5)
    mv = x["w_mem_v"].reshape(L, 2, 4, P, 512).transpose(0, 1, 3, 2, 4)
    uq = x["w_uq"].reshape(L, 3, P, 2, 2, 192).transpose(0, 3, 2, 4, 1, 5)
    ml = np.stack([x["w_mq"], x["w_mk"], x["w_mv"], np.zeros_like(x["w_mv"])], 1)
    ml = ml.reshape(L, 2, 2, 4, P, P).transpose(0, 1, 4, 2, 3, 5)
    out = x["w_out"].reshape(L, MIX_TILES, P, OUT_TILES, P).transpose(0, 3, 2, 1, 4)
    weights = np.zeros((L, CHUNKS, P, SLOT), np.float32)
    first = 0
    for part, chunks in ((w_in, IN_CHUNKS), (mk, 2), (mv, 2), (uq, 2), (ml, 2), (out, OUT_TILES)):
        part = part.reshape(L, chunks, P, -1)
        weights[:, first:first + chunks, :, :part.shape[-1]] = part
        first += chunks
    d["weights"] = weights.reshape(L * CHUNKS, P, SLOT)
    d["lat"] = x["cache_mla_latent"].reshape(-1, P, 256)
    d["krope"] = x["cache_mla_krope"].reshape(-1, P, ROPE).swapaxes(1, 2)
    d["memk"] = x["cache_mem_k"].reshape(-1, P, 1024)
    d["memv"] = x["cache_mem_v"].reshape(-1, P, 1024)
    d["ssm"] = x["state_ssm"].reshape(L * NB, 4, P, P).swapaxes(1, 2).reshape(-1, P, 512)
    d["mlC"] = x["state_mlstm_C"].reshape(L * NB, 4, P, P).swapaxes(1, 2).reshape(-1, P, 512)
    return {k: np.ascontiguousarray(v) for k, v in d.items()}


def lay_out(r):
    L = DEPTH
    y = r["o_y"].transpose(2, 1, 0).reshape(T, D_MODEL)
    lat = r["o_lat"].transpose(0, 3, 2, 1).reshape(L, T, 256)
    krp = r["o_kr"].transpose(0, 2, 1)
    mk = r["o_mk"].reshape(L, P, 4, MEM).transpose(0, 3, 2, 1)[:, None]
    mv = r["o_mv"].reshape(L, P, 2, 4, P).transpose(0, 2, 1, 3, 4).reshape(L, 1, MEM, 4, P)
    conv = r["o_conv"].transpose(0, 3, 2, 1).reshape(L, 3 + NB, CT * P)
    old = r["o_conv_old"].reshape(L, P, CT, 3, NB).transpose(0, 4, 3, 2, 1).reshape(L, NB, 3, CT * P)
    conv_s = np.concatenate([old[:, :, 1:], conv[:, 3:, None]], 2)
    by_head = lambda a, n: a.reshape(-1, P, 4, P).swapaxes(1, 2).reshape(L, n, 4, P, P)
    m = r["o_m"]
    ssd = SSD_W
    out = (
        y[None, :SEQ], y[SEQ:, None], lat[:, None, :SEQ], krp[:, None, :SEQ], mk, mv,
        by_head(r["o_ssm"], 1).reshape(L, 1, SSD_HEADS, ssd, P), conv[:, None, :3, :1024],
        by_head(r["o_C"], 1), r["o_n"].reshape(L, 1, 4, P), m[:, :, SEQ - 1][:, None], conv[:, None, :3, 1024:],
        lat[:, SEQ:, None], krp[:, SEQ:, None],
        by_head(r["o_ssm_s"], NB).reshape(L, NB, SSD_HEADS, ssd, P), conv_s[..., :1024],
        by_head(r["o_C_s"], NB), r["o_ns"].reshape(L, P, 4, NB).transpose(0, 3, 2, 1),
        m[:, :, SEQ:].swapaxes(1, 2), conv_s[..., 1024:])
    return tuple(np.ascontiguousarray(a) for a in out)


def program(nc):
    d = {}
    for name, shape in INS.items():
        dt = mybir.dt.int32 if name == "pages" else F32
        d[name] = nc.dram_tensor("in_" + name, shape, dt, kind="ExternalInput").ap()
    for name, shape in OUTS.items():
        d[name] = nc.dram_tensor(name, shape, F32, kind="ExternalOutput").ap()
    d["rowscr"] = nc.dram_tensor("rowscr", (NB, ROWS), F32, kind="Internal").ap()
    build(nc, d)


def kernel(**inputs):
    import concourse.bacc as bacc
    from concourse.bass_utils import run_bass_kernel_spmd

    nc = bacc.Bacc("TRN2", target_bir_lowering=False, num_devices=1)
    program(nc)
    r = run_bass_kernel_spmd(nc, [{"in_" + k: v for k, v in lay_in(inputs).items()}], core_ids=[0])
    return lay_out(r.results[0])
```

```python
import math
from contextlib import ExitStack

import numpy as np

import concourse.bass as bass
from concourse import mybir
from concourse.alu_op_type import AluOpType as ALU

F32 = mybir.dt.float32
ACT = mybir.ActivationFunctionType
LN_EXP = "natural_log_exp_and_others"
AXX = mybir.AxisListType.X

P = 128
DEPTH, D_MODEL, SEQ, NB = 2, 1024, 256, 8
T = SEQ + NB
KT = D_MODEL // P
HEADS = 4
SSD_HEADS, SSD_W = 8, 64
ROPE = 64
Q_TILES, KV_TILES = 3, 2
PAGES, PAGE, POOL = 16, 128, 160
MEM = 256
EPS = 1e-6
NEG = -1.0e30
MLA_SCALE = (P + ROPE) ** -0.5
X_SCALE = P ** -0.5
K_SCALE = P ** -0.5

CONV, GATE, KR, CQ, CKV, XQ, OG, Z = 0, 12, 13, 14, 17, 19, 23, 27
IN_TILES = 43
CT = 12
OUT_TILES, MIX_TILES = 8, 16
NORMS = 11
IN_CHUNKS = (IN_TILES + 1) // 2
FILL = IN_TILES // 4

C_NORM, C_CW, C_CB, C_SSD, C_ML, C_Q, C_KV = 0, 8, 56, 68, 72, 76, 79
C_QNN, C_QNR, C_KNN, C_KNR, C_MEM, C_XK, C_XQ, C_D = 81, 82, 83, 84, 85, 93, 94, 95
C_FIN, C_DTB, C_ALOG, C_BI, C_BF, C_M0, C_N0, C_ST = 99, 107, 108, 109, 110, 111, 119, 151
N_PAR = C_ST + CT * 3 * NB

K_ID, K_ONE, K_EPS, K_MASK, K_TRI, K_ROT, K_COS, K_SIN, K_SEL, K_EXP = (
    0, 128, 392, 393, 777, 1161, 1225, 1489, 1753, 2777)
N_CST = 3289

SLOT = 2048
CHUNKS = 38
R_MK, R_MV, R_UQ, R_MLQK, R_MLV, R_OUT = 22, 24, 26, 28, 29, 30
ROWS = 2048
ROW_B, ROW_C, ROW_K, ROW_Q, ROW_X = 0, 256, 512, 1024, 1536


MASKED_AFTER = {3: 2, 6: 3, 7: 4, 8: 5}
MASK_AFTER = {3: 2, 7: 3, 8: 4, 9: 5}
MIX_ORDER = (*range(8), *range(12, 16), *range(8, 12))
N_WIDTH = {3: 128, 4: 128, 5: 64, 6: 64, 7: 128, 8: 128}
N_PRODUCT = {3: 4, 4: 0, 5: 6, 6: 2, 7: 4, 8: 0}
N_SUMS = {3: 6, 4: 2, 5: 4, 6: 0, 7: 6, 8: 2}
S_BANK = (7, 6, 0, 1)


def spread_bank(n):
    return (0, 1, 4, 5)[n % 4] if n < 8 else n % 2


class Signal:

    def __init__(self, sem, per_layer, before=0):
        self.sem, self.per_layer, self.before = sem, per_layer, before

    def __call__(self, l, n):
        return self.sem, l * self.per_layer + (n + self.before)


def build(nc, d):
    ctx = ExitStack()
    with ctx:
        def sb(name, shape, dt=F32):
            return ctx.enter_context(nc.sbuf_tensor(name, shape, dt))

        def sig(name, per_layer=1, before=0):
            return Signal(ctx.enter_context(nc.semaphore(name)), per_layer, before)

        cst = sb("cst", [P, N_CST])
        xT = sb("xT", [P, KT, T])
        uT = sb("uT", [P, KT * T])
        pt = sb("pt", [P, IN_TILES, T])
        xc = sb("xc", [P, CT, T])
        ring = sb("ring", [P, 2, SLOT])
        lat0 = sb("lat0", [P, PAGES, 256])
        lat1 = sb("lat1", [P, PAGES, 256])
        kr = sb("kr", [P, 2, PAGES // 2, PAGE])
        states = sb("states", [P, 2, 2, 512])
        rows = sb("rows", [P, ROWS])
        scr = sb("scr", [P, 2112])
        wsm = sb("wsm", [P, 2, 1024])
        wk = sb("wk", [P, 4, 260])
        par = sb("par", [P, N_PAR])
        gates = sb("gates", [SSD_HEADS, 9, T])
        softp = sb("softp", [SSD_HEADS, 2, T])
        QR = sb("QR", [ROPE, HEADS + 1, T])
        btok = sb("btok", [P, 2, 256])
        dtmp = sb("dtmp", [P, 512])
        rsm = sb("rsm", [P, MEM])
        gsmall = sb("gsmall", [SSD_HEADS, 40])
        cols = sb("cols", [P, 2, 32])
        da = sb("da", [P, NB, 4])
        dtx = sb("dtx", [P, NB, 4])
        gb = sb("gb", [P, 3, NB, 4])
        wv = sb("wv", [P, NB, 4])
        qabs = sb("qabs", [P, NB, 2, 4])
        qrs = sb("qrs", [P, NB, 8])
        scur = sb("scur", [P, NB, 4])
        ctxall = sb("ctxall", [P, 2, 4, NB])
        ysa = sb("ysa", [P, NB, 4])
        ysb = sb("ysb", [P, NB, 4])
        ysd = sb("ysd", [P, NB, 4])
        pre = sb("pre", [P, 3, 32])
        ssq = sb("ssq", [P, 2, PAGES, 4])
        raws = sb("raws", [P, 2, PAGES, 4])
        owns = sb("owns", [P, NB, 4])
        dens = sb("dens", [P, NB, 4])
        sx = sb("sx", [P, 2, 2, 4])
        prob = sb("prob", [P, 2, PAGES, 4])
        probx = sb("probx", [P, 2, 2, 4])
        sm = sb("sm", [P, 2, 64])
        pages = sb("pages", [1, NB * PAGES * DEPTH], mybir.dt.int32)
        ps = ctx.enter_context(nc.psum_tensor("ps", [P, 8, 512], F32))

        ident = cst[:, K_ID:K_ID + P]
        ones = cst[:, K_ONE:K_ONE + P]
        tri = cst[:, K_TRI:K_TRI + 384]
        eps = cst[:, K_EPS:K_EPS + 1]
        latb = [lat0, lat1]
        u3 = uT[:, :].rearrange("p (k t) -> p k t", k=KT)
        memk = uT[:, 0:1024]
        memv = uT[:, 1024:2048].rearrange("p (m n) -> p m n", m=2)
        A1 = lat1[:, :, :].rearrange("p a b -> p (a b)")
        mkT = A1[:, 0:1024].rearrange("p (h m) -> p h m", h=4)
        memV = A1[:, 1024:2048].rearrange("p (m n) -> p m n", m=2)
        memn = A1[:, 2048:4096].rearrange("p (k t) -> p k t", k=KT)
        mlaV = A1[:, 2048:3072].rearrange("p (m n) -> p m n", m=2)
        ktok = A1[:, 0:1024].rearrange("p (m n) -> p m n", m=2)
        vtok = A1[:, 1024:2048].rearrange("p (m n) -> p m n", m=2)
        vw = A1[:, 2048:3072].rearrange("p (m n) -> p m n", m=2)
        xw = A1[:, 3072:4096].rearrange("p (m n) -> p m n", m=2)
        xtok = pt[:, XQ:XQ + 4, :].rearrange("p a b -> p (a b)")[:, 0:1024].rearrange("p (m n) -> p m n", m=2)
        qn, kn = pt[:, 0:4, :], pt[:, 4:8, :]
        mlq, mlk = pt[:, 0:4, :], pt[:, 4:8, :]
        A0 = lat0[:, :, :].rearrange("p a b -> p (a b)")
        nsq = [t[:, 0:4 * T].rearrange("p (h t) -> p h t", h=4) for t in (scr, rows)]
        nsq_ssd = A0[:, 4 * T:8 * T].rearrange("p (h t) -> p h t", h=4)
        nrs_ml = A0[:, 0:4 * T].rearrange("p (h t) -> p h t", h=4)
        nrs = scr[:, 4 * T:8 * T].rearrange("p (h t) -> p h t", h=4)
        att = rows[:, :].rearrange("p (u q k) -> p u q k", u=4, q=2)
        attT = scr[:, 1024:2048].rearrange("p (u k q) -> p u k q", u=2, k=2)
        dec = uT[:, 0:1536].rearrange("p (u i) -> p u i", u=4)
        stm = scr[:, 768:1536].rearrange("p (u i) -> p u i", u=2)
        emm = pt[:, 8:12, 0:SEQ]
        latT = scr[:, 0:1024].rearrange("p (u g c k) -> p u g c k", u=2, g=2, c=2)
        sqd = scr[:, 1024:2048].rearrange("p (u n) -> p u n", u=2)
        asm = sm[:, 0, 0:32].rearrange("p (u i) -> p u i", u=4)
        ctxr = gates[0:4].rearrange("p a t -> p (a t)")[:, 0:NB * 256].rearrange("p (b n) -> p b n", b=NB)
        gdt, acum, wend, la, li, lf, gi, nmx, mT = (gates[:, i, :] for i in range(9))


        first, second, x_in = sig("first_loads"), sig("second_loads"), sig("x_in")
        layer_free = sig("layer_free", 4, 4)
        par_in, wsm_in, mem_in = sig("par_in", 16), sig("wsm_in", 32), sig("mem_in", 16)
        slot_in = [sig("slot0_in", 16 * CHUNKS // 2), sig("slot1_in", 16 * CHUNKS // 2)]
        slot_free = sig("slot_free", 8)
        x_sq, x_ss, x_rs, u_ready = sig("x_squares", KT, KT), sig("x_sums", 1, 1), sig("x_rstd"), sig("u_ready", 2)
        pj_mm, pj_act, pj_dve = sig("proj_mm", IN_TILES), sig("proj_act", 22, 2), sig("proj_dve", 21, 2)
        conv_a, conv_d, xc_ready, z_ready = sig("conv_tap3"), sig("conv_done"), sig("xc_ready"), sig("z_ready")
        g_raw, g_neg, g_log, g_scan, g_exp, g_wend, g_pe, g_out = (
            sig(f"gates_{x}") for x in ("raw", "neg", "log", "scan", "exp", "wend", "mm", "out"))
        conv_saved = sig("conv_saved", 16)
        m_sq, m_ss, m_rs = sig("mem_squares"), sig("mem_sums"), sig("mem_rstd")
        mem_ready = sig("mem_ready")
        n_in = sig("norm_in", 7)
        n_sq, n_ss, n_rs, n_out = (sig(f"norm_{x}", NORMS) for x in ("squares", "sums", "rstd", "out"))
        mv_mm, mv_out, lv_mm, lv_out = sig("memv_mm"), sig("memv_out"), sig("latv_mm"), sig("latv_out")
        r_mm, r_out = sig("rot_mm"), sig("rot_out")
        s_mm, s_max, s_exp, s_p, s_t, s_pt, s_y, s_o = (
            sig(f"att_{x}", 8) for x in ("scores", "max", "exp", "prob", "probT", "probT_sb", "y", "out"))
        pre_in, pre_mm, pre_out, pre_row = sig("pre_in"), sig("pre_mm", 3), sig("pre_out"), sig("pre_rows", 2)
        tok_mm, tok_act, tok_dve = sig("tok_mm", 7), sig("tok_act", 4), sig("tok_dve", 3)
        weighted = sig("weighted")
        st_mm, st_out = sig("masked_mm", 6), sig("masked_out", 6)
        bc_mm, seg_out, seg_exp, seg_w, ry_mm = (
            sig(f"rec_{x}", 12) for x in ("bc", "seg", "exp", "weights", "y"))
        ry_out, em_out = sig("rec_out", 8), sig("rec_emm", 4)
        fin_mm, fin_out, fin_saved = sig("fin_mm"), sig("fin_out"), sig("fin_saved", 48)
        rows_saved = sig("rows_saved", 16)
        lat_in = [sig("lat0_in", 16 * 32 * 4), sig("lat1_in", 16 * 32 * 4)]
        mk_in, mv_in, rows_in = sig("memk_in", 16 * NB), sig("memv_in", 16 * NB), sig("rows_in", 16 * NB)
        st_in = [sig("state0_in", 32 * 4), sig("state1_in", 32 * 4)]
        st_saved = [sig("state0_saved", 32 * 4, 32), sig("state1_saved", 32 * 4, 32)]
        q_in, cr_mm, cr_out = sig("query_in", NB), sig("context_by_feature"), sig("context_ready")
        t_mm, t_sb, pair_mm = sig("latT", 8 * NB), sig("latT_sb", 8 * NB, 1), sig("pair_mm", 8 * NB, 2)
        k_mm, k_sq, k_red = sig("key_mm", PAGES * NB), sig("key_squares", PAGES * NB, 2), sig("key_sums", PAGES * NB, 2)
        k_rs, mx_in, mx_all, s_sub = sig("key_rstd", NB), sig("max_in", NB, 2), sig("max_all", NB), sig("shifted", NB)
        p_exp, p_sum, cx_mm, cx_out = sig("probs", NB), sig("prob_sums", NB), sig("context", NB, 2), sig("context_out", NB, 2)
        rows_used, memk_used, decayed, st_new = (
            sig("rows_used", NB), sig("memk_used", NB), sig("decayed", NB), sig("state_new", NB))
        ns_in, nq_mm, uv_mm, a_ready = sig("nstate_in"), sig("nstate_q"), sig("uv_mm"), sig("sample_out")
        mixed = sig("mixed", 2)
        o_mm, o_out = sig("out_mm", OUT_TILES, 2), sig("out_add", OUT_TILES, 2)
        saved, kv_saved = sig("saved", 16 * 5), sig("memory_saved", 32)
        f_rs, f_out, y_saved = sig("fin_rs"), sig("fin_norm"), sig("y_saved")

        block = ctx.enter_context(nc.Block())

        @block.sync
        def _(sp):
            sp.dma_start(memn, d["memT"]).then_inc(first.sem, 16)
            sp.dma_start(cst[:, 0:K_MASK], d["cst"][:, 0:K_MASK]).then_inc(first.sem, 16)
            sp.dma_start(xT[:, :, :], d["xT"]).then_inc(x_in.sem, 16)
            sp.dma_start(cst[:, K_MASK:], d["cst"][:, K_MASK:]).then_inc(second.sem, 16)
            sp.dma_start(pages[:, :], d["pages"]).then_inc(second.sem, 16)
            def one(name, i):
                return d[name][bass.ds(i, 1)].rearrange("o p n -> p (o n)")

            def places_of(l, b):
                return [sp.value_load(pages[0:1, bass.ds(l * (NB * PAGES) + (b * PAGES + j), 1)],
                                      min_val=0, max_val=DEPTH * POOL - 1) for j in range(PAGES)]

            def load_rotary(u, places):
                for j, page in enumerate(places):
                    half = ROPE * (j // 8)
                    sp.dma_start(kr[half:half + ROPE, u, j % 8, :], one("krope", page)).then_inc(lat_in[u].sem, 16)

            def load_latents(u, places):
                for j, page in enumerate(places):
                    sp.dma_start(latb[u][:, j, :], one("lat", page)).then_inc(lat_in[u].sem, 16)

            def load_values(l, b):
                sp.dma_start(uT[:, 1024:2048], one("memv", l * NB + b)).then_inc(mv_in.sem, 16)

            def load_states(l, b, u, k):
                sp.wait_ge(*st_saved[u](l, 32 * k))
                sp.dma_start(states[:, u, 0, :], one("ssm", l * NB + b)).then_inc(st_in[u].sem, 16)
                sp.dma_start(states[:, u, 1, :], one("mlC", l * NB + b)).then_inc(st_in[u].sem, 16)

            def load_rows(l, b):
                if type(b) is not int or b:
                    sp.wait_ge(*memk_used(l, b))
                sp.dma_start(memk, one("memk", l * NB + b)).then_inc(mk_in.sem, 16)
                if type(b) is not int or b:
                    sp.wait_ge(*rows_used(l, b))
                sp.dma_start(rows[:, :], d["rowscr"][bass.ds(b, 1), :].rearrange("o n -> (o n)")
                             .partition_broadcast(P)).then_inc(rows_in.sem, 16)

            with sp.Fori(0, DEPTH) as l:
                sp.wait_ge(*layer_free(l, 0))
                sp.dma_start(par[:, :], one("par", l)).then_inc(par_in.sem, 16)
                sp.wait_ge(m_sq.sem, 1)
                sp.dma_start(memn, d["memT"]).then_inc(mem_in.sem, 16)
                sp.wait_ge(second.sem, 32)
                small = one("wsm", l)
                sp.dma_start(wsm[:, :, :].rearrange("p a n -> p (a n)"), small[:, 1024:3072]).then_inc(wsm_in.sem, 16)
                sp.dma_start(wk[:, :, 2:258], small[:, 0:1024].rearrange("p (a n) -> p a n", a=4)).then_inc(wsm_in.sem, 16)
                places = places_of(l, 0)
                load_rotary(0, places)
                load_latents(0, places)
                load_states(l, 0, 0, 0)
                sp.wait_ge(*par_in(l, 16))
                sp.dma_start(one("o_conv_old", l), par[:, C_ST:]).then_inc(saved.sem, 16)
                sp.wait_ge(*pj_act(l, 22))
                sp.wait_ge(*pj_dve(l, 21))
                sp.dma_start(d["o_conv"][bass.ds(l, 1)].rearrange("o p c t -> p (o c) t"),
                             pt[:, 0:CT, SEQ - 3:T]).then_inc(conv_saved.sem, 16)
                sp.wait_ge(*n_out(l, 2))
                sp.dma_start(one("o_mk", l), A1[:, 0:1024]).then_inc(kv_saved.sem, 16)
                sp.wait_ge(*mv_out(l, 1))
                sp.dma_start(one("o_mv", l), A1[:, 1024:2048]).then_inc(kv_saved.sem, 16)
                sp.wait_ge(*n_out(l, 1))
                sp.dma_start(d["o_lat"][bass.ds(l, 1)].rearrange("o p c t -> p (o c) t"),
                             pt[:, CKV:CKV + 2, :]).then_inc(saved.sem, 16)
                sp.wait_ge(*r_out(l, 1))
                sp.dma_start(one("o_kr", l), QR[:, HEADS, :]).then_inc(saved.sem, 16)
                sp.wait_ge(*g_scan(l, 1))
                sp.dma_start(one("o_m", l), mT[0:4, :]).then_inc(saved.sem, 16)
                sp.wait_ge(*pre_row(l, 2))
                sp.dma_start(d["rowscr"], rows[0:NB, :]).then_inc(rows_saved.sem, 16)
                places = places_of(l, 1)
                load_rotary(1, places)
                sp.wait_ge(*fin_out(l, 1))
                sp.dma_start(one("o_ssm", l), A1[:, 0:512]).then_inc(fin_saved.sem, 16)
                sp.dma_start(one("o_C", l), A1[:, 512:1024]).then_inc(fin_saved.sem, 16)
                sp.dma_start(one("o_n", l), A1[0:1, 1024:1536]).then_inc(fin_saved.sem, 16)
                sp.wait_ge(*fin_saved(l, 48))
                load_values(l, 0)
                load_latents(1, places)
                sp.wait_ge(*rows_saved(l, 16))
                load_rows(l, 0)
                load_states(l, 1, 1, 0)
                load_rows(l, 1)
                with sp.Fori(0, NB // 2 - 1) as i:
                    for u in range(2):
                        b = 2 * i + (2 + u)
                        places = places_of(l, b)
                        sp.wait_ge(*pair_mm(l, 8 * (b - 1)))
                        load_rotary(u, places)
                        sp.wait_ge(*cx_mm(l, b - 1))
                        load_values(l, b - 1)
                        load_latents(u, places)
                        load_states(l, 2 * i + (2 + u), u, i + 1)
                        load_rows(l, 2 * i + (2 + u))
                sp.wait_ge(*cx_mm(l, NB - 1))
                load_values(l, NB - 1)
                sp.wait_ge(*ns_in(l, 1))
                sp.dma_start(one("o_ns", l), par[:, C_N0:C_N0 + 32]).then_inc(saved.sem, 16)
                sp.wait_ge(*saved(l, 80))
                sp.wait_ge(*conv_saved(l, 16))
                sp.sem_inc(layer_free.sem, 1)
            sp.wait_ge(f_out.sem, 1)
            sp.dma_start(d["o_y"], u3).then_inc(y_saved.sem, 16)
            sp.wait_ge(y_saved.sem, 16)

        @block.gpsimd
        def _(pool):
            def chunk(l, n, u, free, wide=2048):
                pool.wait_ge(*free)
                weights = d["weights"][bass.ds(pool.snap(CHUNKS * l + n), 1)].rearrange("o p n -> p (o n)")
                pool.dma_start(ring[:, u, 0:wide], weights[:, 0:wide]).then_inc(slot_in[u].sem, 16)

            with pool.Fori(0, DEPTH) as l:
                for u in range(2):
                    chunk(l, u, u, o_mm(l, u - 1))
                with pool.Fori(1, R_MK // 2) as i:
                    for u in range(2):
                        chunk(l, 2 * i + u, u, pj_mm(l, 4 * i + (2 * u - 2)))
                for u in range(2):
                    chunk(l, R_MK + u, u, pj_mm(l, IN_TILES - 1 + u))
                for u in range(2):
                    chunk(l, R_MV + u, u, slot_free(l, 1 + u))
                for u in range(2):
                    chunk(l, R_UQ + u, u, slot_free(l, 3 + u), 1152)
                for u in range(2):
                    chunk(l, R_MLQK + u, u, slot_free(l, 5 + u), 1024)
                for u in range(2):
                    chunk(l, R_OUT + u, u, slot_free(l, 7 + u))
                with pool.Fori(0, NB // 2) as i:
                    for u in range(2):
                        b = 2 * i + u
                        pool.wait_ge(*st_in[u](l, 32 * i + 32))
                        pool.wait_ge(*g_out(l, 1))
                        for s, factor in ((0, da[:, :, :]), (1, gb[:, 0])):
                            st = states[:, u, s, :].rearrange("p (h n) -> p h n", h=4)
                            f = factor[:, bass.ds(b, 1), :].rearrange("p o h -> p (o h)").unsqueeze(2).broadcast_to([P, 4, P])
                            ins = nc.gpsimd.tensor_tensor(st, st, f, ALU.mult)
                        ins.then_inc(decayed.sem, 1)
                        pool.wait_ge(*mx_in(l, b + 1))
                        nc.gpsimd.tensor_tensor(sm[:, u, 56:64], sm[:, u, 0:8], ones[:, 0:8], ALU.mult)
                        pool.drain()
                        nc.gpsimd.partition_all_reduce(sm[:, u, 8:16], sm[:, u, 56:64], P, bass.bass_isa.ReduceOp.max
                                                       ).then_inc(mx_all.sem, 1)
                with pool.Fori(1, OUT_TILES // 2) as i:
                    for c in range(2):
                        chunk(l, 2 * i + (R_OUT + c), c, o_mm(l, 2 * i + (c - 1)))
        @block.tensor
        def _(pe):
            mm = nc.tensor.matmul

            def slot(l, n):
                pe.wait_ge(*slot_in[n % 2](l, 16 * (n // 2 + 1)))
                return ring[:, n % 2, :]

            def tile_mm(l, m, u, a, bank):
                w = ring[:, u, a * 1024:(a + 1) * 1024].rearrange("p (k m) -> p k m", k=KT)
                for k in range(KT):
                    if k == KT // 2:
                        pe.wait_ge(*u_ready(l, 2))
                    last = mm(ps[:, bank, 0:T], w[:, k, :], u3[:, k, :], start=k == 0, stop=k == KT - 1)
                last.then_inc(pj_mm.sem, 1)
                return last

            def sums(l, k, bank, groups, width=T):
                pe.wait_ge(*n_sq(l, k + 1))
                for i, group in enumerate(groups):
                    for j, (n, t) in enumerate(group):
                        last = mm(ps[:, bank + i, 0:width], ones[0:n, :], t, start=j == 0, stop=j == len(group) - 1)
                last.then_inc(n_ss.sem, 1)

            def heads(k, n=P):
                return [[(n, nsq[k % 2][0:n, h, :])] for h in range(4)]

            def scores(l, h):
                x = h < 4
                if h >= 4:
                    pe.wait_ge(*s_max(l, h - 3))
                for q in range(2):
                    out = ps[:, S_BANK[h % 4], q * 256:(q + 1) * 256]
                    tokens = slice(q * P, (q + 1) * P)
                    if x:
                        last = mm(out, pt[:, XQ + h, tokens], mkT[:, h, :], start=True, stop=True)
                    else:
                        mm(out, qn[:, h - 4, tokens], kn[:, h - 4, 0:SEQ], start=True, stop=False)
                        last = mm(out, QR[:, h - 4, tokens], QR[:, HEADS, 0:SEQ], start=False, stop=True)
                last.then_inc(s_mm.sem, 1)

            def masked(l, item):
                if item >= 2:
                    pe.wait_ge(*st_out(l, item - 1))
                k, q = (xc[:, 4 + item], xc[:, 6 + item]) if item < 2 else (mlk[:, item - 2], mlq[:, item - 2])
                mm(ps[:, 6 + item % 2, 0:256], k[:, 0:P], q[:, 0:256], start=True, stop=True)
                mm(ps[:, 6 + item % 2, 256:384], k[:, P:256], q[:, P:256], start=True, stop=True
                   ).then_inc(st_mm.sem, 1)

            def spread(l, n):
                if n >= 4:
                    pe.wait_ge(*seg_out(l, n - 3 if n < 8 else n - 1))
                if n >= 10:
                    pe.wait_ge(*em_out(l, n - 9))
                h, row = (n, acum[:, 0:SEQ]) if n < 8 else (n - 8, nmx[0:4, 0:SEQ])
                k = 8 if n < 8 else 4
                sel = cst[0:k, K_SEL + h * P:K_SEL + (h + 1) * P]
                last = mm(ps[:, spread_bank(n), 0:256], sel, row, start=True, stop=True)
                if n >= 8:
                    last = mm(ps[:, n % 2, 256:512], sel, mT[0:4, 0:SEQ], start=True, stop=True)
                last.then_inc(bc_mm.sem, 1)

            def recur(l, n):
                pe.wait_ge(*seg_w(l, n + 1))
                s = n // 2 if n < 8 else n - 4
                if s >= 2 and not (n < 8 and n % 2):
                    pe.wait_ge(*ry_out(l, s - 1))
                if n < 8:
                    out = ps[SSD_W * (n % 2):SSD_W * (n % 2 + 1), 2 + s % 2, 0:SEQ]
                    v = [xtok[:, m, n * SSD_W:(n + 1) * SSD_W] for m in range(2)]
                    sets = [(out, v)]
                else:
                    v = [vtok[:, m, (n - 8) * P:(n - 7) * P] for m in range(2)]
                    sets = [(ps[:, 2 + s % 2, 0:SEQ], v), (ps[:, 4 + s % 2, 0:SEQ], [ones, ones])]
                for out, v in sets:
                    mm(out, v[0], dec[:, n % 4, 0:256], start=True, stop=False)
                    last = mm(out[:, P:256], v[1], dec[:, n % 4, 256:384], start=False, stop=True)
                last.then_inc(ry_mm.sem, 1)

            def turn(l, b, u, g):
                pe.wait_ge(*t_sb(l, 8 * b + g))
                for q in range(2):
                    for c in range(2):
                        last = nc.tensor.transpose(ps[:, 0, (2 * q + c) * P:(2 * q + c + 1) * P],
                                                   latb[u][:, 2 * g + q, c * P:(c + 1) * P], ident)
                last.then_inc(t_mm.sem, 1)

            def keys(l, b, u, g):
                pe.wait_ge(*t_sb(l, 8 * b + (g + 1)))
                for q in range(2):
                    j = 2 * g + q
                    pe.wait_ge(*k_sq(l, PAGES * b + (j - 1)))
                    at = 2 * u
                    for half in range(2):
                        for c in range(2):
                            last = mm(ps[:, 1 + 2 * (j % 2) + half, 0:258], latT[:, g % 2, q, c, :],
                                      wk[:, 2 * c + half, at:at + 258], start=c == 0, stop=c == 1)
                    last.then_inc(k_mm.sem, 1)
                mm(ps[:, 5 + u, 8 * g:8 * g + 8], kr[:, u, g, :],
                   qrs[:, bass.ds(b, 1), :].rearrange("p o h -> p (o h)"), start=True, stop=True).then_inc(pair_mm.sem, 1)

            def context(l, b, u):
                pe.wait_ge(*p_sum(l, b + 1))
                pe.wait_ge(*cx_out(l, b - 1))
                pe.wait_ge(*mv_in(l, 16 * b + 16))
                at = 32 * u
                mm(ps[:, 7, at:at + 8], ones, sm[:, u, 16:24], start=True, stop=True)
                for j in range(PAGES):
                    mm(ps[0:4, 7, 128:384], prob[:, u, j, :], latb[u][:, j, :], start=j == 0, stop=j == PAGES - 1)
                for h in range(HEADS):
                    for m in range(2):
                        last = mm(ps[:, 7, at + 16 + h:at + 17 + h], memv[:, m, h * P:(h + 1) * P],
                                  probx[:, u, m, h:h + 1], start=m == 0, stop=m == 1)
                last.then_inc(cx_mm.sem, 1)

            def sample(l, b, u, before, pages_next):
                if before is not None:
                    pe.wait_ge(*mx_in(l, b - 1))
                pe.wait_ge(*q_in(l, b + 1))
                for g in range(8):
                    if g < 7:
                        turn(l, b, u, g + 1)
                    elif pages_next is not None:
                        pe.wait_ge(*lat_in[1 - u](l, pages_next))
                        turn(l, b + 1, 1 - u, 0)
                    keys(l, b, u, g)
                    if g == 2 and before is not None:
                        context(l, before, 1 - u)

            pe.sem_inc(o_mm.sem, 2)
            pe.sem_inc(pair_mm.sem, 2)
            pe.sem_inc(cx_mm.sem, 2)
            pe.wait_ge(m_sq.sem, 1)
            for k in range(KT):
                last = mm(ps[:, 0, 0:MEM], ones, pt[:, k, 0:MEM], start=k == 0, stop=k == KT - 1)
            last.then_inc(m_ss.sem, 1)
            pe.wait_ge(m_rs.sem, 1)

            pe.wait_ge(x_sq.sem, KT)
            for k in range(KT):
                last = mm(ps[:, 4, 0:T], ones, u3[:, k, :], start=k == 0, stop=k == KT - 1)
            last.then_inc(x_ss.sem, 1)

            with pe.Fori(0, DEPTH) as l:
                with pe.Fori(0, FILL) as i:
                    for u in range(2):
                        pe.wait_ge(*u_ready(l, 1))
                        pe.wait_ge(*slot_in[u](l, 16 * i + 16))
                        for a in range(2):
                            pe.wait_ge(*(pj_dve if a else pj_act)(l, 2 * i + (u - 1)))
                            tile_mm(l, None, u, a, 2 * u + a)
                for m in range(4 * FILL, IN_TILES):
                    if m % 2 == 0:
                        slot(l, m // 2)
                    pe.wait_ge(*(pj_dve if m % 2 else pj_act)(l, m // 2 - 1))
                    tile_mm(l, m, (m // 2) % 2, m % 2, m % 4)
                sums(l, 0, 4, [[(P, nsq[0][:, i, :]) for i in range(3)], [(P, nsq[1][:, i, :]) for i in range(2)],
                               [(ROPE, nsq[0][0:ROPE, 3, :])]])
                pe.wait_ge(*mem_ready(l, 1))
                pe.wait_ge(*pj_act(l, 22))
                pe.wait_ge(*pj_dve(l, 21))
                for c in range(2):
                    w = slot(l, R_MK + c).rearrange("p (h k m) -> p h k m", h=2, k=KT)
                    for h in range(2):
                        for k in range(KT):
                            last = mm(ps[:, 2 * c + h, 0:MEM], w[:, h, k, :], memn[:, k, :], start=k == 0, stop=k == KT - 1)
                    last.then_inc(slot_free.sem, 1)
                pe.drain().then_inc(n_in.sem, 1)
                pe.wait_ge(*n_rs(l, 1))
                for c in range(2):
                    w = slot(l, R_MV + c).rearrange("p (k n) -> p k n", k=4)
                    for m in range(2):
                        for k in range(4):
                            last = mm(ps[:, 6 + m, :], memn[:, 4 * c + k, m * P:(m + 1) * P], w[:, k, :],
                                      start=c == 0 and k == 0, stop=c == 1 and k == 3)
                    last.then_inc(slot_free.sem, 1)
                    if c == 0:
                        sums(l, 1, 4, [[(P, nsq[1][:, 2 * i:2 * i + 2, 0:MEM])] for i in range(2)], 2 * MEM)
                pe.drain().then_inc(mv_mm.sem, 1)
                pe.wait_ge(*n_rs(l, 2))
                pe.wait_ge(*g_wend(l, 1))
                for m in range(2):
                    t = slice(m * P, (m + 1) * P)
                    for at, k, row in ((0, 8, acum), (8, 8, gdt), (16, 8, wend), (24, 4, gi), (28, 4, lf)):
                        mm(ps[:, 4, 32 * m + at:32 * m + at + k], row[0:k, t], ident[0:k, 0:k], start=True, stop=True)
                for q in range(4):
                    ex = cst[0:8, K_EXP + q * P:K_EXP + (q + 1) * P]
                    mm(ps[:, 4, 64 + 8 * q:72 + 8 * q], ex, la[:, SEQ:T], start=True, stop=True)
                    mm(ps[:, 4, 96 + 8 * q:104 + 8 * q], ex, gdt[:, SEQ:T], start=True, stop=True)
                    last = mm(ps[:, 4, 128 + 24 * q:152 + 24 * q], cst[0:4, K_SEL + q * P:K_SEL + (q + 1) * P],
                              gsmall[0:4, 0:24], start=True, stop=True)
                last.then_inc(g_pe.sem, 1)
                pe.wait_ge(*n_out(l, 2))
                sums(l, 2, 0, heads(2))
                pe.wait_ge(*g_out(l, 1))
                pe.wait_ge(*mv_out(l, 1))
                uq = [ring[:, c, 0:1152].rearrange("p (h k m) -> p h k m", h=2, k=Q_TILES) for c in range(2)]

                def product(k):
                    c, bank = (k + 1) % 2, N_PRODUCT[k]
                    if k >= 4:
                        pe.wait_ge(*n_rs(l, max(k - 1, 3)))
                    for h in range(2):
                        head = 2 * c + h
                        if k < 7:
                            m = slice(0, P) if k < 5 else slice(P, P + ROPE)
                            parts = [(uq[c][:, h, i, m], pt[:, CQ + i, :]) for i in range(Q_TILES)]
                        else:
                            parts = [(wk[:, 2 * i + c, 2 + h * P:2 + (h + 1) * P], pt[:, CKV + i, :]) for i in range(2)]
                        for i, (w, x) in enumerate(parts):
                            last = mm(ps[0:N_WIDTH[k], bank + h, 0:T], w, x, start=i == 0, stop=i == len(parts) - 1)
                    last.then_inc(n_in.sem, 1)

                def product_sums(k):
                    if k >= 5:
                        pe.wait_ge(*n_out(l, k - 1))
                    n = N_WIDTH[k]
                    sums(l, k, N_SUMS[k], [[(n, nsq[k % 2][0:n, h, :])] for h in range(2)])

                for k in (3, 5, 7):
                    if k == 3:
                        slot(l, R_UQ)
                    if k == 7:
                        pe.wait_ge(*wsm_in(l, 32))
                    product(k)
                    if k == 3:
                        slot(l, R_UQ + 1)
                    product(k + 1)
                    if k == 5:
                        pe.drain().then_inc(slot_free.sem, 2)
                    product_sums(k)
                    product_sums(k + 1)
                pe.wait_ge(*n_out(l, 9))
                for m in range(2):
                    if m:
                        for h in range(HEADS + 1):
                            last = mm(ps[0:ROPE, h, 0:T], cst[0:ROPE, K_ROT:K_ROT + ROPE], QR[:, h, :], start=True, stop=True)
                        last.then_inc(r_mm.sem, 1)
                    for c in range(2):
                        last = mm(ps[:, 5 + m, :], pt[:, CKV + c, m * P:(m + 1) * P], wsm[:, 0, c * 512:(c + 1) * 512],
                                  start=c == 0, stop=c == 1)
                last.then_inc(lv_mm.sem, 1)
                pe.wait_ge(*r_out(l, 1))
                pe.wait_ge(*lv_out(l, 1))
                for h in range(3):
                    scores(l, h)
                for h in range(8):
                    pe.wait_ge(*s_p(l, h + 1))
                    if h >= 2:
                        pe.wait_ge(*s_pt(l, h - 1))
                    for m in range(2):
                        for q in range(2):
                            last = nc.tensor.transpose(ps[:, 2 + h % 2, m * 256 + q * P:m * 256 + (q + 1) * P],
                                                       att[:, h % 4, q, m * P:(m + 1) * P], ident)
                    last.then_inc(s_t.sem, 1)
                    if h < 5:
                        scores(l, h + 3)
                    pe.wait_ge(*s_pt(l, h + 1))
                    if h >= 2:
                        pe.wait_ge(*s_o(l, h - 1))
                    v = memV if h < 4 else mlaV
                    for m in range(2):
                        last = mm(ps[:, 4 + h % 2, 0:SEQ], v[:, m, (h % 4) * P:(h % 4 + 1) * P], attT[:, h % 2, m, :],
                                  start=m == 0, stop=m == 1)
                    last.then_inc(s_y.sem, 1)
                pe.wait_ge(*pre_in(l, 1))
                for h in range(HEADS):
                    for c in range(2):
                        at = (c * 4 + h) * NB
                        mm(ps[:, 6, at:at + NB], wsm[:, 1, h * 256 + c * P:h * 256 + (c + 1) * P],
                           pre[:, 0, h * NB:(h + 1) * NB], start=True, stop=True)
                mm(ps[:, 6, 64:96], ones, pre[:, 1, :], start=True, stop=False)
                mm(ps[:, 6, 64:96], ones[0:ROPE, :], pre[0:ROPE, 2, :], start=False, stop=True).then_inc(pre_mm.sem, 1)
                for h in range(HEADS):
                    last = mm(ps[0:NB, 7, h * P:(h + 1) * P], pt[:, XQ + h, SEQ:T], ident, start=True, stop=True)
                last.then_inc(pre_mm.sem, 1)
                wq = slot(l, R_MLQK)[:, 0:1024].rearrange("p (a h m) -> p a h m", a=2, h=4)
                pe.wait_ge(*s_o(l, 8))
                pe.wait_ge(*pre_out(l, 1))
                pe.wait_ge(*xc_ready(l, 1))
                for h in range(HEADS):
                    last = mm(ps[:, h, 0:T], wq[:, 0, h, :], xc[:, 8 + h, :], start=True, stop=True)
                last.then_inc(tok_mm.sem, 1)
                pe.wait_ge(*tok_act(l, 1))
                for h in range(HEADS):
                    last = mm(ps[:, h, 0:T], wq[:, 1, h, :], xc[:, 8 + h, :], start=True, stop=True)
                last.then_inc(tok_mm.sem, 1)
                for m in range(2):
                    for h in range(HEADS):
                        last = mm(ps[:, 4 + m, h * P:(h + 1) * P], xc[:, 8 + h, m * P:(m + 1) * P], wq[:, 1, h, :],
                                  start=True, stop=True)
                last.then_inc(tok_mm.sem, 1)
                pe.drain().then_inc(slot_free.sem, 1)
                wvl = slot(l, R_MLV)[:, 0:512].rearrange("p (h m) -> p h m", h=4)
                pe.wait_ge(*tok_act(l, 2))
                for m in range(2):
                    for h in range(HEADS):
                        last = mm(ps[:, m, h * P:(h + 1) * P], pt[:, 8 + h, m * P:(m + 1) * P], wvl[:, h, :],
                                  start=True, stop=True)
                last.then_inc(tok_mm.sem, 1)
                for m in range(2):
                    for h in range(4):
                        last = nc.tensor.transpose(ps[:, 2 + m, h * P:(h + 1) * P], xc[:, h, m * P:(m + 1) * P], ident)
                last.then_inc(tok_mm.sem, 1)
                pe.wait_ge(*pre_row(l, 1))
                pe.wait_ge(*tok_act(l, 3))
                for m in range(2):
                    for h in range(2):
                        last = nc.tensor.transpose(ps[:, 4, m * 256 + h * P:m * 256 + (h + 1) * P],
                                                   xc[:, 4 + h, m * P:(m + 1) * P], ident)
                last.then_inc(tok_mm.sem, 1)
                for h in range(HEADS):
                    last = mm(ps[:, 7, h * NB:(h + 1) * NB], wvl[:, h, :], pt[:, 8 + h, SEQ:T], start=True, stop=True)
                last.then_inc(tok_mm.sem, 1)
                pe.drain().then_inc(slot_free.sem, 1)
                pe.wait_ge(*tok_dve(l, 2))
                for bank, tiles in ((0, xc[:, 4:8, :]), (1, mlk), (2, mlq)):
                    for h in range(4):
                        last = mm(ps[0:NB, bank, h * P:(h + 1) * P], tiles[:, h, SEQ:T], ident, start=True, stop=True)
                last.then_inc(pre_mm.sem, 1)
                pe.wait_ge(*tok_act(l, 4))
                pe.wait_ge(*tok_dve(l, 3))
                pe.wait_ge(*weighted(l, 1))
                masked(l, 0)
                masked(l, 1)
                pe.wait_ge(*pre_row(l, 2))
                for n in range(3):
                    spread(l, n)
                ahead = 3
                for n in range(12):
                    recur(l, n)
                    if n in MASKED_AFTER:
                        masked(l, MASKED_AFTER[n])
                    while ahead < 12 and ahead <= (n + 3 if n < 5 else n + 2):
                        spread(l, ahead)
                        ahead += 1
                pe.wait_ge(*seg_out(l, 12))
                pe.wait_ge(*em_out(l, 4))
                for q in range(4):
                    for m in range(2):
                        mm(ps[:, 0, q * P:(q + 1) * P], xw[:, m, q * P:(q + 1) * P], btok[:, m, (q // 2) * P:(q // 2 + 1) * P],
                           start=m == 0, stop=m == 1)
                for h in range(HEADS):
                    for m in range(2):
                        mm(ps[:, 1, h * P:(h + 1) * P], vw[:, m, h * P:(h + 1) * P], ktok[:, m, h * P:(h + 1) * P],
                           start=m == 0, stop=m == 1)
                pe.wait_ge(*ry_out(l, 8))
                for h in range(HEADS):
                    for m in range(2):
                        last = mm(ps[0:1, 2, h * P:(h + 1) * P], cols[:, m, 28 + h:29 + h], ktok[:, m, h * P:(h + 1) * P],
                                  start=m == 0, stop=m == 1)
                last.then_inc(fin_mm.sem, 1)
                pe.wait_ge(*ns_in(l, 1))
                mm(ps[:, 7, 0:32], ones, pre[:, 0, :], start=True, stop=True).then_inc(nq_mm.sem, 1)
                pe.wait_ge(*fin_out(l, 1))
                pe.wait_ge(*lat_in[0](l, 512))
                turn(l, 0, 0, 0)
                sample(l, 0, 0, None, 512)
                with pe.Fori(0, NB // 2 - 1) as i:
                    for u in (1, 0):
                        b = 2 * i + (1 if u else 2)
                        sample(l, b, u, b - 1, 512 * i + 1024)
                sample(l, NB - 1, 1, NB - 2, None)
                sums(l, 9, 0, [[(P, nsq_ssd[:, 2 * i + j, :]) for j in range(2)] for i in range(2)])
                sums(l, 10, 2, heads(1))
                def by_feature(samples):
                    for c in range(2):
                        for b in samples:
                            at = 384 + (c * NB + b) * 4
                            last = mm(ps[:, 7, at:at + 4], ctxr[:, b, c * P:(c + 1) * P], ident[0:4, 0:4], start=True, stop=True)
                    return last

                pe.wait_ge(*cx_out(l, NB - 1))
                by_feature(range(NB - 1))
                context(l, NB - 1, 1)
                pe.wait_ge(*cx_out(l, NB))
                by_feature((NB - 1,)).then_inc(cr_mm.sem, 1)
                pe.wait_ge(*cr_out(l, 1))
                for h in range(HEADS):
                    for c in range(2):
                        last = mm(ps[:, 7, 448 + h * NB:448 + (h + 1) * NB], wsm[:, 0, c * 512 + h * P:c * 512 + (h + 1) * P],
                                  ctxall[:, c, h, :], start=c == 0, stop=c == 1)
                last.then_inc(uv_mm.sem, 1)
                def out_tile(m, c):
                    pe.wait_ge(*slot_in[c](l, 8 * (m - c) + 16 * (R_OUT // 2 + 1)))
                    pe.wait_ge(*o_out(l, m - 1))
                    w = ring[:, c, :].rearrange("p (k m) -> p k m", k=MIX_TILES)
                    for i, k in enumerate(MIX_ORDER):
                        if type(m) is int and m == 0 and i == MIX_TILES - 4:
                            pe.wait_ge(*mixed(l, 2))
                        last = mm(ps[:, c, 0:T], w[:, k, :], pt[:, Z + k, :], start=i == 0, stop=i == MIX_TILES - 1)
                    last.then_inc(o_mm.sem, 1)

                def x_sum(m, start=False, stop=False):
                    pe.wait_ge(*x_sq(l, m + 1))
                    x2 = u3[:, m, :] if type(m) is int else u3[:, bass.ds(m, 1), :].rearrange("p o t -> p (o t)")
                    return mm(ps[:, 4, 0:T], ones, x2, start=start, stop=stop)

                pe.wait_ge(*mixed(l, 1))
                for m in range(4):
                    out_tile(m, m % 2)
                    if m >= 2:
                        x_sum(m - 2, start=m == 2)
                with pe.Fori(2, OUT_TILES // 2) as i:
                    for c in range(2):
                        out_tile(2 * i + c, c)
                        x_sum(2 * i + (c - 2))
                x_sum(OUT_TILES - 2)
                x_sum(OUT_TILES - 1, stop=True).then_inc(x_ss.sem, 1)
                pe.drain().then_inc(layer_free.sem, 1)

        @block.scalar
        def _(act):
            fn = nc.scalar.activation

            def root(out, mean, scale=1.0):
                fn(out, mean, ACT.Ln, bias=eps[0:out.shape[0]], scale=scale)
                act.drain()
                return fn(out, out, ACT.Exp, scale=-0.5)

            def squares(l, k, parts):
                if k:
                    act.wait_ge(*n_ss(l, max(k - 1, 1)))
                for i, (rows_, first_tile, src, n) in enumerate(parts):
                    tiles, width = src.shape[1], src.shape[2]
                    last = fn(nsq[k % 2 if k else i % 2][0:rows_, first_tile:first_tile + tiles, 0:width],
                              src, ACT.Square, scale=n ** -0.5)
                last.then_inc(n_sq.sem, 1)

            def roots(l, k, out, mean, used=None):
                act.wait_ge(*n_ss(l, k + 1))
                if k:
                    act.wait_ge(*n_out(l, used or k))
                root(out, mean).then_inc(n_rs.sem, 1)

            def probs(l, h):
                act.wait_ge(*s_max(l, h + 1))
                for q in range(2):
                    last = fn(att[:, h % 4, q, :], att[:, h % 4, q, :], ACT.Exp, bias=asm[:, h % 4, q:q + 1],
                              accum_out=asm[:, h % 4, 2 + q:3 + q])
                last.then_inc(s_exp.sem, 1)

            def copy_pair(l, b, g):
                act.wait_ge(*t_mm(l, 8 * b + (g + 1)))
                act.wait_ge(*pair_mm(l, 8 * b + (g - 1)))
                fn(latT[:, g % 2], ps[:, 0, :], ACT.Copy).then_inc(t_sb.sem, 1)

            def square(l, b, j, u):
                n = PAGES * b + j
                act.wait_ge(*k_mm(l, n + 1))
                first_bank, scores_at, keys_at = 1 + 2 * (j % 2), 256 * u, 2 - 2 * u
                fn(raws[:, u, j, :].rearrange("p (a h) -> p a h", a=2),
                   ps[:, first_bank:first_bank + 2, scores_at:scores_at + 2], ACT.Copy)
                act.wait_ge(*k_red(l, n - 1))
                fn(sqd[:, j % 2, :].rearrange("p (a n) -> p a n", a=2),
                   ps[:, first_bank:first_bank + 2, keys_at:keys_at + 256], ACT.Square).then_inc(k_sq.sem, 1)

            def key_roots(l, b, u):
                act.wait_ge(*k_red(l, PAGES * b + PAGES))
                root(ssq[:, u], ssq[:, u], 1.0 / P).then_inc(k_rs.sem, 1)

            def exps(l, b, u):
                act.wait_ge(*s_sub(l, b + 1))
                fn(prob[:, u], prob[:, u], ACT.Exp, scale=MLA_SCALE)
                fn(probx[:, u], probx[:, u], ACT.Exp, scale=X_SCALE)
                fn(sm[:, u, 24:28], sm[:, u, 24:28], ACT.Exp, scale=MLA_SCALE).then_inc(p_exp.sem, 1)

            def save_states(l, b, u):
                act.wait_ge(*st_new(l, b + 1))
                for s, name in ((0, "o_ssm_s"), (1, "o_C_s")):
                    act.dma_start(d[name][bass.ds(l * NB + b, 1)].rearrange("o p n -> p (o n)"), states[:, u, s, :]
                                  ).then_inc(st_saved[u].sem, 16)

            def sample(l, b, u, before, more=True):
                if before is not None:
                    save_states(l, before, 1 - u)
                    key_roots(l, before, 1 - u)
                for g in range(8):
                    if g < 7:
                        copy_pair(l, b, g + 1)
                    elif more:
                        copy_pair(l, b + 1, 0)
                    square(l, b, 2 * g, u)
                    square(l, b, 2 * g + 1, u)
                    if g == 1 and before is not None:
                        exps(l, before, 1 - u)

            nc.scalar.preload_act_table_set(LN_EXP)
            act.sem_inc(pj_act.sem, 2)
            act.sem_inc(t_sb.sem, 1)
            act.sem_inc(k_sq.sem, 2)
            act.wait_ge(m_ss.sem, 1)
            root(rsm[:, :], ps[:, 0, 0:MEM], 1.0 / D_MODEL).then_inc(m_rs.sem, 1)
            with act.Fori(0, DEPTH) as l:
                act.wait_ge(*layer_free(l, 0))
                act.wait_ge(*x_ss(l, 0))
                root(nrs[:, 0, :], ps[:, 4, 0:T], 1.0 / D_MODEL).then_inc(x_rs.sem, 1)
                with act.Fori(0, FILL) as i:
                    for u in range(2):
                        act.wait_ge(*pj_mm(l, 4 * i + (2 * u + 1)))
                        fn(pt[:, bass.ds(4 * i + 2 * u, 1), :].rearrange("p o t -> p (o t)"), ps[:, 2 * u, 0:T], ACT.Copy
                           ).then_inc(pj_act.sem, 1)
                act.wait_ge(*pj_mm(l, 41))
                fn(pt[:, 40, :], ps[:, 0, 0:T], ACT.Copy).then_inc(pj_act.sem, 1)
                act.drain()
                act.wait_ge(*pj_dve(l, 20))
                squares(l, 0, ((P, 0, pt[:, CQ:CQ + 3, :], 3 * P), (P, 0, pt[:, CKV:CKV + 2, :], 2 * P),
                               (ROPE, 3, pt[0:ROPE, KR:KR + 1, :], ROPE)))
                act.wait_ge(*pj_mm(l, 43))
                fn(pt[:, 42, :], ps[:, 2, 0:T], ACT.Copy).then_inc(pj_act.sem, 1)
                act.wait_ge(*par_in(l, 16))
                fn(gdt[:, :], pt[0:8, GATE, :], ACT.Copy)
                fn(li[0:4, :], pt[32:36, GATE, :], ACT.Copy)
                fn(lf[0:4, :], pt[64:68, GATE, :], ACT.Copy).then_inc(g_raw.sem, 1)
                for c in range(CT):
                    last = fn(xc[:, c, 0:SEQ], pt[:, c, 0:SEQ], ACT.Identity, bias=par[:, C_CB + c:C_CB + c + 1],
                              scale=par[:, C_CW + 3 * CT + c:C_CW + 3 * CT + c + 1])
                last.then_inc(conv_a.sem, 1)
                act.wait_ge(*g_neg(l, 1))
                fn(softp[:, 0, :], softp[:, 0, :], ACT.Exp)
                fn(softp[0:4, 1, :], softp[0:4, 1, :], ACT.Exp)
                fn(gsmall[:, 32:33], par[0:8, C_ALOG:C_ALOG + 1], ACT.Exp)
                act.drain()
                fn(softp[:, 0, :], softp[:, 0, :], ACT.Ln, bias=1.0)
                fn(softp[0:4, 1, :], softp[0:4, 1, :], ACT.Ln, bias=1.0).then_inc(g_log.sem, 1)
                roots(l, 0, nrs[:, 0:3, :], ps[:, 4:7, 0:T])
                fn(pt[:, Z:Z + 16, :], pt[:, Z:Z + 16, :], ACT.Silu)
                fn(pt[:, OG:OG + 4, :], pt[:, OG:OG + 4, :], ACT.Sigmoid).then_inc(z_ready.sem, 1)
                nc.scalar.preload_act_table_set(LN_EXP)
                act.wait_ge(*g_scan(l, 1))
                fn(wend[:, 0:SEQ], acum[:, 0:SEQ], ACT.Exp, bias=acum[:, SEQ - 1:SEQ], scale=-1.0)
                fn(lf[0:4, 0:SEQ], gi[0:4, 0:SEQ], ACT.Exp, bias=nmx[0:4, SEQ - 1:SEQ])
                fn(la[:, SEQ:T], la[:, SEQ:T], ACT.Exp)
                fn(gsmall[0:4, 0:24], gsmall[0:4, 0:24], ACT.Exp).then_inc(g_exp.sem, 1)
                act.wait_ge(*n_in(l, 1))
                squares(l, 1, ((P, 0, ps[:, 0:4, 0:MEM], P),))
                squares(l, 2, ((P, 0, pt[:, XQ:XQ + 4, :], P),))
                act.wait_ge(*n_ss(l, 2))
                roots(l, 1, nrs[:, :, 0:MEM].rearrange("p (a h) t -> p a h t", a=2),
                      ps[:, 4:6, :].rearrange("p a (h t) -> p a h t", h=2))
                act.wait_ge(*mv_mm(l, 1))
                fn(memV, ps[:, 6:8, :], ACT.Copy).then_inc(mv_out.sem, 1)
                roots(l, 2, nrs, ps[:, 0:4, 0:T])
                for pair in (3, 5, 7):
                    for k in (pair, pair + 1):
                        n, bank = N_WIDTH[k], N_PRODUCT[k]
                        act.wait_ge(*n_in(l, k - 1))
                        squares(l, k, ((n, 0, ps[0:n, bank:bank + 2, 0:T], n),))
                    for k in (pair, pair + 1):
                        n, bank, half = N_WIDTH[k], N_SUMS[k], 2 * (k % 2)
                        roots(l, k, nrs[0:n, half:half + 2], ps[0:n, bank:bank + 2, 0:T], k - 1 if k > 3 else k)
                act.wait_ge(*lv_mm(l, 1))
                fn(mlaV, ps[:, 5:7, :], ACT.Copy).then_inc(lv_out.sem, 1)
                probs(l, 0)
                probs(l, 1)
                for h in range(8):
                    act.wait_ge(*s_t(l, h + 1))
                    if h >= 2:
                        act.wait_ge(*s_y(l, h - 1))
                    fn(attT[:, h % 2], ps[:, 2 + h % 2, :], ACT.Copy).then_inc(s_pt.sem, 1)
                    if h < 6:
                        probs(l, h + 2)
                act.wait_ge(*conv_d(l, 1))
                fn(xc[:, :, :], xc[:, :, :], ACT.Silu).then_inc(xc_ready.sem, 1)
                nc.scalar.preload_act_table_set(LN_EXP)
                act.wait_ge(*conv_saved(l, 16))
                act.wait_ge(*kv_saved(l, 32))
                act.wait_ge(*tok_mm(l, 1))
                fn(mlq, ps[:, 0:4, 0:T], ACT.Copy).then_inc(tok_act.sem, 1)
                act.wait_ge(*tok_mm(l, 2))
                fn(mlk, ps[:, 0:4, 0:T], ACT.Copy, scale=K_SCALE).then_inc(tok_act.sem, 1)
                act.wait_ge(*tok_mm(l, 3))
                fn(ktok, ps[:, 4:6, :], ACT.Copy, scale=K_SCALE).then_inc(tok_act.sem, 1)
                act.wait_ge(*tok_mm(l, 6))
                fn(btok[:, :, :], ps[:, 4, :].rearrange("p (m n) -> p m n", m=2), ACT.Copy).then_inc(tok_act.sem, 1)
                for n in range(12):
                    act.wait_ge(*seg_out(l, n + 1))
                    fn(dec[:, n % 4, :], dec[:, n % 4, :], ACT.Exp).then_inc(seg_exp.sem, 1)
                    if n >= 8:
                        fn(emm[:, n - 8, :], ps[:, n % 2, 256:512], ACT.Exp, scale=-1.0).then_inc(em_out.sem, 1)
                act.wait_ge(*fin_mm(l, 1))
                fn(A1[:, 0:1024], ps[:, 0:2, :], ACT.Copy)
                fn(A1[0:1, 1024:1536], ps[0:1, 2, :], ACT.Copy).then_inc(fin_out.sem, 1)
                copy_pair(l, 0, 0)
                sample(l, 0, 0, None)
                with act.Fori(0, NB // 2 - 1) as i:
                    for u in (1, 0):
                        b = 2 * i + (1 if u else 2)
                        sample(l, b, u, b - 1)
                sample(l, NB - 1, 1, NB - 2, more=False)
                act.wait_ge(*a_ready(l, 1))
                fn(nsq_ssd, xc[:, 0:4, :], ACT.Square, scale=(2 * P) ** -0.5).then_inc(n_sq.sem, 1)
                save_states(l, NB - 1, 1)
                key_roots(l, NB - 1, 1)
                fn(nsq[1], xc[:, 8:12, :], ACT.Square, scale=P ** -0.5).then_inc(n_sq.sem, 1)
                exps(l, NB - 1, 1)
                act.wait_ge(*n_ss(l, 10))
                root(nrs[:, 0:2, :], ps[:, 0:2, 0:T]).then_inc(n_rs.sem, 1)
                act.wait_ge(*n_ss(l, 11))
                root(nrs_ml, ps[:, 2:6, 0:T]).then_inc(n_rs.sem, 1)
                act.drain().then_inc(layer_free.sem, 1)
            for u in range(2):
                act.wait_ge(*st_saved[u](DEPTH - 1, 32 * 4))
            act.wait_ge(*x_ss(DEPTH - 1, 1))
            root(nrs[:, 0, :], ps[:, 4, 0:T], 1.0 / D_MODEL).then_inc(f_rs.sem, 1)

        @block.vector
        def _(dve):
            tt, ts, stt = nc.vector.tensor_tensor, nc.vector.tensor_scalar, nc.vector.scalar_tensor_tensor
            red, copy = nc.vector.tensor_reduce, nc.vector.tensor_copy

            def col(i, k=P):
                return par[0:k, i:i + 1]

            def over(ap, n, axis=2):
                v = ap.unsqueeze(axis)
                shape = list(v.shape)
                shape[axis] = n
                return v.broadcast_to(shape)

            def at_b(t, b):
                return t[:, bass.ds(b, 1), :].rearrange("p o h -> p (o h)")

            def seg(l, n):
                dve.wait_ge(*bc_mm(l, n + 1))
                if n >= 4:
                    dve.wait_ge(*ry_mm(l, n - 3))
                c, op = (n, ALU.subtract) if n < 8 else (24 + n - 8, ALU.add)
                ts(dec[:, n % 4, 0:256], ps[:, spread_bank(n), 0:256], cols[:, 0, c:c + 1], 0.0, op, ALU.min)
                ts(dec[:, n % 4, 256:384], ps[:, spread_bank(n), P:256], cols[:, 1, c:c + 1], 0.0, op, ALU.min
                   ).then_inc(seg_out.sem, 1)

            def rec_out(l, n):
                if n < 8 and n % 2 == 0:
                    return
                dve.wait_ge(*ry_mm(l, n + 1))
                if n < 8:
                    q = n // 2
                    stt(xc[:, q, 0:SEQ], xc[:, q, 0:SEQ], col(C_D + q), ps[:, 2 + q % 2, 0:SEQ], ALU.mult, ALU.add
                        ).then_inc(ry_out.sem, 1)
                else:
                    h = n - 8
                    dve.wait_ge(*em_out(l, h + 1))
                    e = emm[:, h, :]
                    stt(e, ps[:, 4 + h % 2, 0:SEQ], -1.0, e, ALU.mult, ALU.max)
                    copy(xc[:, 8 + h, 0:SEQ], ps[:, 2 + h % 2, 0:SEQ])
                    dve.drain()
                    tt(e, ps[:, 4 + h % 2, 0:SEQ], e, ALU.max).then_inc(ry_out.sem, 1)

            def divide(h):
                nc.vector.reciprocal(emm[:, h, :], emm[:, h, :])
                dve.drain()
                tt(xc[:, 8 + h, 0:SEQ], xc[:, 8 + h, 0:SEQ], emm[:, h, :], ALU.mult)

            def key_sum(l, b, u, j):
                dve.wait_ge(*k_sq(l, PAGES * b + (j + 1)))
                red(ssq[:, u, j, :], sqd[:, j % 2, :].rearrange("p (h n) -> p h n", h=4), AXX, ALU.add
                    ).then_inc(k_red.sem, 1)

            def update(l, b, u, s):
                st = states[:, u, s, :].rearrange("p (h n) -> p h n", h=4)
                if s:
                    dve.drain()
                if s == 0:
                    for g in range(2):
                        tt(dtmp[:, g * 256:(g + 1) * 256].rearrange("p (r n) -> p r n", r=2),
                           over(rows[:, g * P:(g + 1) * P], 2, 1),
                           over(dtx[:, bass.ds(b, 1), 2 * g:2 * g + 2].rearrange("p o h -> p (o h)"), P), ALU.mult)
                else:
                    tt(dtmp[:, :].rearrange("p (h n) -> p h n", h=4),
                       rows[:, ROW_K:ROW_K + 512].rearrange("p (h n) -> p h n", h=4), over(at_b(wv, b), P), ALU.mult)
                dve.drain()
                tt(states[:, u, s, :], states[:, u, s, :], dtmp[:, :], ALU.add)
                dve.drain()
                if s == 0:
                    for g in range(2):
                        tt(dtmp[:, g * 256:(g + 1) * 256].rearrange("p (r n) -> p r n", r=2), st[:, 2 * g:2 * g + 2, :],
                           over(rows[:, ROW_C + g * P:ROW_C + (g + 1) * P], 2, 1), ALU.mult)
                else:
                    last = tt(dtmp[:, :], states[:, u, s, :], rows[:, ROW_Q:ROW_Q + 512], ALU.mult)
                    last.then_inc(st_new.sem, 1)
                dve.drain()
                last = red(at_b(ysa if s == 0 else ysb, b), dtmp[:, :].rearrange("p (h n) -> p h n", h=4), AXX, ALU.add)
                return last

            def mem_scores(l, b, u):
                dve.wait_ge(*mk_in(l, 16 * b + 16))
                k = memk.rearrange("p (m n) -> p m n", m=2)
                tt(k, k, over(rows[:, ROW_X:ROW_X + 512], 2, 1), ALU.mult)
                dve.drain()
                red(sx[:, u].rearrange("p m h -> p (m h)"), memk.rearrange("p (a n) -> p a n", a=8), AXX, ALU.add
                    ).then_inc(memk_used.sem, 1)

            def softmax_max(l, b, u):
                dve.wait_ge(*k_rs(l, b + 1))
                dve.wait_ge(*pair_mm(l, 8 * b + 8))
                rot = ps[:, 5 + u, 0:64].rearrange("p (j a h) -> p a j h", a=2, h=4)
                tt(prob[:, u], raws[:, u], ssq[:, u], ALU.mult)
                dve.drain()
                s = prob[:, u].rearrange("p (a j) h -> p a j h", a=2)
                tt(s, rot, s, ALU.add)
                dve.drain()
                red(sm[:, u, 0:4], prob[:, u].rearrange("p j h -> p h j"), AXX, ALU.max)
                red(sm[:, u, 4:8], sx[:, u].rearrange("p m h -> p h m"), AXX, ALU.max).then_inc(mx_in.sem, 1)

            def softmax_shift(l, b, u):
                dve.wait_ge(*mx_all(l, b + 1))
                tt(sm[:, u, 8:12], sm[:, u, 8:12], at_b(scur, b), ALU.max)
                dve.drain()
                tt(prob[:, u], prob[:, u], over(sm[:, u, 8:12], PAGES, 1), ALU.subtract)
                tt(probx[:, u], sx[:, u], over(sm[:, u, 12:16], 2, 1), ALU.subtract)
                tt(sm[:, u, 24:28], at_b(scur, b), sm[:, u, 8:12], ALU.subtract).then_inc(s_sub.sem, 1)

            def softmax_sum(l, b, u):
                dve.wait_ge(*p_exp(l, b + 1))
                red(sm[:, u, 16:20], prob[:, u].rearrange("p j h -> p h j"), AXX, ALU.add)
                red(sm[:, u, 20:24], probx[:, u].rearrange("p m h -> p h m"), AXX, ALU.add).then_inc(p_sum.sem, 1)

            def context_out(l, b, u):
                dve.wait_ge(*cx_mm(l, b + 1))
                at = 32 * u
                own = sm[:, u, 24:28]
                copy(at_b(owns, b), own)
                tt(at_b(dens, b), ps[:, 7, at:at + 4], own, ALU.add)
                nc.vector.reciprocal(sm[:, u, 36:40], ps[:, 7, at + 4:at + 8])
                copy(ctxr[:, bass.ds(b, 1), :].rearrange("p o n -> p (o n)"), ps[0:4, 7, 128:384])
                dve.drain()
                tt(at_b(ysd, b), ps[:, 7, at + 16:at + 20], sm[:, u, 36:40], ALU.mult).then_inc(cx_out.sem, 1)

            def query(l, b, u):
                copy(wk[:, :, 258 * u:258 * u + 2], qabs[:, bass.ds(b, 1), :, :].rearrange("p o c (a h) -> p (o c a) h", a=2)
                     ).then_inc(q_in.sem, 1)

            def gated():
                by = lambda ap: ap.rearrange("p b h -> p h b")
                dve.drain()
                tt(xc[:, 8:12, SEQ:T], by(ysb[:, :, :]), pre[:, 1, :].rearrange("p (h b) -> p h b", h=4), ALU.mult)
                tt(xc[:, 0:4, SEQ:T], xc[:, 0:4, SEQ:T], over(par[:, C_D:C_D + 4], NB), ALU.mult)
                dve.drain()
                tt(xc[:, 8:12, :], xc[:, 8:12, :], pt[:, OG:OG + 4, :], ALU.mult)
                tt(xc[:, 0:4, SEQ:T], xc[:, 0:4, SEQ:T], by(ysa[:, :, :]), ALU.add)
                dve.drain()
                tt(xc[:, 0:4, :], xc[:, 0:4, :], pt[:, Z:Z + 4, :], ALU.mult).then_inc(a_ready.sem, 1)

            def sample(l, b, u, before, more=True):
                if before is not None:
                    softmax_max(l, before, 1 - u)
                for j in range(PAGES):
                    key_sum(l, b, u, j)
                    if before is not None:
                        if j == 1:
                            softmax_shift(l, before, 1 - u)
                        if j == 2 and more:
                            query(l, b + 1, 1 - u)
                        if j == 3:
                            softmax_sum(l, before, 1 - u)
                        if j == 7:
                            context_out(l, before, 1 - u)
                    elif j in (1, 3, 5, 14):
                        divide((1, 3, 5, 14).index(j))
                    if j == 6:
                        dve.wait_ge(*rows_in(l, 16 * b + 16))
                        mem_scores(l, b, u)
                    if j == 8:
                        dve.wait_ge(*decayed(l, b + 1))
                        update(l, b, u, 0)
                    if j == 10:
                        update(l, b, u, 1).then_inc(rows_used.sem, 1)
                    if j == 11 and not more:
                        gated()

            dve.sem_inc(layer_free.sem, 4)
            dve.sem_inc(pj_dve.sem, 2)
            dve.sem_inc(k_red.sem, 2)
            dve.sem_inc(mx_in.sem, 2)
            dve.sem_inc(cx_out.sem, 2)
            dve.sem_inc(o_out.sem, 2)
            for u in range(2):
                dve.sem_inc(st_saved[u].sem, 32)
            nc.vector.memset(qrs[:, :, :], 0.0)
            dve.wait_ge(first.sem, 32)
            tt(pt[:, 0:8, 0:MEM], memn, memn, ALU.mult).then_inc(m_sq.sem, 1)
            dve.wait_ge(x_in.sem, 16)

            for k in range(KT):
                tt(u3[:, k, :], xT[:, k, :], xT[:, k, :], ALU.mult).then_inc(x_sq.sem, 1)

            with dve.Fori(0, DEPTH) as l:
                dve.wait_ge(*layer_free(l, 0))
                dve.wait_ge(*par_in(l, 16))
                dve.wait_ge(*x_rs(l, 1))
                for k in range(KT):
                    last = stt(u3[:, k, :], xT[:, k, :], col(C_NORM + k), nrs[:, 0, :], ALU.mult, ALU.mult)
                    if k % 4 == 3:
                        last.then_inc(u_ready.sem, 1)
                dve.wait_ge(second.sem, 32)
                dve.wait_ge(m_rs.sem, 1)
                dve.wait_ge(*mem_in(l, 16))
                for k in range(KT):
                    last = stt(memn[:, k, :], memn[:, k, :], col(C_MEM + k), rsm[:, :], ALU.mult, ALU.mult)
                last.then_inc(mem_ready.sem, 1)
                with dve.Fori(0, FILL) as i:
                    for u in range(2):
                        dve.wait_ge(*pj_mm(l, 4 * i + (2 * u + 2)))
                        copy(pt[:, bass.ds(4 * i + (2 * u + 1), 1), :].rearrange("p o t -> p (o t)"), ps[:, 2 * u + 1, 0:T]
                             ).then_inc(pj_dve.sem, 1)
                dve.wait_ge(*pj_mm(l, 42))
                copy(pt[:, 41, :], ps[:, 1, 0:T]).then_inc(pj_dve.sem, 1)
                dve.drain()
                dve.wait_ge(*pj_act(l, 22))
                dve.wait_ge(*g_raw(l, 1))
                ts(gdt[:, :], gdt[:, :], col(C_DTB, 8), None, ALU.add)
                ts(li[0:4, :], li[0:4, :], col(C_BI, 4), None, ALU.add)
                ts(lf[0:4, :], lf[0:4, :], col(C_BF, 4), None, ALU.add)
                dve.drain()
                stt(softp[:, 0, :], gdt[:, :], -1.0, gdt[:, :], ALU.mult, ALU.min)
                stt(softp[0:4, 1, :], lf[0:4, :], -1.0, lf[0:4, :], ALU.mult, ALU.min).then_inc(g_neg.sem, 1)
                dve.wait_ge(*n_rs(l, 1))
                for i, tile, g, n in ((0, CQ, C_Q, 3), (1, CKV, C_KV, 2)):
                    for c in range(n):
                        stt(pt[:, tile + c, :], pt[:, tile + c, :], col(g + c), nrs[:, i, :], ALU.mult, ALU.mult)
                stt(QR[:, HEADS, :], pt[0:ROPE, KR, :], col(C_KNR, ROPE), nrs[0:ROPE, 2, :], ALU.mult, ALU.mult
                    ).then_inc(n_out.sem, 1)
                def tap(j):
                    s = 3 - j
                    if j < 2:
                        dve.drain()
                    for c in range(CT):
                        stt(xc[:, c, s:SEQ], pt[:, c, 0:SEQ - s], col(C_CW + j * CT + c), xc[:, c, s:SEQ], ALU.mult, ALU.add)

                dve.wait_ge(*conv_a(l, 1))
                tap(2)
                dve.wait_ge(*g_log(l, 1))
                stt(gdt[:, :], gdt[:, :], 0.0, softp[:, 0, :], ALU.max, ALU.add)
                stt(lf[0:4, :], lf[0:4, :], 0.0, softp[0:4, 1, :], ALU.min, ALU.subtract)
                dve.drain()
                ts(la[:, :], gdt[:, :], gsmall[:, 32:33], -1.0, ALU.mult, ALU.mult)
                dve.drain()
                one8 = cst[0:8, K_ONE:K_ONE + SEQ]
                scan = nc.vector.tensor_tensor_scan
                scan(acum[:, 0:SEQ], one8, la[:, 0:SEQ], 0.0, ALU.mult, ALU.add)
                scan(mT[0:4, 0:SEQ], one8[0:4], lf[0:4, 0:SEQ], 0.0, ALU.mult, ALU.add)
                tt(lf[0:4, SEQ:T], lf[0:4, SEQ:T], par[0:4, C_M0:C_M0 + NB], ALU.add)
                dve.drain()
                tt(gi[0:4, 0:SEQ], li[0:4, 0:SEQ], mT[0:4, 0:SEQ], ALU.subtract)
                tt(mT[0:4, SEQ:T], lf[0:4, SEQ:T], li[0:4, SEQ:T], ALU.max)
                dve.drain()
                scan(nmx[0:4, 0:SEQ], one8[0:4], gi[0:4, 0:SEQ], 0.0, ALU.mult, ALU.max)
                tt(gsmall[0:4, 0:8], lf[0:4, SEQ:T], mT[0:4, SEQ:T], ALU.subtract)
                tt(gsmall[0:4, 8:16], li[0:4, SEQ:T], mT[0:4, SEQ:T], ALU.subtract)
                ts(gsmall[0:4, 16:24], mT[0:4, SEQ:T], -1.0, None, ALU.mult)
                dve.drain()
                tt(mT[0:4, 0:SEQ], mT[0:4, 0:SEQ], nmx[0:4, 0:SEQ], ALU.add)
                dve.drain()
                ts(nmx[0:4, 0:SEQ], nmx[0:4, 0:SEQ], -1.0, None, ALU.mult).then_inc(g_scan.sem, 1)
                dve.wait_ge(*g_exp(l, 1))
                tt(wend[:, 0:SEQ], wend[:, 0:SEQ], gdt[:, 0:SEQ], ALU.mult).then_inc(g_wend.sem, 1)
                tap(1)
                dve.wait_ge(*n_rs(l, 2))
                stt(mkT, ps[:, 0:4, 0:MEM], col(C_XK), nrs[:, :, 0:MEM], ALU.mult, ALU.mult).then_inc(n_out.sem, 1)
                dve.wait_ge(*g_pe(l, 1))
                bank = ps[:, 4, :]
                copy(cols[:, :, :], bank[:, 0:64].rearrange("p (m n) -> p m n", m=2))
                copy(da[:, :, :], bank[:, 64:96].rearrange("p (q b) -> p b q", q=4))
                copy(dtx[:, :, :], bank[:, 96:128].rearrange("p (q b) -> p b q", q=4))
                copy(gb[:, :, :, :].rearrange("p k b h -> p h k b"), bank[:, 128:224].rearrange("p (h k b) -> p h k b", h=4, k=3)
                     ).then_inc(g_out.sem, 1)
                tap(0)
                dve.drain()
                now = xc[:, :, SEQ:T]
                t = dtmp[:, 0:96].rearrange("p (c b) -> p c b", b=NB)
                old = par[:, C_ST:].rearrange("p (c j b) -> p j c b", j=3, b=NB)
                tt(now, pt[:, 0:CT, SEQ:T], over(par[:, C_CW + 3 * CT:C_CW + 4 * CT], NB), ALU.mult)
                dve.drain()
                tt(now, now, over(par[:, C_CB:C_CB + CT], NB), ALU.add)
                for j in range(3):
                    tt(t, old[:, j], over(par[:, C_CW + j * CT:C_CW + (j + 1) * CT], NB), ALU.mult)
                    dve.drain()
                    last = tt(now, now, t, ALU.add)
                    if j < 2:
                        dve.drain()
                last.then_inc(conv_d.sem, 1)
                dve.wait_ge(*n_rs(l, 3))
                stt(pt[:, XQ:XQ + 4, :], pt[:, XQ:XQ + 4, :], col(C_XQ), nrs, ALU.mult, ALU.mult).then_inc(n_out.sem, 1)
                dve.wait_ge(*conv_saved(l, 16))
                for k in range(3, 9):
                    n, bank, half, head = N_WIDTH[k], N_PRODUCT[k], 2 * (k % 2), 2 * ((k + 1) % 2)
                    dst, g = ((qn, C_QNN), (QR, C_QNR), (kn, C_KNN))[(k - 3) // 2]
                    dve.wait_ge(*n_rs(l, k + 1))
                    stt(dst[:, head:head + 2, :], ps[0:n, bank:bank + 2, 0:T], col(g, n), nrs[0:n, half:half + 2],
                        ALU.mult, ALU.mult).then_inc(n_out.sem, 1)
                dve.wait_ge(*r_mm(l, 1))
                t = scr[0:ROPE, 0:5 * T].rearrange("p (h t) -> p h t", h=5)
                cos, sin = (over(cst[0:ROPE, i:i + T], 5, 1) for i in (K_COS, K_SIN))
                tt(t, ps[0:ROPE, 0:5, 0:T], sin, ALU.mult)
                tt(QR[:, :, :], QR[:, :, :], cos, ALU.mult)
                dve.drain()
                tt(QR[:, :, :], QR[:, :, :], t, ALU.add).then_inc(r_out.sem, 1)
                dve.drain()

                def att_max(h):
                    x = h < 4
                    dve.wait_ge(*s_mm(l, h + 1))
                    if h >= 4:
                        dve.wait_ge(*s_t(l, h - 3))
                    for q in range(2):
                        src, dst = ps[:, S_BANK[h % 4], q * 256:(q + 1) * 256], att[:, h % 4, q, :]
                        if x:
                            ts(dst, src, X_SCALE, None, ALU.mult)
                        else:
                            m = cst[:, K_MASK + P * (1 - q):K_MASK + P * (1 - q) + 256]
                            stt(dst, src, MLA_SCALE, m, ALU.mult, ALU.add)
                    dve.drain()
                    red(asm[:, h % 4, 0:2], att[:, h % 4], AXX, ALU.max, negate=True).then_inc(s_max.sem, 1)

                def att_out(h):
                    dve.wait_ge(*s_y(l, h + 1))
                    z = pt[:, Z + 12 + h if h < 4 else Z + 8 + h - 4, 0:SEQ]
                    tt(z, ps[:, 4 + h % 2, 0:SEQ], z, ALU.mult).then_inc(s_o.sem, 1)

                dve.wait_ge(*z_ready(l, 1))
                att_max(0)
                att_max(1)
                for h in range(8):
                    dve.wait_ge(*s_exp(l, h + 1))
                    nc.vector.reciprocal(asm[:, h % 4, 4:6], asm[:, h % 4, 2:4])
                    dve.drain()
                    tt(att[:, h % 4], att[:, h % 4], over(asm[:, h % 4, 4:6], 256), ALU.mult).then_inc(s_p.sem, 1)
                    if h < 6:
                        att_max(h + 2)
                    if h:
                        att_out(h - 1)
                att_out(7)
                s8 = lambda i, n=P: pre[0:n, i, :].rearrange("p (h b) -> p h b", h=4)
                ts(s8(0), qn[:, :, SEQ:T], col(C_KNN), None, ALU.mult)
                tt(s8(1), qn[:, :, SEQ:T], kn[:, :, SEQ:T], ALU.mult)
                tt(s8(2, ROPE), QR[:, 0:4, SEQ:T], over(QR[:, HEADS, SEQ:T], 4, 1), ALU.mult).then_inc(pre_in.sem, 1)
                for half in range(2):
                    copy(qrs[ROPE * half:ROPE * (half + 1), :, 4 * half:4 * half + 4].rearrange("p b h -> p h b"),
                         QR[:, 0:4, SEQ:T])
                dve.wait_ge(*pre_mm(l, 1))
                copy(qabs[:, :, :, :].rearrange("p b c h -> p (c h) b"), ps[:, 6, 0:64].rearrange("p (n b) -> p n b", b=NB))
                copy(scur[:, :, :].rearrange("p b h -> p h b"), ps[:, 6, 64:96].rearrange("p (h b) -> p h b", h=4)
                     ).then_inc(pre_out.sem, 1)
                dve.drain()
                query(l, 0, 0)
                query(l, 1, 1)
                dve.wait_ge(*pre_mm(l, 2))
                copy(rows[0:NB, ROW_X:ROW_X + 512], ps[0:NB, 7, :]).then_inc(pre_row.sem, 1)
                dve.wait_ge(*xc_ready(l, 1))
                tt(dtx[:, :, :], dtx[:, :, :], xc[:, 0:4, SEQ:T].rearrange("p q b -> p b q"), ALU.mult)
                dve.wait_ge(*kv_saved(l, 32))
                dve.wait_ge(*tok_mm(l, 4))
                copy(vtok, ps[:, 0:2, :]).then_inc(tok_dve.sem, 1)
                dve.wait_ge(*tok_mm(l, 5))
                x8 = lambda t, m: t[:, m, :].rearrange("p (h n) -> p h n", h=8)
                for m in range(2):
                    v = ps[:, 2 + m, :].rearrange("p (h n) -> p h n", h=8)
                    tt(x8(xtok, m), v, over(cols[:, m, 8:16], SSD_W), ALU.mult)
                    last = tt(x8(xw, m), v, over(cols[:, m, 16:24], SSD_W), ALU.mult)
                last.then_inc(tok_dve.sem, 1)
                dve.wait_ge(*tok_mm(l, 7))
                tt(wv[:, :, :].rearrange("p b h -> p h b"), ps[:, 7, 0:32].rearrange("p (h b) -> p h b", h=4),
                   gb[:, 1].rearrange("p b h -> p h b"), ALU.mult).then_inc(tok_dve.sem, 1)
                dve.drain()
                for m in range(2):
                    last = tt(vw[:, m, :].rearrange("p (h n) -> p h n", h=4), vtok[:, m, :].rearrange("p (h n) -> p h n", h=4),
                              over(cols[:, m, 28:32], P), ALU.mult)
                last.then_inc(weighted.sem, 1)
                dve.wait_ge(*pre_mm(l, 3))
                copy(rows[0:NB, 0:1536].rearrange("p (k n) -> p k n", k=3), ps[0:NB, 0:3, :]).then_inc(pre_row.sem, 1)

                def mask(item):
                    dve.wait_ge(*st_mm(l, item + 1))
                    tt(stm[:, item % 2, :], ps[:, 6 + item % 2, 0:384], tri, ALU.mult).then_inc(st_out.sem, 1)
                    dve.drain()

                mask(0)
                mask(1)
                seg(l, 0)
                seg(l, 1)
                for n in range(12):
                    dve.wait_ge(*seg_exp(l, n + 1))
                    item = n // 4 if n < 8 else n - 6
                    tt(dec[:, n % 4, :], dec[:, n % 4, :], stm[:, item % 2, :], ALU.mult).then_inc(seg_w.sem, 1)
                    if n in MASK_AFTER:
                        dve.drain()
                        mask(MASK_AFTER[n])
                    if n < 10:
                        seg(l, n + 2)
                    if n:
                        rec_out(l, n - 1)
                rec_out(l, 11)
                n0 = par[:, C_N0:C_N0 + 32].rearrange("p (h b) -> p h b", h=4)
                by = lambda ap: ap.rearrange("p b h -> p h b")
                tt(n0, n0, by(gb[:, 0]), ALU.mult)
                tt(s8(1), mlk[:, :, SEQ:T], by(gb[:, 1]), ALU.mult)
                dve.drain()
                tt(n0, n0, s8(1), ALU.add)
                dve.drain()
                tt(s8(0), n0, mlq[:, :, SEQ:T], ALU.mult).then_inc(ns_in.sem, 1)
                dve.wait_ge(*nq_mm(l, 1))
                den = ps[:, 7, 0:32].rearrange("p (h b) -> p h b", h=4)
                stt(s8(1), den, -1.0, by(gb[:, 2]), ALU.mult, ALU.max)
                dve.drain()
                tt(s8(1), den, s8(1), ALU.max)
                dve.drain()
                nc.vector.reciprocal(s8(1), s8(1))
                sample(l, 0, 0, None)
                with dve.Fori(0, NB // 2 - 1) as i:
                    for u in (1, 0):
                        b = 2 * i + (1 if u else 2)
                        sample(l, b, u, b - 1)
                sample(l, NB - 1, 1, NB - 2, more=False)
                softmax_max(l, NB - 1, 1)
                softmax_shift(l, NB - 1, 1)
                softmax_sum(l, NB - 1, 1)
                dve.wait_ge(*n_rs(l, 10))
                for c in range(4):
                    last = stt(pt[:, Z + c, :], xc[:, c, :], col(C_SSD + c), nrs[:, c // 2, :], ALU.mult, ALU.mult)
                last.then_inc(n_out.sem, 1)
                dve.wait_ge(*n_rs(l, 11))
                for c in range(4):
                    stt(xc[:, 8 + c, :], xc[:, 8 + c, :], col(C_ML + c), nrs_ml[:, c, :], ALU.mult, ALU.mult)
                dve.drain()
                tt(pt[:, Z + 4:Z + 8, :], pt[:, Z + 4:Z + 8, :], xc[:, 8:12, :], ALU.mult)
                nc.vector.reciprocal(dens[:, 0:NB - 1, :], dens[:, 0:NB - 1, :])
                context_out(l, NB - 1, 1)
                dve.drain()
                z = pt[:, Z + 12:Z + 16, SEQ:T]
                tt(z, by(ysd[:, :, :]), z, ALU.mult).then_inc(mixed.sem, 1)
                nc.vector.reciprocal(dens[:, NB - 1, :], dens[:, NB - 1, :])
                t = dtmp[:, 0:64].rearrange("p (c b h) -> p c b h", c=2, b=NB)
                tt(t, pt[:, CKV:CKV + 2, SEQ:T].unsqueeze(3).broadcast_to([P, 2, NB, 4]), over(owns[:, :, :], 2, 1), ALU.mult)
                dve.drain()
                dve.wait_ge(*cr_mm(l, 1))
                tt(t, ps[:, 7, 384:448].rearrange("p (c b h) -> p c b h", c=2, b=NB), t, ALU.add)
                dve.drain()
                tt(ctxall[:, :, :, :].rearrange("p c h b -> p c b h"), t, over(dens[:, :, :], 2, 1), ALU.mult
                   ).then_inc(cr_out.sem, 1)
                dve.wait_ge(*uv_mm(l, 1))
                z = pt[:, Z + 8:Z + 12, SEQ:T]
                tt(z, ps[:, 7, 448:480].rearrange("p (h b) -> p h b", h=4), z, ALU.mult).then_inc(mixed.sem, 1)
                dve.sem_inc(n_out.sem, 1)
                with dve.Fori(0, OUT_TILES // 2) as i:
                    for c in range(2):
                        dve.wait_ge(*o_mm(l, 2 * i + (c + 1)))
                        x = xT[:, bass.ds(2 * i + c, 1), :].rearrange("p o t -> p (o t)")
                        tt(x, ps[:, c, 0:T], x, ALU.add).then_inc(o_out.sem, 1)
                        dve.drain()
                        x2 = u3[:, bass.ds(2 * i + c, 1), :].rearrange("p o t -> p (o t)")
                        tt(x2, x, x, ALU.mult).then_inc(x_sq.sem, 1)
                dve.drain().then_inc(layer_free.sem, 1)
            dve.wait_ge(f_rs.sem, 1)
            for k in range(KT):
                last = stt(u3[:, k, :], xT[:, k, :], col(C_FIN + k), nrs[:, 0, :], ALU.mult, ALU.mult)
            last.then_inc(f_out.sem, 1)


INS = dict(
    cst=(P, N_CST), xT=(P, KT, T), memT=(P, KT, MEM), pages=(1, DEPTH * NB * PAGES),
    par=(DEPTH, P, N_PAR), wsm=(DEPTH, P, 3072), weights=(DEPTH * CHUNKS, P, SLOT),
    lat=(DEPTH * POOL, P, 256), krope=(DEPTH * POOL, ROPE, P),
    memk=(DEPTH * NB, P, 1024), memv=(DEPTH * NB, P, 1024),
    ssm=(DEPTH * NB, P, 512), mlC=(DEPTH * NB, P, 512))
OUTS = dict(
    o_y=(P, KT, T), o_lat=(DEPTH, P, 2, T), o_kr=(DEPTH, ROPE, T), o_mk=(DEPTH, P, 1024), o_mv=(DEPTH, P, 1024),
    o_ssm=(DEPTH, P, 512), o_conv=(DEPTH, P, CT, T - SEQ + 3), o_conv_old=(DEPTH, P, CT * 3 * NB),
    o_C=(DEPTH, P, 512), o_n=(DEPTH, 1, 512), o_m=(DEPTH, 4, T), o_ssm_s=(DEPTH * NB, P, 512),
    o_C_s=(DEPTH * NB, P, 512), o_ns=(DEPTH, P, 32))


def constants():
    c = np.zeros((P, N_CST), np.float32)
    i = np.arange(P)
    c[:, K_ID:K_ID + P] = np.eye(P)
    c[:, K_ONE:K_ONE + T] = 1.0
    c[:, K_MASK + P:K_MASK + 2 * P] = np.where(i[None] <= i[:, None], 0.0, NEG)
    c[:, K_MASK + 2 * P:K_MASK + 3 * P] = NEG
    upper = (i[None] >= i[:, None]).astype(np.float32)
    c[:, K_TRI:K_TRI + P] = upper
    c[:, K_TRI + P:K_TRI + 2 * P] = 1.0
    c[:, K_TRI + 2 * P:K_TRI + 3 * P] = upper
    half = ROPE // 2
    for k in range(half):
        c[half + k, K_ROT + k] = -1.0
        c[k, K_ROT + half + k] = 1.0
    pos = np.concatenate([np.arange(SEQ), np.full(NB, PAGES * PAGE)]).astype(np.float32)
    inv = (np.float32(10000.0) ** (-np.arange(half, dtype=np.float32) * np.float32(2.0) / np.float32(ROPE))).astype(np.float32)
    ang = (inv[:, None] * pos[None]).astype(np.float32)
    c[0:ROPE, K_COS:K_COS + T] = np.tile(np.cos(ang), (2, 1))
    c[0:ROPE, K_SIN:K_SIN + T] = np.tile(np.sin(ang), (2, 1))
    for h in range(8):
        c[h, K_SEL + h * P:K_SEL + (h + 1) * P] = 1.0
        c[h, K_EXP + h * SSD_W:K_EXP + (h + 1) * SSD_W] = 1.0
    c[:, K_EPS] = EPS
    return c


def lay_in(x):
    x = {k: np.asarray(v) for k, v in x.items()}
    L = DEPTH

    def tiles(a):
        return np.swapaxes(a.reshape(*a.shape[:-1], -1, P), -1, -2)

    def rows_(a, n=P):
        out = np.zeros((*a.shape[:-1], n, 1), np.float32)
        out[..., :a.shape[-1], 0] = a
        return out

    def cols_pad(a):
        out = np.zeros((L, P, a.shape[-1]), np.float32)
        out[:, :a.shape[1]] = a
        return out

    d = {"cst": constants()}
    tokens = np.concatenate([x["x_prompt"][0], x["x_sample"][:, 0]], 0)
    d["xT"] = tokens.T.reshape(KT, P, T).swapaxes(0, 1)
    d["memT"] = x["mem_prompt"][0].T.reshape(KT, P, MEM).swapaxes(0, 1)
    table = x["page_table"].astype(np.int32).reshape(1, -1)
    d["pages"] = np.concatenate([table + POOL * l for l in range(L)], 1).astype(np.int32)
    cw = np.concatenate([tiles(x["conv_a_w"]), tiles(x["conv_b_w"])], -1)
    st = np.concatenate([x["state_ssm_conv"], x["state_mlstm_conv"]], -1)
    st = tiles(st).transpose(0, 3, 4, 2, 1).reshape(L, P, -1)
    n0 = x["state_mlstm_n"].transpose(0, 3, 2, 1).reshape(L, P, -1)
    m0 = cols_pad(x["state_mlstm_m"].transpose(0, 2, 1))
    dsk = tiles(np.repeat(x["d_skip"], SSD_W, axis=-1))
    fin = np.broadcast_to(tiles(x["final_norm_g"])[None], (L, P, KT))
    d["par"] = np.concatenate(
        [tiles(x["norm_g"]), cw.transpose(0, 2, 1, 3).reshape(L, P, -1),
         np.concatenate([tiles(x["conv_a_b"]), tiles(x["conv_b_b"])], -1), tiles(x["ssd_norm_g"]), tiles(x["ml_norm_g"]),
         tiles(x["q_norm_g"]), tiles(x["kv_norm_g"]), rows_(x["qn_nope_g"]), rows_(x["qn_rope_g"]), rows_(x["kn_nope_g"]),
         rows_(x["kn_rope_g"]), tiles(x["mem_norm_g"]), rows_(x["xk_norm_g"]), rows_(x["xq_norm_g"]), dsk, fin,
         rows_(x["dt_bias"]), rows_(x["a_log"]), rows_(x["b_i"]), rows_(x["b_f"]), m0, n0, st], -1)
    uk = x["w_uk"].reshape(L, 2, P, 512).transpose(0, 2, 1, 3).reshape(L, P, 1024)
    uv = x["w_uv"].reshape(L, 2, P, 512).transpose(0, 2, 1, 3).reshape(L, P, 1024)
    ukT = x["w_uk"].transpose(0, 3, 2, 1).reshape(L, P, 1024)
    d["wsm"] = np.concatenate([uk, uv, ukT], -1)
    w = x["w_in"]
    z, xbc, dt, xm, ig, fg, og, cq, ckv, krp, xq = np.split(
        w, np.cumsum([2048, 1024, 8, 512, 4, 4, 512, 384, 256, 64]).tolist(), axis=-1)
    gate = np.zeros((L, D_MODEL, P), np.float32)
    gate[..., 0:8], gate[..., 32:36], gate[..., 64:68] = dt, ig, fg
    krp = np.concatenate([krp, np.zeros((L, D_MODEL, P - ROPE), np.float32)], -1)
    w = np.concatenate([xbc, xm, gate, krp, cq, ckv, xq, og, z], -1)
    w = np.concatenate([w, np.zeros((L, D_MODEL, P), np.float32)], -1)
    w_in = w.reshape(L, KT, P, IN_CHUNKS, 2, P).transpose(0, 3, 2, 4, 1, 5)
    mk = x["w_mem_k"].reshape(L, KT, P, 2, 2, P).transpose(0, 3, 2, 4, 1, 5)
    mv = x["w_mem_v"].reshape(L, 2, 4, P, 512).transpose(0, 1, 3, 2, 4)
    uq = x["w_uq"].reshape(L, 3, P, 2, 2, 192).transpose(0, 3, 2, 4, 1, 5)
    ml = np.stack([x["w_mq"], x["w_mk"], x["w_mv"], np.zeros_like(x["w_mv"])], 1)
    ml = ml.reshape(L, 2, 2, 4, P, P).transpose(0, 1, 4, 2, 3, 5)
    out = x["w_out"].reshape(L, MIX_TILES, P, OUT_TILES, P).transpose(0, 3, 2, 1, 4)
    weights = np.zeros((L, CHUNKS, P, SLOT), np.float32)
    first = 0
    for part, chunks in ((w_in, IN_CHUNKS), (mk, 2), (mv, 2), (uq, 2), (ml, 2), (out, OUT_TILES)):
        part = part.reshape(L, chunks, P, -1)
        weights[:, first:first + chunks, :, :part.shape[-1]] = part
        first += chunks
    d["weights"] = weights.reshape(L * CHUNKS, P, SLOT)
    d["lat"] = x["cache_mla_latent"].reshape(-1, P, 256)
    d["krope"] = x["cache_mla_krope"].reshape(-1, P, ROPE).swapaxes(1, 2)
    d["memk"] = x["cache_mem_k"].reshape(-1, P, 1024)
    d["memv"] = x["cache_mem_v"].reshape(-1, P, 1024)
    d["ssm"] = x["state_ssm"].reshape(L * NB, 4, P, P).swapaxes(1, 2).reshape(-1, P, 512)
    d["mlC"] = x["state_mlstm_C"].reshape(L * NB, 4, P, P).swapaxes(1, 2).reshape(-1, P, 512)
    return {k: np.ascontiguousarray(v) for k, v in d.items()}


def lay_out(r):
    L = DEPTH
    y = r["o_y"].transpose(2, 1, 0).reshape(T, D_MODEL)
    lat = r["o_lat"].transpose(0, 3, 2, 1).reshape(L, T, 256)
    krp = r["o_kr"].transpose(0, 2, 1)
    mk = r["o_mk"].reshape(L, P, 4, MEM).transpose(0, 3, 2, 1)[:, None]
    mv = r["o_mv"].reshape(L, P, 2, 4, P).transpose(0, 2, 1, 3, 4).reshape(L, 1, MEM, 4, P)
    conv = r["o_conv"].transpose(0, 3, 2, 1).reshape(L, 3 + NB, CT * P)
    old = r["o_conv_old"].reshape(L, P, CT, 3, NB).transpose(0, 4, 3, 2, 1).reshape(L, NB, 3, CT * P)
    conv_s = np.concatenate([old[:, :, 1:], conv[:, 3:, None]], 2)
    by_head = lambda a, n: a.reshape(-1, P, 4, P).swapaxes(1, 2).reshape(L, n, 4, P, P)
    m = r["o_m"]
    ssd = SSD_W
    out = (
        y[None, :SEQ], y[SEQ:, None], lat[:, None, :SEQ], krp[:, None, :SEQ], mk, mv,
        by_head(r["o_ssm"], 1).reshape(L, 1, SSD_HEADS, ssd, P), conv[:, None, :3, :1024],
        by_head(r["o_C"], 1), r["o_n"].reshape(L, 1, 4, P), m[:, :, SEQ - 1][:, None], conv[:, None, :3, 1024:],
        lat[:, SEQ:, None], krp[:, SEQ:, None],
        by_head(r["o_ssm_s"], NB).reshape(L, NB, SSD_HEADS, ssd, P), conv_s[..., :1024],
        by_head(r["o_C_s"], NB), r["o_ns"].reshape(L, P, 4, NB).transpose(0, 3, 2, 1),
        m[:, :, SEQ:].swapaxes(1, 2), conv_s[..., 1024:])
    return tuple(np.ascontiguousarray(a) for a in out)


def program(nc):
    d = {}
    for name, shape in INS.items():
        dt = mybir.dt.int32 if name == "pages" else F32
        d[name] = nc.dram_tensor("in_" + name, shape, dt, kind="ExternalInput").ap()
    for name, shape in OUTS.items():
        d[name] = nc.dram_tensor(name, shape, F32, kind="ExternalOutput").ap()
    d["rowscr"] = nc.dram_tensor("rowscr", (NB, ROWS), F32, kind="Internal").ap()
    build(nc, d)


def kernel(**inputs):
    import concourse.bacc as bacc
    from concourse.bass_utils import run_bass_kernel_spmd

    nc = bacc.Bacc("TRN2", target_bir_lowering=False, num_devices=1)
    program(nc)
    r = run_bass_kernel_spmd(nc, [{"in_" + k: v for k, v in lay_in(inputs).items()}], core_ids=[0])
    return lay_out(r.results[0])
```
